# Optimizing a Trainium2 kernel written in Bass

```python
import jax, jax.numpy as jnp
from jax import lax
import numpy as np
import math

D_MODEL = 1024
BATCH = 1
SEQ = 256
DEPTH = 1

GRID_W = 64
CTX_LEN = 256
N_MIXERS = 2
CONV_WIDTH = 3
GLA_HEADS = 4
GLA_DK_TOT = D_MODEL // 2
GLA_DV_TOT = D_MODEL
GLA_DK = GLA_DK_TOT // GLA_HEADS
GLA_DV = GLA_DV_TOT // GLA_HEADS
GLA_GATE_RANK = 16
GLA_TAU = 16.0
GLA_CHUNK = 64
D_FF = -(-8 * D_MODEL // (3 * 256)) * 256
N_ADA = 6
EPS = 1e-6


def rmsnorm(x, g):
    xf = x.astype(jnp.float32)
    y = xf * lax.rsqrt(jnp.mean(xf * xf, axis=-1, keepdims=True) + EPS)
    return (y * g.astype(jnp.float32)).astype(x.dtype)

def ada_terms(cond, w, b):
    return jnp.split(jax.nn.silu(cond) @ w + b, N_ADA, axis=-1)

def modulate(h, shift, scale):
    return h * (1.0 + scale) + shift

def conv3_seq(u, w):
    up = jnp.pad(u, ((0, 0), (1, 1), (0, 0)))
    return w[0] * up[:, :-2] + w[1] * up[:, 1:-1] + w[2] * up[:, 2:]

def conv3_grid(u, w):
    B, L, C = u.shape
    rows = L // GRID_W
    return conv3_seq(u.reshape(B * rows, GRID_W, C), w).reshape(B, L, C)

def short_conv_mixer(h, w_in, conv_w, w_out, on_grid):
    gate_b, gate_c, hv = jnp.split(h @ w_in, 3, axis=-1)
    u = gate_c * hv
    conv = conv3_grid(u, conv_w) if on_grid else conv3_seq(u, conv_w)
    return (gate_b * conv) @ w_out

def gla_project(h, w_in, b_r, w_a1, w_a2, b_a):
    B, L, _ = h.shape
    q, k, v, r = jnp.split(h @ w_in, [GLA_DK_TOT, 2 * GLA_DK_TOT, 2 * GLA_DK_TOT + GLA_DV_TOT], axis=-1)

    def heads(t, d):
        return t.reshape(B, L, GLA_HEADS, d).transpose(0, 2, 1, 3).astype(jnp.float32)

    q = heads(q, GLA_DK) * (GLA_DK ** -0.5)
    k = heads(k, GLA_DK)
    v = heads(v, GLA_DV)
    logit = jnp.einsum('zblr,zrk->zblk', jnp.einsum('bld,zdr->zblr', h, w_a1), w_a2) + b_a[:, None, None, :]
    la = jax.nn.log_sigmoid(logit.astype(jnp.float32)) / GLA_TAU
    la = la.reshape(2, B, L, GLA_HEADS, GLA_DK).transpose(0, 1, 3, 2, 4)
    return q, k, v, r + b_r, la

def gla_chunked(q, k, v, la, s0, with_output):
    B, H, T, dk = q.shape
    dv = v.shape[-1]
    n = T // GLA_CHUNK
    q = q.reshape(B, H, n, GLA_CHUNK, dk)
    k = k.reshape(B, H, n, GLA_CHUNK, dk)
    v = v.reshape(B, H, n, GLA_CHUNK, dv)
    b = jnp.cumsum(la.reshape(B, H, n, GLA_CHUNK, dk), axis=3)
    b_last = b[:, :, :, -1]
    k_dec = k * jnp.exp(b_last[:, :, :, None] - b)
    u = jnp.einsum('bhnsd,bhnse->bhnde', k_dec, v)

    def step(state, inp):
        decay, u_n = inp
        return decay[..., None] * state + u_n, state

    s_final, s_prev = lax.scan(step, s0, (jnp.moveaxis(jnp.exp(b_last), 2, 0), jnp.moveaxis(u, 2, 0)))
    if not with_output:
        return None, s_final
    s_prev = jnp.moveaxis(s_prev, 0, 2)
    q_dec = q * jnp.exp(b)
    o_inter = jnp.einsum('bhncd,bhnde->bhnce', q_dec, s_prev)
    scores = jnp.einsum('bhncd,bhnsd->bhncs', q_dec, k * jnp.exp(-b))
    mask = jnp.tril(jnp.ones((GLA_CHUNK, GLA_CHUNK), dtype=bool))
    scores = jnp.where(mask, scores, 0.0)
    o_intra = jnp.einsum('bhncs,bhnse->bhnce', scores, v)
    return (o_inter + o_intra).reshape(B, H, T, dv), s_final

def gla_output(o, r, norm_g, w_out, dtype):
    B, H, T, dv = o.shape
    o = rmsnorm(o.transpose(0, 2, 1, 3), norm_g).reshape(B, T, H * dv).astype(dtype)
    return (o * jax.nn.silu(r)) @ w_out

def gla_mixer(hl, hc, w_in, b_r, w_a1, w_a2, b_a, norm_g, w_out, ctx_out):
    ql, kl, vl, rl, la_l = gla_project(hl, w_in, b_r, w_a1, w_a2, b_a)
    qc, kc, vc, rc, la_c = gla_project(hc, w_in, b_r, w_a1, w_a2, b_a)
    flip = lambda t: jnp.flip(t, axis=2)
    s0 = jnp.zeros((hl.shape[0], GLA_HEADS, GLA_DK, GLA_DV), jnp.float32)
    o_cf, s_cf = gla_chunked(qc, kc, vc, la_c[0], s0, ctx_out)
    o_cb, s_cb = gla_chunked(flip(qc), flip(kc), flip(vc), flip(la_c[1]), s0, ctx_out)
    o_lf, _ = gla_chunked(ql, kl, vl, la_l[0], s_cf, True)
    o_lb, _ = gla_chunked(flip(ql), flip(kl), flip(vl), flip(la_l[1]), s_cb, True)
    yl = gla_output(o_lf + flip(o_lb), rl, norm_g, w_out, hl.dtype)
    yc = gla_output(o_cf + flip(o_cb), rc, norm_g, w_out, hc.dtype) if ctx_out else None
    return yl, yc

def swiglu(h, w_in, w_out):
    gate, up = jnp.split(h @ w_in, 2, axis=-1)
    return (jax.nn.silu(gate) * up) @ w_out

def first_inputs(seed: int = 0) -> dict:
    key = jax.random.key(seed)
    ks = jax.random.split(key, 24)
    n_conv = (DEPTH + N_MIXERS - 1) // N_MIXERS
    n_gla = DEPTH // N_MIXERS
    nrm = lambda k, shape, s: jax.random.normal(k, shape, jnp.float32) * s
    d = D_MODEL
    return {
        "x": nrm(ks[0], (BATCH, SEQ, d), 1.0),
        "c": nrm(ks[1], (BATCH, d), 1.0),
        "ctx": nrm(ks[2], (BATCH, CTX_LEN, d), 1.0),
        "c_ctx": nrm(ks[3], (d,), 1.0),
        "ada_w": nrm(ks[4], (DEPTH, d, N_ADA * d), 0.5 * d ** -0.5),
        "ada_b": nrm(ks[5], (DEPTH, N_ADA * d), 0.01),
        "norm1_g": 1.0 + nrm(ks[6], (DEPTH, d), 0.02),
        "norm2_g": 1.0 + nrm(ks[7], (DEPTH, d), 0.02),
        "conv_w_in": nrm(ks[8], (n_conv, d, 3 * d), d ** -0.5),
        "conv_w": nrm(ks[9], (n_conv, CONV_WIDTH, d), CONV_WIDTH ** -0.5),
        "conv_w_out": nrm(ks[10], (n_conv, d, d), d ** -0.5),
        "gla_w_in": nrm(ks[11], (n_gla, d, 2 * GLA_DK_TOT + 2 * GLA_DV_TOT), d ** -0.5),
        "gla_b_r": nrm(ks[12], (n_gla, GLA_DV_TOT), 0.01),
        "gla_w_a1": nrm(ks[13], (n_gla, 2, d, GLA_GATE_RANK), d ** -0.5),
        "gla_w_a2": nrm(ks[14], (n_gla, 2, GLA_GATE_RANK, GLA_DK_TOT), GLA_GATE_RANK ** -0.5),
        "gla_b_a": nrm(ks[15], (n_gla, 2, GLA_DK_TOT), 0.01),
        "gla_norm_g": 1.0 + nrm(ks[16], (n_gla, GLA_DV), 0.02),
        "gla_w_out": nrm(ks[17], (n_gla, GLA_DV_TOT, d), GLA_DV_TOT ** -0.5),
        "ffn_w_in": nrm(ks[18], (DEPTH, d, 2 * D_FF), d ** -0.5),
        "ffn_w_out": nrm(ks[19], (DEPTH, D_FF, d), D_FF ** -0.5),
        "final_g": 1.0 + nrm(ks[20], (d,), 0.02),
    }

def first_block(x, c, ctx, c_ctx, ada_w, ada_b, norm1_g, norm2_g, conv_w_in, conv_w, conv_w_out,
              gla_w_in, gla_b_r, gla_w_a1, gla_w_a2, gla_b_a, gla_norm_g, gla_w_out,
              ffn_w_in, ffn_w_out, final_g):
    cond_lat = c[:, None, :]
    for i in range(DEPTH):
        last = i == DEPTH - 1
        kind = i % N_MIXERS
        j = i // N_MIXERS
        need_ctx_in = (not last) or kind == 1
        sh1, sc1, g1, sh2, sc2, g2 = ada_terms(cond_lat, ada_w[i], ada_b[i])
        hl = modulate(rmsnorm(x, norm1_g[i]), sh1, sc1)
        if need_ctx_in:
            csh1, csc1, cg1, csh2, csc2, cg2 = ada_terms(c_ctx, ada_w[i], ada_b[i])
            hc = modulate(rmsnorm(ctx, norm1_g[i]), csh1, csc1)
        if kind == 0:
            yl = short_conv_mixer(hl, conv_w_in[j], conv_w[j], conv_w_out[j], True)
            yc = short_conv_mixer(hc, conv_w_in[j], conv_w[j], conv_w_out[j], False) if not last else None
        else:
            yl, yc = gla_mixer(hl, hc, gla_w_in[j], gla_b_r[j], gla_w_a1[j], gla_w_a2[j], gla_b_a[j],
                               gla_norm_g[j], gla_w_out[j], not last)
        x = x + g1 * yl
        x = x + g2 * swiglu(modulate(rmsnorm(x, norm2_g[i]), sh2, sc2), ffn_w_in[i], ffn_w_out[i])
        if not last:
            ctx = ctx + cg1 * yc
            ctx = ctx + cg2 * swiglu(modulate(rmsnorm(ctx, norm2_g[i]), csh2, csc2), ffn_w_in[i], ffn_w_out[i])
    return rmsnorm(x, final_g)


DEPTH_2 = 2

D_FF_2 = 2816
N_NORMS = 6
HEAD_DIM = 64
CONV_CH = 512
CONV_K = 31
SWA_HQ = 8
SWA_HKV = 2
SWA_G = SWA_HQ // SWA_HKV
WINDOW = 128
BLK = 128
FOX_H = 16
AB_IN = 2 * CONV_CH + SWA_HQ * HEAD_DIM + 2 * SWA_HKV * HEAD_DIM
AB_OUT = CONV_CH + SWA_HQ * HEAD_DIM
FOX_IN = 3 * FOX_H * HEAD_DIM + FOX_H
FOX_OUT = FOX_H * HEAD_DIM
NEG = -1e30


def _rmsnorm(x, g):
    xf = x.astype(jnp.float32)
    y = xf * lax.rsqrt(jnp.mean(xf * xf, axis=-1, keepdims=True) + EPS)
    return (y * g.astype(jnp.float32)).astype(x.dtype)

def _swiglu(x, wg, wu, wd):
    return (jax.nn.silu(x @ wg) * (x @ wu)) @ wd

def _alibi_slopes(n):
    return jnp.asarray([2.0 ** (-8.0 * (i + 1) / n) for i in range(n)], dtype=jnp.float32)

def _conv_module(u, gate, w, b, ln_g, ln_b):
    a = u * jax.nn.sigmoid(gate)
    y = lax.conv_general_dilated(
        a, w.reshape(CONV_K, 1, CONV_CH).astype(a.dtype),
        window_strides=(1,), padding=[(CONV_K - 1, 0)],
        dimension_numbers=("NWC", "WIO", "NWC"),
        feature_group_count=CONV_CH) + b
    yf = y.astype(jnp.float32)
    mu = jnp.mean(yf, axis=-1, keepdims=True)
    var = jnp.mean(jnp.square(yf - mu), axis=-1, keepdims=True)
    yf = (yf - mu) * lax.rsqrt(var + EPS) * ln_g.astype(jnp.float32) + ln_b.astype(jnp.float32)
    return jax.nn.silu(yf).astype(u.dtype)

def _swa_sinks(q, k, v, sinks):
    b, s, _, dh = q.shape
    nb = s // BLK
    qb = q.reshape(b, nb, BLK, SWA_HKV, SWA_G, dh)
    kb = k.reshape(b, nb, BLK, SWA_HKV, dh)
    vb = v.reshape(b, nb, BLK, SWA_HKV, dh)
    pad = ((0, 0), (1, 0), (0, 0), (0, 0), (0, 0))
    kk = jnp.concatenate([jnp.pad(kb, pad)[:, :-1], kb], axis=2)
    vv = jnp.concatenate([jnp.pad(vb, pad)[:, :-1], vb], axis=2)
    sc = jnp.einsum("bnqhgd,bnkhd->bnhgqk", qb, kk).astype(jnp.float32) / math.sqrt(dh)
    t_loc = jnp.arange(BLK)[:, None]
    s_loc = jnp.arange(2 * BLK)[None, :]
    dist = t_loc + BLK - s_loc
    valid = (dist >= 0) & (dist < WINDOW)
    mask = valid[None] & ((jnp.arange(nb)[:, None, None] > 0) | (s_loc >= BLK)[None])
    slopes = _alibi_slopes(SWA_HQ).reshape(SWA_HKV, SWA_G)
    sc = sc - slopes[:, :, None, None] * dist.astype(jnp.float32)
    sc = jnp.where(mask[None, :, None, None], sc, NEG)
    sink = jnp.broadcast_to(sinks.astype(jnp.float32).reshape(SWA_HKV, SWA_G)[None, None, :, :, None, None],
                            sc.shape[:-1] + (1,))
    p = jax.nn.softmax(jnp.concatenate([sc, sink], axis=-1), axis=-1)[..., :-1]
    o = jnp.einsum("bnhgqk,bnkhd->bnqhgd", p.astype(v.dtype), vv)
    return o.reshape(b, s, SWA_HQ * dh)

def _fox_attention(q, k, v, zf, b_f):
    b, s, h, dh = q.shape
    nb = s // BLK
    qh = q.transpose(0, 2, 1, 3)
    kh = k.transpose(0, 2, 1, 3)
    vh = v.transpose(0, 2, 1, 3)
    logf = jax.nn.log_sigmoid(zf.astype(jnp.float32) + b_f.astype(jnp.float32))
    c = jnp.cumsum(logf.transpose(0, 2, 1), axis=-1)
    key_pos = jnp.arange(s)

    def one_block(i):
        start = i * BLK
        qs = lax.dynamic_slice_in_dim(qh, start, BLK, axis=2)
        cs = lax.dynamic_slice_in_dim(c, start, BLK, axis=2)
        sc = jnp.einsum("bhqd,bhkd->bhqk", qs, kh).astype(jnp.float32) / math.sqrt(dh)
        sc = sc + cs[..., :, None] - c[..., None, :]
        tpos = start + jnp.arange(BLK)
        sc = jnp.where(tpos[:, None] >= key_pos[None, :], sc, NEG)
        p = jax.nn.softmax(sc, axis=-1)
        return jnp.einsum("bhqk,bhkd->bhqd", p.astype(vh.dtype), vh)

    o = lax.map(one_block, jnp.arange(nb))
    return o.transpose(1, 0, 3, 2, 4).reshape(b, s, h * dh)

def _mixer_even(h, w_in, conv_w, conv_b, ln_g, ln_b, sinks, w_out):
    b, s, _ = h.shape
    z = h @ w_in
    o0 = CONV_CH
    o1 = o0 + CONV_CH
    o2 = o1 + SWA_HQ * HEAD_DIM
    o3 = o2 + SWA_HKV * HEAD_DIM
    u, gate = z[..., :o0], z[..., o0:o1]
    q = z[..., o1:o2].reshape(b, s, SWA_HQ, HEAD_DIM)
    k = z[..., o2:o3].reshape(b, s, SWA_HKV, HEAD_DIM)
    v = z[..., o3:].reshape(b, s, SWA_HKV, HEAD_DIM)
    a_out = _conv_module(u, gate, conv_w, conv_b, ln_g, ln_b)
    b_out = _swa_sinks(q, k, v, sinks)
    return jnp.concatenate([a_out, b_out], axis=-1) @ w_out

def _mixer_odd(h, w_in, b_f, w_out):
    b, s, _ = h.shape
    z = h @ w_in
    hd = FOX_H * HEAD_DIM
    q = z[..., :hd].reshape(b, s, FOX_H, HEAD_DIM)
    k = z[..., hd:2 * hd].reshape(b, s, FOX_H, HEAD_DIM)
    v = z[..., 2 * hd:3 * hd].reshape(b, s, FOX_H, HEAD_DIM)
    zf = z[..., 3 * hd:]
    return _fox_attention(q, k, v, zf, b_f) @ w_out

def second_inputs(seed: int = 0) -> dict:
    key = jax.random.key(seed)
    ks = jax.random.split(key, 16)
    n_even = (DEPTH_2 + 1) // 2
    n_odd = DEPTH_2 // 2
    f32 = jnp.float32
    nrm = lambda k, shp, fan: jax.random.normal(k, shp, f32) * fan ** -0.5
    return {
        "x": jax.random.normal(ks[0], (BATCH, SEQ, D_MODEL), f32),
        "norm_g": 1.0 + 0.05 * jax.random.normal(ks[1], (DEPTH_2, N_NORMS, D_MODEL), f32),
        "ffn_w_gate": nrm(ks[2], (DEPTH_2, 2, D_MODEL, D_FF_2), D_MODEL),
        "ffn_w_up": nrm(ks[3], (DEPTH_2, 2, D_MODEL, D_FF_2), D_MODEL),
        "ffn_w_down": nrm(ks[4], (DEPTH_2, 2, D_FF_2, D_MODEL), D_FF_2),
        "ab_w_in": nrm(ks[5], (n_even, D_MODEL, AB_IN), D_MODEL),
        "conv_w": nrm(ks[6], (n_even, CONV_K, CONV_CH), CONV_K),
        "conv_b": 0.02 * jax.random.normal(ks[7], (n_even, CONV_CH), f32),
        "conv_ln_g": 1.0 + 0.05 * jax.random.normal(ks[8], (n_even, CONV_CH), f32),
        "conv_ln_b": 0.02 * jax.random.normal(ks[9], (n_even, CONV_CH), f32),
        "swa_sinks": 0.5 * jax.random.normal(ks[10], (n_even, SWA_HQ), f32),
        "ab_w_out": nrm(ks[11], (n_even, AB_OUT, D_MODEL), AB_OUT),
        "fox_w_in": nrm(ks[12], (n_odd, D_MODEL, FOX_IN), D_MODEL),
        "fox_b_f": jax.random.uniform(ks[13], (n_odd, FOX_H), f32, 1.0, 6.0),
        "fox_w_out": nrm(ks[14], (n_odd, FOX_OUT, D_MODEL), FOX_OUT),
    }

def second_block(x, norm_g, ffn_w_gate, ffn_w_up, ffn_w_down, ab_w_in, conv_w, conv_b,
              conv_ln_g, conv_ln_b, swa_sinks, ab_w_out, fox_w_in, fox_b_f, fox_w_out):
    for l in range(DEPTH_2):
        g = norm_g[l]
        h = _swiglu(_rmsnorm(x, g[0]), ffn_w_gate[l, 0], ffn_w_up[l, 0], ffn_w_down[l, 0])
        x = x + 0.5 * _rmsnorm(h, g[1])
        h = _rmsnorm(x, g[2])
        if l % 2 == 0:
            i = l // 2
            h = _mixer_even(h, ab_w_in[i], conv_w[i], conv_b[i], conv_ln_g[i], conv_ln_b[i],
                            swa_sinks[i], ab_w_out[i])
        else:
            i = l // 2
            h = _mixer_odd(h, fox_w_in[i], fox_b_f[i], fox_w_out[i])
        x = x + _rmsnorm(h, g[3])
        h = _swiglu(_rmsnorm(x, g[4]), ffn_w_gate[l, 1], ffn_w_up[l, 1], ffn_w_down[l, 1])
        x = x + 0.5 * _rmsnorm(h, g[5])
    return x


def setup_inputs(seed=0):
    out = dict(first_inputs(seed))
    for name, value in second_inputs(seed + 1).items():
        if name != "x":
            out[name + "_2"] = value
    return out


def reference(
    x, c, ctx, c_ctx, ada_w, ada_b, norm1_g, norm2_g, conv_w_in, conv_w, conv_w_out, gla_w_in,
    gla_b_r, gla_w_a1, gla_w_a2, gla_b_a, gla_norm_g, gla_w_out, ffn_w_in, ffn_w_out, final_g,
    norm_g_2, ffn_w_gate_2, ffn_w_up_2, ffn_w_down_2, ab_w_in_2, conv_w_2, conv_b_2,
    conv_ln_g_2, conv_ln_b_2, swa_sinks_2, ab_w_out_2, fox_w_in_2, fox_b_f_2, fox_w_out_2,
):
    x = first_block(
        x, c, ctx, c_ctx, ada_w, ada_b, norm1_g, norm2_g, conv_w_in, conv_w, conv_w_out,
        gla_w_in, gla_b_r, gla_w_a1, gla_w_a2, gla_b_a, gla_norm_g, gla_w_out, ffn_w_in,
        ffn_w_out, final_g,
    )
    return second_block(
        x, norm_g_2, ffn_w_gate_2, ffn_w_up_2, ffn_w_down_2, ab_w_in_2, conv_w_2, conv_b_2,
        conv_ln_g_2, conv_ln_b_2, swa_sinks_2, ab_w_out_2, fox_w_in_2, fox_b_f_2, fox_w_out_2,
    )


_drawn_inputs = setup_inputs


def setup_inputs(seed=0):
    import zlib

    import numpy as np

    out = dict(_drawn_inputs(seed))
    spreads = {}
    factors = {'norm1_g': 3.016, 'norm2_g': 6.493, 'conv_ln_b_2': 2.976}
    for name, (base, spread) in spreads.items():
        noise = np.random.default_rng([zlib.crc32(name.encode()), seed]).standard_normal(out[name].shape)
        drawn = base * np.exp(spread * noise) if base else spread * noise
        out[name] = __import__('jax').numpy.asarray(drawn.astype(out[name].dtype))
    for name, factor in factors.items():
        out[name] = (out[name] * factor).astype(out[name].dtype)
    return out
```

```python
from contextlib import ExitStack

import concourse.bass as bass
from concourse import mybir

ALU = mybir.AluOpType
ACT = mybir.ActivationFunctionType
F32 = mybir.dt.float32
F32R = mybir.dt.float32r
AX_X = mybir.AxisListType.X

P = 128
SEQ = 256
TOKT = SEQ // P
D = 1024
KT = D // P
EPS = 1e-6
NEG = -1e30
SLOT = 2048
NSLOT = 3

FF = 2816
FCH = 256
NCH = FF // FCH
FFN_UNITS = 3 * NCH

ADA_FIRST = 8
ADA_REST_SLOTS = 3
ADA_SECTIONS = (2, 3, 4, 5)

CONV_CH = 512
CONV_K = 31
CCT = CONV_CH // P
DH = 64
SWA_HQ = 8
SWA_HKV = 2
SWA_G = SWA_HQ // SWA_HKV
FOX_H = 16
GRID_W = 64
AB_IN = 1792

CONV, FFN0, FFN1, AB, FFN2, FFN3, FOX, FFN4 = range(8)
UNITS = {CONV: 16, AB: 11, FOX: 16}
BASE = {}
_n = ADA_FIRST
for _s in range(8):
    BASE[_s] = _n
    _n += UNITS.get(_s, FFN_UNITS)
TOTAL = _n

C_COND, C_CONVW, C_CB, C_LNG, C_LNB = 0, 8, 32, 36, 40
N_PAR = 44
N_CW31 = CONV_K * CCT


def post_event(b):
    return 2 * b


def pre_event(s):
    return (0, 1, 3)[s] if s < 3 else 2 * s - 1


FINAL_EVENT = 2


def x_count(b, t):
    return (1, 5)[b] + t if b < 2 else 2 * (b + 1) + t + 1


def block_program(nc, out, last_sub=FFN4, **w):
    x_d = w["x"].rearrange("b (t p) d -> p (b t) d", p=P)
    out_d = out.rearrange("b (t p) d -> p (b t) d", p=P)
    ada_w = w["ada_w"].rearrange("l (kt p) n -> p (l kt) n", p=P)
    conv_in = w["conv_w_in"].rearrange("l (kt p) n -> p (l kt) n", p=P)
    conv_out = w["conv_w_out"].rearrange("l (kt p) n -> p (l kt) n", p=P)
    ab_in = w["ab_w_in_2"].rearrange("l (kt p) n -> p (l kt) n", p=P)
    ab_out = w["ab_w_out_2"].rearrange("l (kt p) n -> p (l kt) n", p=P)
    fox_in = w["fox_w_in_2"].rearrange("l (kt p) n -> p (l kt) n", p=P)
    fox_out = w["fox_w_out_2"].rearrange("l (kt p) n -> p (l kt) n", p=P)

    def ffn_weights(s):
        if s == FFN0:
            both = w["ffn_w_in"].rearrange("l (kt p) n -> p (l kt) n", p=P)
            return both[:, :, 0:FF], both[:, :, FF:2 * FF], \
                w["ffn_w_out"].rearrange("l (kt p) n -> p (l kt) n", p=P)
        layer, half = {FFN1: (0, 0), FFN2: (0, 1), FFN3: (1, 0), FFN4: (1, 1)}[s]
        return (w["ffn_w_gate_2"][layer, half].rearrange("(kt p) n -> p kt n", p=P),
                w["ffn_w_up_2"][layer, half].rearrange("(kt p) n -> p kt n", p=P),
                w["ffn_w_down_2"][layer, half].rearrange("(kt p) n -> p kt n", p=P))

    def norm_row(layer, i):
        return w["norm_g_2"][layer, i:i + 1, :].to_broadcast([P, D])

    PRE_ROW = {FFN1: (0, 0), AB: (0, 2), FFN2: (0, 4), FFN3: (1, 0), FOX: (1, 2), FFN4: (1, 4)}
    POST_ROW = {FFN1: (0, 1), AB: (0, 3), FFN2: (0, 5), FFN3: (1, 1), FOX: (1, 3), FFN4: (1, 5)}

    with ExitStack() as ctx:
        def sb(name, shape, dt=F32):
            return ctx.enter_context(nc.sbuf_tensor(name, shape, dt))

        def sem(name):
            return ctx.enter_context(nc.semaphore(name))

        ps = ctx.enter_context(nc.psum_tensor("ps", [P, 8, 512], F32))
        raw = sb("raw", [P, NSLOT, SLOT])
        w_hi = sb("w_hi", [P, NSLOT, SLOT], F32R)
        w_lo = sb("w_lo", [P, NSLOT, SLOT], F32R)
        x = sb("x_sb", [P, TOKT, D])
        tmp = sb("tmp", [P, TOKT, D])
        xn = sb("xn", [P, TOKT, D])
        xT_hi = sb("xT_hi", [P, KT, SEQ], F32R)
        xT_lo = sb("xT_lo", [P, KT, SEQ], F32R)
        yT_hi = sb("yT_hi", [P, KT, SEQ], F32R)
        yT_lo = sb("yT_lo", [P, KT, SEQ], F32R)
        sil = sb("sil", [P, TOKT, FCH])
        hid = sb("hid", [P, TOKT, FCH])
        hT_hi = sb("hT_hi", [P, 2, SEQ], F32R)
        hT_lo = sb("hT_lo", [P, 2, SEQ], F32R)
        rows = sb("rows", [P, 4, D])
        ident = sb("ident", [P, P])
        ones = sb("ones", [P, P])
        upper = sb("upper", [P, P])
        par_rows = sb("par_rows", [P, 2, P])
        par = sb("par", [P, N_PAR])
        cw31 = sb("cw31", [P, N_CW31])
        cond = sb("cond", [P, KT])
        eps = sb("eps", [P, 1])
        warm = sb("warm", [P, 24])
        stat = sb("stat", [P, 3, 32])
        sinks = sb("sinks", [P, SWA_HQ])
        b_f = sb("b_f", [P, FOX_H])
        soft = sb("soft", [P, 8, 64])
        zf = sb("zf", [P, 8, 2 * FOX_H])
        zf_hi = sb("zf_hi", [P, KT, FOX_H], F32R)
        zf_lo = sb("zf_lo", [P, KT, FOX_H], F32R)
        zf_raw = sb("zf_raw", [P, KT, FOX_H])
        cT = sb("cT", [FOX_H, SEQ])
        arena = sb("arena", [P, 11776])

        def part(at, *shape):
            n = 1
            for k in shape:
                n *= k
            assert at + n <= 11776
            ap = arena[:, at:at + n]
            if len(shape) == 1:
                return ap
            names = "abcd"[:len(shape)]
            return ap.rearrange(f"p ({' '.join(names)}) -> p {' '.join(names)}",
                                **dict(zip(names[1:], shape[1:])))

        ada_raw = part(0, ADA_REST_SLOTS, 2, D)
        ada_acc = part(6144, D)
        gate_c = part(7168, CCT, SEQ)
        u_pad = part(8192, CCT, SEQ // GRID_W, GRID_W + 2)
        conv_acc = part(9248, CCT, SEQ)
        conv_y = part(10272, CCT, SEQ)
        alibi = part(0, SWA_HQ, 384)
        a_pad = part(3072, CCT, SEQ + CONV_K - 1)
        sig = part(4216, CCT, SEQ)
        acc31 = part(5240, CCT, SEQ)
        q_ab = part(6264, CCT, SEQ)
        k_ab = part(7288, SWA_HKV, SEQ)
        v_ab = part(7800, TOKT, P)
        p_ab = part(8056, 2, 2, 384)
        pT_ab = part(9592, 2, 2, 384)
        ln_y = part(8056, TOKT, CONV_CH)
        ab_y = part(9592, CCT, SEQ)
        q_fox = part(0, KT, SEQ)
        k_fox = part(2048, KT, SEQ)
        decay = part(4096, FOX_H, 384)
        pT_fox = part(10240, 2, 2, 384)
        v_fox = tmp
        p_fox = xn[:, :, :].rearrange("p t d -> p (t d)")[:, 0:1536].rearrange(
            "p (b h s) -> p b h s", b=2, h=2)
        ada_sum0 = tmp[:, :, :].rearrange("p t d -> p (t d)")

        landed = [sem(f"landed{i}") for i in range(NSLOT)]
        hi_ready = sem("hi_ready")
        raw_done = sem("raw_done")
        w_used = sem("w_used")
        x_landed = sem("x_landed")
        par_landed = sem("par_landed")
        bias_landed = sem("bias_landed")
        row_g1_landed = sem("row_g1_landed")
        misc_landed = sem("misc_landed")
        consts = sem("consts")
        par_ps = sem("par_ps")
        par_ready = sem("par_ready")
        cond_ready = sem("cond_ready")
        ada_landed = [sem(f"ada_landed{i}") for i in range(ADA_REST_SLOTS)]
        ada_b_landed = sem("ada_b_landed")
        ada_scaled = sem("ada_scaled")
        ada_added = sem("ada_added")
        ada_cleared = sem("ada_cleared")
        ada_ps = sem("ada_ps")
        ada_row_a = sem("ada_row_a")
        ada_row_v = sem("ada_row_v")
        ada0_cleared = sem("ada0_cleared")
        g2_row_landed = sem("g2_row_landed")
        y_tok0 = sem("y_tok0")
        sq_done = sem("sq_done")
        std_done = sem("std_done")
        rstd_done = sem("rstd_done")
        t_done = sem("t_done")
        x_new = sem("x_new")
        xn_part = sem("xn_part")
        xn_done = sem("xn_done")
        xT_ps = sem("xT_ps")
        xT_hi_ok = sem("xT_hi_ok")
        xT_ok = sem("xT_ok")
        rows_landed = sem("rows_landed")
        out_landed = sem("out_landed")
        up_tok0 = sem("up_tok0")
        sil_done = sem("sil_done")
        hid_done = sem("hid_done")
        hT_ps = sem("hT_ps")
        hT_hi_ok = sem("hT_hi_ok")
        hT_ok = sem("hT_ok")
        evac_a = sem("evac_a")
        evac_v = sem("evac_v")
        pads = sem("pads")
        tap = sem("tap")
        conv_done = sem("conv_done")
        yT_hi_ok = sem("yT_hi_ok")
        yT_ok = sem("yT_ok")
        bias_built = sem("bias_built")
        k_landed = sem("k_landed")
        ln_ps = sem("ln_ps")
        ln_stat = sem("ln_stat")
        ln_std = sem("ln_std")
        ln_out = sem("ln_out")
        lnT_ps = sem("lnT_ps")
        ab_y_ok = sem("ab_y_ok")
        s_ps = sem("s_ps")
        s_sb = sem("s_sb")
        m_chain = sem("m_chain")
        m_ok = sem("m_ok")
        e_done = sem("e_done")
        p_done = sem("p_done")
        pT_psd = sem("pT_psd")
        pT_okA = sem("pT_okA")
        pT_okV = sem("pT_okV")
        o_ps = sem("o_ps")
        oT_hi_ok = sem("oT_hi_ok")
        oT_ok = sem("oT_ok")
        zf_ok = sem("zf_ok")
        zf_v = sem("zf_v")
        zf_a = sem("zf_a")
        zf_p = sem("zf_p")
        zf_z = sem("zf_z")
        zf_e = sem("zf_e")
        pool_chain = sem("pool_chain")
        d_ps = sem("d_ps")
        d_raw = sem("d_raw")
        d_ok = sem("d_ok")

        def slot_of(n):
            return n % NSLOT

        def weight_count(n):
            return n - ADA_FIRST + 1

        def y_unit(b):
            return BASE[b] + UNITS.get(b, FFN_UNITS) - 1

        def ffn_index(s):
            return (FFN0, FFN1, FFN2, FFN3, FFN4).index(s)

        block = ctx.enter_context(nc.Block())

        @block.sync
        def _(sp):
            def load(n, j, dst_src):
                if not (isinstance(j, int) and n + NSLOT * j < NSLOT):
                    sp.wait_ge(raw_done, n - NSLOT + 1 + NSLOT * j)
                assert len(dst_src) == 2
                for dst, src in dst_src:
                    sp.dma_start(dst, src).then_inc(landed[slot_of(n)], 16)

            def columns(n, wd, k0, c0, width, kts=4):
                dst = raw[:, slot_of(n), 0:kts * width].rearrange("p (k c) -> p k c", k=kts)
                h = kts // 2
                return [(dst[:, i:i + h, :], wd[:, k0 + i:k0 + i + h, c0:c0 + width]) for i in (0, h)]

            def pair_rows(n, wd, k):
                dst = raw[:, slot_of(n), :].rearrange("p (k c) -> p k c", k=2)
                return [(dst[:, i:i + 1, :], wd[:, bass.ds(k + i, 1), :]) for i in range(2)]

            def up_unit(n, gate, up, k0, c0):
                dst = raw[:, slot_of(n), :].rearrange("p (k h c) -> p k h c", k=4, h=2)
                return [(dst[:, :, i, :], wd[:, k0:k0 + 4, bass.ds(c0, FCH)]) for i, wd in enumerate((gate, up))]

            def load_rows(s):
                sp.wait_ge(xn_done, 2 * s + 2)
                post = w["final_g"].rearrange("(a d) -> a d", a=1).to_broadcast([P, D]) if s == FFN0 \
                    else norm_row(*POST_ROW[s])
                sp.dma_start(rows[:, 1, :], post).then_inc(rows_landed, 16)
                if s < FFN4:
                    sp.dma_start(rows[:, 0, :], norm_row(*PRE_ROW[s + 1])).then_inc(rows_landed, 16)

            def load_ffn(s):
                gate, up, down = ffn_weights(s)
                n = BASE[s]
                load(n, 0, up_unit(n, gate, up, 0, 0))
                load(n + 1, 0, up_unit(n + 1, gate, up, 4, 0))
                with sp.Fori(1, NCH) as j:
                    load(n - 1, j, up_unit(n - 1, gate, up, 0, j * FCH))
                    load(n, j, up_unit(n, gate, up, 4, j * FCH))
                    load(n + 1, j, pair_rows(n + 1, down, j * 2 - 2))
                load_rows(s)
                load(n + FFN_UNITS - 1, 0, pair_rows(n + FFN_UNITS - 1, down, 2 * NCH - 2))

            sp.dma_start(par_rows[C_COND:C_COND + 8, 0, :], w["c"].rearrange("b (r q) -> (b r) q", q=P)).then_inc(par_landed, 16)
            sp.dma_start(par_rows[C_CONVW:C_CONVW + 24, 0, :], w["conv_w"].rearrange("l k (r q) -> (l k r) q", q=P)).then_inc(par_landed, 16)
            sp.dma_start(par_rows[C_CB:C_CB + 4, 0, :], w["conv_b_2"].rearrange("l (r q) -> (l r) q", q=P)).then_inc(par_landed, 16)
            sp.dma_start(par_rows[C_LNG:C_LNG + 4, 0, :], w["conv_ln_g_2"].rearrange("l (r q) -> (l r) q", q=P)).then_inc(par_landed, 16)
            sp.dma_start(par_rows[C_LNB:C_LNB + 4, 0, :], w["conv_ln_b_2"].rearrange("l (r q) -> (l r) q", q=P)).then_inc(par_landed, 16)
            sp.dma_start(par_rows[0:N_CW31, 1, :], w["conv_w_2"].rearrange("l k (r q) -> (l k r) q", q=P)).then_inc(par_landed, 16)
            sp.wait_ge(ada0_cleared, 1)
            sp.dma_start(ada_sum0[0:1, :], w["ada_b"][:, 0:2 * D]).then_inc(bias_landed, 16)
            for n in range(ADA_FIRST):
                load(n, 0, [(raw[:, slot_of(n), h * D:(h + 1) * D], ada_w[:, n, h * D:(h + 1) * D]) for h in range(2)])
                if n == 0:
                    sp.dma_start(x[:, :, :], x_d).then_inc(x_landed, 16)
                    sp.dma_start(rows[:, 0, :], w["norm1_g"].to_broadcast([P, D])).then_inc(row_g1_landed, 16)
            n = BASE[CONV]
            for half in range(2):
                for section in (1, 2, 0):
                    for k0 in (0, 4):
                        load(n, 0, columns(n, conv_in, k0, section * D + half * 512, 512))
                        n += 1
            for k in range(0, KT, 2):
                load(n, 0, pair_rows(n, conv_out, k))
                n += 1
            sp.dma_start(sinks[:, :], w["swa_sinks_2"].to_broadcast([P, SWA_HQ])).then_inc(misc_landed, 16)
            sp.dma_start(b_f[:, :], w["fox_b_f_2"].to_broadcast([P, FOX_H])).then_inc(misc_landed, 16)
            sp.dma_start(zf_raw[:, :, :], fox_in[:, :, 3 * D:3 * D + FOX_H]).then_inc(misc_landed, 16)
            if last_sub >= FFN0:
                load_ffn(FFN0)
            if last_sub >= FFN1:
                load_ffn(FFN1)
            if last_sub >= AB:
                n = BASE[AB]
                for c0 in (0, CONV_CH):
                    for k0 in (0, 4):
                        load(n, 0, columns(n, ab_in, k0, c0, 512))
                        n += 1
                for k0 in (0, 4):
                    load(n, 0, columns(n, ab_in, k0, 2 * CONV_CH, 512))
                    n += 1
                load(n, 0, columns(n, ab_in, 0, 1536, 256, kts=8))
                n += 1
                load_rows(AB)
                for k in (4, 6, 0, 2):
                    load(n, 0, pair_rows(n, ab_out, k))
                    n += 1
            if last_sub >= FFN2:
                load_ffn(FFN2)
            if last_sub >= FFN3:
                load_ffn(FFN3)
            if last_sub >= FOX:
                n = BASE[FOX]
                for c0 in range(0, 3 * D, 512):
                    for k0 in (0, 4):
                        load(n, 0, columns(n, fox_in, k0, c0, 512))
                        n += 1
                load_rows(FOX)
                for k in range(0, KT, 2):
                    load(n, 0, pair_rows(n, fox_out, k))
                    n += 1
            if last_sub >= FFN4:
                load_ffn(FFN4)
            for t in range(TOKT):
                sp.wait_ge(x_new, x_count(last_sub, t))
                sp.dma_start(out_d[:, t, :], x[:, t, :]).then_inc(out_landed, 16)
            sp.wait_ge(out_landed, 16 * TOKT)

        @block.tensor
        def _(pe):
            def product(o, a_hi, a_lo, b_hi, b_lo, first, last):
                pe.matmul(o, a_hi, b_lo, start=first, stop=False, skip_group_check=True)
                pe.matmul(o, a_hi, b_hi, start=False, stop=False, skip_group_check=True)
                return pe.matmul(o, a_lo, b_hi, start=False, stop=last, skip_group_check=True)

            def unit(n, j=0):
                pe.wait_ge(raw_done, n + 1 + NSLOT * j)
                return w_hi[:, slot_of(n), :], w_lo[:, slot_of(n), :]

            def tok(t):
                return slice(t * P, (t + 1) * P)

            def turn_x(s):
                for t in range(TOKT):
                    pe.wait_ge(xn_done, 2 * s + t + 1)
                    for h in range(2):
                        for k in range(4):
                            tr = pe.transpose(ps[:, 2 * t + h, tok(k)], xn[:, t, tok(4 * h + k)], ident[:, :])
                        tr.then_inc(xT_ps, 1)

            def up_part(n, k0, t, j=0):
                hi, lo = unit(n, j)
                for k in range(4):
                    c = slice(k * 512, (k + 1) * 512)
                    mm = product(ps[:, t, :], xT_hi[:, k0 + k, tok(t)], xT_lo[:, k0 + k, tok(t)], hi[:, c], lo[:, c],
                                 k0 + k == 0, k0 + k == KT - 1)
                return mm

            def turn_hid(s, j):
                for f in range(2):
                    for t in range(TOKT):
                        tr = pe.transpose(ps[:, 2, f * SEQ + t * P:f * SEQ + (t + 1) * P], hid[:, t, tok(f)], ident[:, :])
                tr.then_inc(hT_ps, 1)

            def down_part(n, aT_hi, aT_lo, k0, t, first, last, j=0):
                hi, lo = unit(n, j)
                for k in range(2):
                    for h in range(2):
                        c = slice(k * D + h * 512, k * D + (h + 1) * 512)
                        mm = product(ps[:, 4 + 2 * t + h, :], aT_hi[:, k0 + k, tok(t)], aT_lo[:, k0 + k, tok(t)],
                                     hi[:, c], lo[:, c], first and k == 0, last and k == 1)
                return mm

            def ffn(s):
                f, n = ffn_index(s), BASE[s]
                for t in range(TOKT):
                    pe.wait_ge(xT_ok, 4 * s + 2 * t + 2)
                    mm = up_part(n, 0, t)
                    if t == 1:
                        mm.then_inc(w_used, 1)
                    up_part(n + 1, 4, t).then_inc(w_used if t else up_tok0, 1)

                def chunk(n_a, j_hid, j, first):
                    pe.wait_ge(hid_done, 2 * (NCH * f + j_hid + 1))
                    up_part(n_a, 0, 0, j)
                    up_part(n_a, 0, 1, j).then_inc(w_used, 1)
                    turn_hid(s, j_hid)
                    up_part(n_a + 1, 4, 0, j).then_inc(up_tok0, 1)
                    up_part(n_a + 1, 4, 1, j).then_inc(w_used, 1)
                    pe.wait_ge(hT_ok, NCH * f + j_hid + 1)
                    down_part(n_a + 2, hT_hi, hT_lo, 0, 0, first, False, j)
                    down_part(n_a + 2, hT_hi, hT_lo, 0, 1, first, False, j).then_inc(w_used, 1)

                chunk(n + 2, 0, 0, True)
                with pe.Fori(1, NCH - 1) as i:
                    chunk(n + 2, i, i, False)
                pe.wait_ge(hid_done, 2 * NCH * (f + 1))
                turn_hid(s, NCH - 1)
                pe.wait_ge(hT_ok, NCH * (f + 1))
                last = n + FFN_UNITS - 1
                down_part(last, hT_hi, hT_lo, 0, 0, False, True).then_inc(y_tok0, 1)
                down_part(last, hT_hi, hT_lo, 0, 1, False, True).then_inc(w_used, 1)

            def channel_chunk(n, bank):
                for u in range(2):
                    hi, lo = unit(n + u)
                    for k in range(4):
                        for c in range(4):
                            w_k = [v[:, k * 512 + c * P:k * 512 + (c + 1) * P] for v in (hi, lo)]
                            mm = product(ps[:, bank + c // 2, (c % 2) * SEQ:(c % 2 + 1) * SEQ], *w_k,
                                         xT_hi[:, 4 * u + k, :], xT_lo[:, 4 * u + k, :],
                                         u == 0 and k == 0 and c % 2 == 0, u == 1 and k == 3)
                    mm.then_inc(w_used, 1)

            def token_chunk(n, bank):
                for u in range(2):
                    hi, lo = unit(n + u)
                    for t in range(TOKT):
                        for k in range(4):
                            c = slice(k * 512, (k + 1) * 512)
                            mm = product(ps[:, bank + t, :], xT_hi[:, 4 * u + k, tok(t)], xT_lo[:, 4 * u + k, tok(t)],
                                         hi[:, c], lo[:, c], u == 0 and k == 0, u == 1 and k == 3)
                    mm.then_inc(w_used, 1)

            def row_everywhere(banks, acc):
                for h in range(2):
                    mm = pe.matmul(ps[:, banks + h, :], ones[:, :], acc[:, h * 512:(h + 1) * 512], start=True, stop=True)
                mm.then_inc(ada_ps, 1)

            def attention(items, first_item, q, k_of, v_of):
                def scores(i):
                    for g in range(2):
                        r = slice(g * DH, (g + 1) * DH)
                        pe.matmul(ps[:, 2 * (i % 2) + g, 0:P], q[r, i, 0:P], k_of(i)[r, 0:P], start=True, stop=True)
                    for g in range(2):
                        r = slice(g * DH, (g + 1) * DH)
                        mm = pe.matmul(ps[:, 2 * (i % 2) + g, P:3 * P], q[r, i, P:SEQ], k_of(i)[r, :], start=True, stop=True)
                    mm.then_inc(s_ps, 1)

                scores(0)
                scores(1)
                for i in range(items):
                    item = first_item + i
                    pe.wait_ge(p_done, item + 1)
                    for g in range(2):
                        for b in range(3):
                            p = (p_ab if q is q_ab else p_fox)[:, i % 2, g, tok(b)]
                            tr = pe.transpose(ps[:, 4 + g, tok(b)], p, ident[:, :])
                    tr.then_inc(pT_psd, 1)
                    if i + 2 < items:
                        scores(i + 2)
                    pe.wait_ge(pT_okA, item + 1)
                    pe.wait_ge(pT_okV, item + 1)
                    for g in range(2):
                        pT = (pT_ab if q is q_ab else pT_fox)[:, i % 2, g, :]
                        r = slice(g * DH, (g + 1) * DH)
                        o_bank = 6 + i % 2
                        pe.matmul(ps[r, o_bank, 0:P], v_of(i, g, 0), pT[:, 0:P], start=True, stop=True)
                        pe.matmul(ps[r, o_bank, P:SEQ], v_of(i, g, 0), pT[:, P:2 * P], start=True, stop=False)
                        mm = pe.matmul(ps[r, o_bank, P:SEQ], v_of(i, g, 1), pT[:, 2 * P:3 * P], start=False, stop=True)
                    mm.then_inc(o_ps, 1)

            pe.wait_ge(consts, 1)
            pe.wait_ge(par_landed, 96)
            pe.transpose(ps[:, 6, 0:N_PAR], par_rows[0:N_PAR, 0, :], ident[0:N_PAR, 0:N_PAR])
            pe.transpose(ps[:, 7, 0:N_CW31], par_rows[0:N_CW31, 1, :], ident[0:N_CW31, 0:N_CW31]).then_inc(par_ps, 1)
            pe.wait_ge(raw_done, ADA_FIRST)
            row_everywhere(0, ada_sum0[:, 0:D])
            row_everywhere(2, ada_sum0[:, D:2 * D])

            turn_x(CONV)
            pe.wait_ge(xT_ok, 4)
            n = BASE[CONV]
            pe.wait_ge(par_ready, 3)
            for m in range(6):
                if m == 3:
                    pe.wait_ge(evac_a, 1)
                if m > 3:
                    pe.wait_ge(evac_v, m - 3)
                channel_chunk(n + 2 * m, 2 * (m % 3))
                if m == 2:
                    pe.wait_ge(ada_added, 4)
                    row_everywhere(6, tmp[:, 1, :])
                if m == 4:
                    pe.wait_ge(ada_added, 8)
                    pe.wait_ge(ada_row_a, 2)
                    row_everywhere(6, ada_acc)
            pe.wait_ge(evac_v, 4)
            pe.wait_ge(ada_row_a, 3)
            for i in range(4):
                pe.wait_ge(yT_ok, i // 2 + 1)
                first, last = i == 0, i == 3
                mm = down_part(n + 12 + i, yT_hi, yT_lo, 2 * i, 0, first, last)
                if last:
                    mm.then_inc(y_tok0, 1)
                down_part(n + 12 + i, yT_hi, yT_lo, 2 * i, 1, first, last).then_inc(w_used, 1)
                if i == 2:
                    pe.wait_ge(ada_added, 12)
                    row_everywhere(0, tmp[:, 1, :])
            pe.wait_ge(ada_added, 16)
            row_everywhere(2, ada_acc)

            def mixer_out(s, n, order, waits):
                for i, k0 in enumerate(order):
                    pe.wait_ge(*waits[i])
                    first, last = i == 0, i == len(order) - 1
                    mm = down_part(n + i, yT_hi, yT_lo, k0, 0, first, last)
                    if last:
                        mm.then_inc(y_tok0, 1)
                    down_part(n + i, yT_hi, yT_lo, k0, 1, first, last).then_inc(w_used, 1)

            if last_sub >= FFN0:
                turn_x(FFN0)
                ffn(FFN0)
            if last_sub >= FFN1:
                turn_x(FFN1)
                ffn(FFN1)
            if last_sub >= AB:
                turn_x(AB)
                pe.wait_ge(xT_ok, 4 * AB + 4)
                n = BASE[AB]
                channel_chunk(n, 0)
                channel_chunk(n + 2, 2)
                channel_chunk(n + 4, 4)
                hi, lo = unit(n + 6)
                for k in range(KT):
                    product(ps[:, 6, 0:SEQ], hi[:, k * 256:k * 256 + P], lo[:, k * 256:k * 256 + P], xT_hi[:, k, :], xT_lo[:, k, :],
                            k == 0, k == KT - 1)
                for t in range(TOKT):
                    for k in range(KT):
                        c = slice(k * 256 + P, (k + 1) * 256)
                        mm = product(ps[:, 7, tok(t)], xT_hi[:, k, tok(t)], xT_lo[:, k, tok(t)], hi[:, c], lo[:, c],
                                     k == 0, k == KT - 1)
                mm.then_inc(w_used, 1)
                pe.wait_ge(evac_v, 5)
                pe.wait_ge(evac_a, 7)
                pe.wait_ge(k_landed, 32)
                attention(4, 0, q_ab, lambda i: k_ab[:, i // 2, :],
                          lambda i, g, b: v_ab[:, b, i // 2 * DH:(i // 2 + 1) * DH])
                pe.wait_ge(conv_done, 1)
                for t in range(TOKT):
                    for c in range(CCT):
                        tr = pe.transpose(ps[:, t, tok(c)], acc31[:, c, tok(t)], ident[:, :])
                    tr.then_inc(ln_ps, 1)
                for t in range(TOKT):
                    pe.wait_ge(ln_out, t + 1)
                    for c in range(CCT):
                        tr = pe.transpose(ps[:, 2 + c // 2, (c % 2) * SEQ + t * P:(c % 2) * SEQ + (t + 1) * P],
                                          ln_y[:, t, tok(c)], ident[:, :])
                    tr.then_inc(lnT_ps, 1)
                mixer_out(AB, n + 7, (4, 6, 0, 2), [(oT_ok, 4), (oT_ok, 4), (yT_ok, 3), (yT_ok, 3)])
            if last_sub >= FFN2:
                turn_x(FFN2)
                ffn(FFN2)
            if last_sub >= FFN3:
                turn_x(FFN3)
                ffn(FFN3)
            if last_sub >= FOX:
                turn_x(FOX)
                pe.wait_ge(xT_ok, 4 * FOX + 4)
                pe.wait_ge(zf_ok, 2)
                for t in range(TOKT):
                    for k in range(KT):
                        mm = product(ps[:, 6, t * FOX_H:(t + 1) * FOX_H], xT_hi[:, k, tok(t)], xT_lo[:, k, tok(t)],
                                     zf_hi[:, k, :], zf_lo[:, k, :], k == 0, k == KT - 1)
                mm.then_inc(zf_p, 1)
                n = BASE[FOX]
                logf = zf[:, 5, :]
                c_tok = zf[:, 6, :]

                def pairs(first):
                    for i in (first, first + 1):
                        if i >= 2:
                            pe.wait_ge(d_raw, i - 1)
                        for g in range(2):
                            h = 2 * i + g
                            mm = pe.matmul(ps[:, 6 + i % 2, g * SEQ:(g + 1) * SEQ],
                                           ident[0:FOX_H, h:h + 1].to_broadcast([FOX_H, P]), cT[:, :], start=True, stop=True)
                        mm.then_inc(d_ps, 1)

                channel_chunk(n, 0)
                pe.wait_ge(zf_v, 1)
                pe.matmul(ps[:, 6, 64:80], upper[:, :], logf[:, 0:16], start=True, stop=True)
                pe.matmul(ps[:, 6, 80:96], upper[:, :], logf[:, 16:32], start=True, stop=False)
                pe.matmul(ps[:, 6, 80:96], ones[:, :], logf[:, 0:16], start=False, stop=True).then_inc(zf_p, 1)
                channel_chunk(n + 2, 2)
                pe.wait_ge(zf_a, 1)
                for t in range(TOKT):
                    tr = pe.transpose(ps[0:FOX_H, 6, P + t * P:P + (t + 1) * P], c_tok[:, t * 16:(t + 1) * 16], ident[:, :])
                tr.then_inc(zf_p, 1)
                channel_chunk(n + 4, 4)
                pe.wait_ge(zf_a, 2)
                pairs(0)
                pe.wait_ge(evac_a, 8)
                channel_chunk(n + 6, 0)
                pairs(2)
                pe.wait_ge(evac_a, 9)
                token_chunk(n + 8, 2)
                pairs(4)
                pe.wait_ge(evac_a, 10)
                token_chunk(n + 10, 4)
                pairs(6)
                pe.wait_ge(evac_a, 13)
                pe.wait_ge(d_raw, 8)
                attention(8, 4, q_fox, lambda i: k_fox[:, i, :],
                          lambda i, g, b: v_fox[:, b, (2 * i + g) * DH:(2 * i + g + 1) * DH])
                mixer_out(FOX, n + 12, (0, 2, 4, 6), [(oT_ok, 12)] * 4)
            if last_sub >= FFN4:
                turn_x(FFN4)
                ffn(FFN4)

        @block.scalar
        def _(act):
            warmed = [0]

            def warm_up(func):
                c = warmed[0]
                warmed[0] += 1
                act.activation(warm[:, c:c + 1], eps[:, 0:1], func)

            def split(n, j=0, wait_used=True):
                v = weight_count(n) - 1
                if n >= TOTAL or n >= limit:
                    return
                act.wait_ge(landed[slot_of(n)], 32 * (n // NSLOT + 1 + j) if isinstance(j, int) else j * 32 + 32 * (n // NSLOT + 1))
                if not (isinstance(j, int) and v + NSLOT * j < NSLOT):
                    act.wait_ge(w_used, v - NSLOT + 1 + NSLOT * j)
                act.activation(w_hi[:, slot_of(n), :], raw[:, slot_of(n), :], ACT.Copy).then_inc(hi_ready, 1)

            limit = y_unit(last_sub) + 1

            def root(e, t):
                act.wait_ge(sq_done, 2 * e + t + 1)
                c = 2 * e + t
                act.activation(stat[:, 1, c:c + 1], stat[:, 0, c:c + 1], ACT.Sqrt, bias=eps[:, 0:1]).then_inc(std_done, 1)

            def square(e, t, src):
                c = 2 * e + t
                act.activation(xn[:, t, :], src, ACT.Square, scale=D ** -0.5, accum_out=stat[:, 0, c:c + 1]).then_inc(sq_done, 1)

            def close(b):
                warm_up(ACT.Sqrt)
                for t in range(TOKT):
                    if b > FFN0:
                        act.wait_ge(w_used if t else y_tok0, weight_count(y_unit(b)) if t else b + 1)
                        square(post_event(b), t, ps[:, 4 + 2 * t:6 + 2 * t, :].rearrange("p b n -> p (b n)"))
                        root(post_event(b), t)

            def mean_square_x(e, t, count):
                act.wait_ge(x_new, count)
                square(e, t, x[:, t, :])
                root(e, t)

            def open_sub(s, func):
                if s > CONV:
                    for t in range(TOKT):
                        mean_square_x(pre_event(s), t, x_count(s - 1, t))
                for t in range(TOKT):
                    for h in range(2):
                        act.wait_ge(xT_ps, 4 * s + 2 * t + h + 1)
                        act.activation(xT_hi[:, 4 * h:4 * h + 4, t * P:(t + 1) * P],
                                       ps[:, 2 * t + h, :].rearrange("p (k c) -> p k c", k=4), ACT.Copy).then_inc(xT_hi_ok, 1)
                if func is not None:
                    warm_up(func)

            def ffn(s):
                f, n = ffn_index(s), BASE[s]
                v = weight_count(n)

                def chunk(j, last=False):
                    if not last or n + 3 * j + 2 < limit:
                        split(n + 2, j) if not isinstance(j, int) else split(n + 2 + 3 * j)
                    for t in range(TOKT):
                        if t == 0:
                            act.wait_ge(up_tok0, NCH * f + 1 + j)
                        else:
                            act.wait_ge(w_used, v + 1 if isinstance(j, int) and j == 0 else v + 3 * j)
                        act.activation(sil[:, t, :], ps[:, t, 0:FCH], ACT.Silu).then_inc(sil_done, 1)
                    for c in (3, 4):
                        split(n + c, j) if not isinstance(j, int) else split(n + c + 3 * j)
                    act.wait_ge(hT_ps, NCH * f + 1 + j)
                    act.activation(hT_hi[:, :, :], ps[:, 2, :].rearrange("p (f c) -> p f c", f=2), ACT.Copy).then_inc(hT_hi_ok, 1)

                chunk(0)
                with act.Fori(1, NCH - 1) as j:
                    chunk(j)
                chunk(NCH - 1, True)

            act.wait_ge(par_ps, 1)
            act.wait_ge(consts, 1)
            act.activation(cond[:, :], ps[:, 6, C_COND:C_COND + KT], ACT.Silu).then_inc(par_ready, 1)
            act.activation(par[:, :], ps[:, 6, 0:N_PAR], ACT.Copy).then_inc(par_ready, 1)
            act.activation(cw31[:, :], ps[:, 7, 0:N_CW31], ACT.Copy).then_inc(par_ready, 1)
            act.wait_ge(par_ready, 3)
            act.wait_ge(x_landed, 16)
            for t in range(TOKT):
                square(0, t, x[:, t, :])
                root(0, t)
            split(BASE[CONV])
            split(BASE[CONV] + 1)
            act.wait_ge(ada_ps, 1)
            act.activation(rows[:, 3, :], ps[:, 0:2, :].rearrange("p b n -> p (b n)"), ACT.Copy).then_inc(ada_row_a, 1)
            open_sub(CONV, None)

            def ada_scale(r):
                act.wait_ge(ada_landed[r % ADA_REST_SLOTS], 16 * (r // ADA_REST_SLOTS + 1))
                for i in range(2):
                    k = 2 * (r % 4) + i
                    a = act.activation(ada_raw[:, r % ADA_REST_SLOTS, i, :], ada_raw[:, r % ADA_REST_SLOTS, i, :], ACT.Copy,
                                       scale=cond[:, k:k + 1])
                a.then_inc(ada_scaled, 1)

            n = BASE[CONV]
            for k in range(2, 18):
                m = (k - 4) // 2
                if k % 2 == 0 and 0 <= m < 6:
                    act.wait_ge(w_used, weight_count(n + 2 * m + 1))
                    if m % 3 == 0:
                        if m == 3:
                            act.wait_ge(evac_v, 1)
                        act.activation(gate_c[:, :, :].rearrange("p a b -> p (a b)"),
                                       ps[:, 0:2, :].rearrange("p b n -> p (b n)"), ACT.Copy).then_inc(evac_a, 1)
                    if m % 3 == 2:
                        h = m // 3
                        act.wait_ge(evac_v, 2 * h + 2)
                        act.activation(yT_hi[:, 4 * h:4 * h + 4, :], conv_y[:, :, :], ACT.Copy).then_inc(yT_hi_ok, 1)
                split(n + k)
                ada_scale(k - 2)
                if k == 9:
                    act.wait_ge(ada_ps, 3)
                    act.activation(rows[:, 1, :], ps[:, 6:8, :].rearrange("p b n -> p (b n)"), ACT.Copy).then_inc(ada_row_a, 1)
                if k == 13:
                    act.wait_ge(ada_ps, 4)
                    act.activation(rows[:, 3, :], ps[:, 6:8, :].rearrange("p b n -> p (b n)"), ACT.Copy).then_inc(ada_row_a, 1)
            act.wait_ge(ada_ps, 6)
            act.activation(rows[:, 2, :], ps[:, 2:4, :].rearrange("p b n -> p (b n)"), ACT.Copy).then_inc(ada_row_a, 1)

            def attention(items, first_item, p, pT, kt0, sink, between):
                def exps(i):
                    item = first_item + i
                    c = 4 * item
                    act.wait_ge(m_ok, item + 1)
                    for b in range(2):
                        for g in range(2):
                            a = c + 2 * b + g
                            s = p[:, i % 2, g, 0:P] if b == 0 else p[:, i % 2, g, P:3 * P]
                            e = act.activation(s, s, ACT.Exp, bias=soft[:, 1, a:a + 1], accum_out=soft[:, 3, a:a + 1])
                    if sink:
                        e = act.activation(soft[:, 5, c:c + 4], soft[:, 2, c:c + 4], ACT.Exp)
                    e.then_inc(e_done, 1)

                exps(0)
                for i in range(items):
                    item = first_item + i
                    if i + 1 < items:
                        exps(i + 1)
                    act.wait_ge(pT_psd, item + 1)
                    act.activation(pT[:, i % 2, 0, :], ps[:, 4, 0:384], ACT.Copy).then_inc(pT_okA, 1)
                    act.wait_ge(o_ps, item + 1)
                    act.activation(yT_hi[:, kt0 + i, :], ps[:, 6 + i % 2, 0:SEQ], ACT.Copy).then_inc(oT_hi_ok, 1)
                    between(i)

            if last_sub >= FFN0:
                close(CONV)
                open_sub(FFN0, ACT.Silu)
                ffn(FFN0)
            if last_sub >= FFN1:
                close(FFN0)
                for t in range(TOKT):
                    mean_square_x(FINAL_EVENT, t, 3 + t)
                open_sub(FFN1, ACT.Silu)
                ffn(FFN1)
            if last_sub >= AB:
                close(FFN1)
                open_sub(AB, ACT.Sigmoid)
                n = BASE[AB]
                for k in range(2, 10):
                    if k == 7:
                        act.wait_ge(w_used, weight_count(n + 3))
                        act.activation(sig.rearrange("p a b -> p (a b)"), ps[:, 2:4, :].rearrange("p b n -> p (b n)"),
                                       ACT.Sigmoid).then_inc(evac_a, 1)
                    if k == 9:
                        act.wait_ge(w_used, weight_count(n + 5))
                        act.activation(q_ab.rearrange("p a b -> p (a b)"), ps[:, 4:6, :].rearrange("p b n -> p (b n)"),
                                       ACT.Copy).then_inc(evac_a, 1)
                        act.wait_ge(w_used, weight_count(n + 6))
                        for g in range(SWA_HKV):
                            r = slice(g * DH, (g + 1) * DH)
                            act.activation(k_ab[r, g, :], ps[r, 6, 0:SEQ], ACT.Copy).then_inc(evac_a, 1)
                        act.wait_ge(evac_a, 6)
                        act.dma_start(k_ab[DH:P, 0, :], k_ab[0:DH, 0, :]).then_inc(k_landed, 16)
                        act.dma_start(k_ab[0:DH, 1, :], k_ab[DH:P, 1, :]).then_inc(k_landed, 16)
                        act.activation(v_ab.rearrange("p a b -> p (a b)"), ps[:, 7, 0:SEQ], ACT.Copy).then_inc(evac_a, 1)
                    split(n + k)
                attention(4, 0, p_ab, pT_ab, 4, True, lambda i: None)
                warm_up(ACT.Sqrt)
                for t in range(TOKT):
                    act.wait_ge(ln_stat, t + 1)
                    act.activation(zf[:, 7, 8 * t + 2:8 * t + 3], zf[:, 7, 8 * t + 1:8 * t + 2], ACT.Sqrt, bias=eps[:, 0:1]).then_inc(ln_std, 1)
                warm_up(ACT.Silu)
                act.wait_ge(lnT_ps, 2)
                for c in range(CCT):
                    a = act.activation(ab_y[:, c, :], ps[:, 2 + c // 2, (c % 2) * SEQ:(c % 2 + 1) * SEQ], ACT.Silu,
                                       scale=par[:, C_LNG + c:C_LNG + c + 1], bias=par[:, C_LNB + c:C_LNB + c + 1])
                a.then_inc(ab_y_ok, 1)
                act.wait_ge(ab_y_ok, 1)
                act.activation(yT_hi[:, 0:4, :], ab_y, ACT.Copy).then_inc(yT_hi_ok, 1)
                for k in range(10, 13):
                    split(n + k)
            if last_sub >= FFN2:
                close(AB)
                open_sub(FFN2, ACT.Silu)
                ffn(FFN2)
            if last_sub >= FFN3:
                close(FFN2)
                open_sub(FFN3, ACT.Silu)
                ffn(FFN3)
            if last_sub >= FOX:
                close(FFN3)
                open_sub(FOX, ACT.Exp)
                n = BASE[FOX]
                split(n + 2)
                act.wait_ge(zf_z, 1)
                act.activation(zf[:, 2, :], zf[:, 1, :], ACT.Exp, scale=-1.0).then_inc(zf_e, 1)
                act.wait_ge(zf_e, 1)
                act.activation(zf[:, 3, :], zf[:, 2, :], ACT.Ln, bias=1.0).then_inc(zf_e, 1)

                def distances(i):
                    act.wait_ge(d_ps, i + 1)
                    for g in range(2):
                        h = 2 * i + g
                        s = ps[:, 6 + i % 2, g * SEQ:(g + 1) * SEQ]
                        act.activation(decay[:, h, 0:P], s[:, 0:P], ACT.Identity, bias=zf[:, 6, h:h + 1])
                        a = act.activation(decay[:, h, P:3 * P], s, ACT.Identity, bias=zf[:, 6, 16 + h:17 + h])
                    a.then_inc(d_raw, 1)

                for k in range(3, 15):
                    if k in (5, 7, 9, 11, 13):
                        m = (k - 5) // 2
                        act.wait_ge(w_used, weight_count(n + 2 * m + 1))
                        bank = (0, 2, 4, 0, 2, 4)[m]
                        dst = (q_fox[:, 0:4, :], q_fox[:, 4:8, :], k_fox[:, 0:4, :], k_fox[:, 4:8, :],
                               v_fox[:, :, 0:512])[m]
                        src = ps[:, bank:bank + 2, :]
                        if m < 4:
                            src = src.rearrange("p b (a c) -> p (b a) c", a=2)
                        act.activation(dst, src, ACT.Copy).then_inc(evac_a, 1)
                    if k == 5:
                        act.wait_ge(zf_p, 2)
                        act.activation(zf[:, 6, :], ps[:, 6, 64:96], ACT.Copy).then_inc(zf_a, 1)
                    if k == 7:
                        act.wait_ge(zf_p, 3)
                        act.activation(cT[:, :], ps[0:FOX_H, 6, P:P + SEQ], ACT.Copy, scale=-1.0).then_inc(zf_a, 1)
                    split(n + k)
                    if k in (9, 11, 13):
                        distances(k - 9)
                        distances(k - 8)
                act.wait_ge(w_used, weight_count(n + 11))
                act.activation(v_fox[:, :, 512:1024], ps[:, 4:6, :], ACT.Copy).then_inc(evac_a, 1)
                distances(6)
                distances(7)
                attention(8, 4, p_fox, pT_fox, 0, False, lambda i: None)
                for k in range(15, 18):
                    split(n + k)
            if last_sub >= FFN4:
                close(FOX)
                open_sub(FFN4, ACT.Silu)
                ffn(FFN4)
            if last_sub > FFN0:
                close(last_sub)

        @block.vector
        def _(dve):
            limit = y_unit(last_sub) + 1
            chained = [0]

            def link(ins):
                chained[0] += 1
                ins.then_inc(m_chain, 1)
                dve.wait_ge(m_chain, chained[0])

            def split(n, j=0):
                if n >= limit:
                    return
                dve.wait_ge(hi_ready, weight_count(n) + NSLOT * j)
                dve.tensor_tensor(w_lo[:, slot_of(n), :], raw[:, slot_of(n), :], w_hi[:, slot_of(n), :].bitcast(F32),
                                  ALU.subtract).then_inc(raw_done, 1)

            def reciprocal_root(e, t):
                c = 2 * e + t
                dve.wait_ge(std_done, c + 1)
                dve.reciprocal(stat[:, 2, c:c + 1], stat[:, 1, c:c + 1]).then_inc(rstd_done, 1)
                dve.wait_ge(rstd_done, c + 1)
                return stat[:, 2, c:c + 1]

            def output(t):
                return ps[:, 4 + 2 * t:6 + 2 * t, :].rearrange("p b n -> p (b n)")

            def close(b):
                if b > CONV:
                    dve.wait_ge(rows_landed, 16 * 2 * b if b < FFN4 else 16 * (2 * b - 1))
                for t in range(TOKT):
                    if b <= FFN0:
                        dve.wait_ge(w_used if t else y_tok0, weight_count(y_unit(b)) if t else b + 1)
                        dve.tensor_tensor(tmp[:, t, :], output(t), rows[:, 2 if b else 1, :], ALU.mult).then_inc(t_done, 1)
                        scale = 1.0
                    else:
                        r = reciprocal_root(post_event(b), t)
                        dve.scalar_tensor_tensor(tmp[:, t, :], output(t), r, rows[:, 1, :], ALU.mult, ALU.mult).then_inc(t_done, 1)
                        scale = 1.0 if b in (AB, FOX) else 0.5
                    dve.wait_ge(t_done, 2 * b + t + 1)
                    dve.scalar_tensor_tensor(x[:, t, :], tmp[:, t, :], scale, x[:, t, :], ALU.mult, ALU.add).then_inc(x_new, 1)

            def open_sub(s):
                for t in range(TOKT):
                    r = reciprocal_root(pre_event(s), t)
                    n = dve.scalar_tensor_tensor(xn[:, t, :], x[:, t, :], r, rows[:, 0, :], ALU.mult, ALU.mult)
                    if s <= FFN0:
                        n.then_inc(xn_part, 1)
                        dve.wait_ge(xn_part, 2 * s + t + 1)
                        n = dve.tensor_tensor(xn[:, t, :], xn[:, t, :], rows[:, 3, :], ALU.add)
                    n.then_inc(xn_done, 1)
                for t in range(TOKT):
                    for h in range(2):
                        at = xT_lo[:, 4 * h:4 * h + 4, t * P:(t + 1) * P]
                        dve.wait_ge(xT_hi_ok, 4 * s + 2 * t + h + 1)
                        dve.tensor_tensor(at, ps[:, 2 * t + h, :].rearrange("p (k c) -> p k c", k=4),
                                          xT_hi[:, 4 * h:4 * h + 4, t * P:(t + 1) * P].bitcast(F32), ALU.subtract).then_inc(xT_ok, 1)

            def ffn(s):
                f, n = ffn_index(s), BASE[s]

                def chunk(j):
                    fixed = isinstance(j, int)
                    at = (lambda c: split(n + c + 3 * j)) if fixed else (lambda c: split(n + c, j))
                    at(2) if not fixed or n + 2 + 3 * j < limit else None
                    for t in range(TOKT):
                        dve.wait_ge(sil_done, 2 * NCH * f + t + 1 + 2 * j)
                        dve.tensor_tensor(hid[:, t, :], ps[:, t, FCH:2 * FCH], sil[:, t, :], ALU.mult).then_inc(hid_done, 1)
                    at(3)
                    at(4)
                    dve.wait_ge(hT_hi_ok, NCH * f + 1 + j)
                    dve.tensor_tensor(hT_lo[:, :, :], ps[:, 2, :].rearrange("p (f c) -> p f c", f=2),
                                      hT_hi[:, :, :].bitcast(F32), ALU.subtract).then_inc(hT_ok, 1)

                chunk(0)
                with dve.Fori(1, NCH - 1) as j:
                    chunk(j)
                chunk(NCH - 1)

            dve.wait_ge(par_ready, 1)
            dve.wait_ge(bias_landed, 16)
            for k in range(KT):
                dve.wait_ge(landed[slot_of(k)], 32 * (k // NSLOT + 1))
                if k:
                    dve.wait_ge(raw_done, k)
                dve.scalar_tensor_tensor(ada_sum0, raw[:, slot_of(k), :], cond[:, k:k + 1], ada_sum0, ALU.mult, ALU.add)\
                    .then_inc(raw_done, 1)
            n = BASE[CONV]
            split(n)
            split(n + 1)
            dve.wait_ge(ada_ps, 2)
            dve.wait_ge(row_g1_landed, 16)
            dve.scalar_tensor_tensor(rows[:, 0, :], ps[:, 2:4, :].rearrange("p b n -> p (b n)"), 1.0, rows[:, 0, :],
                                     ALU.add, ALU.mult).then_inc(ada_row_v, 1)
            dve.wait_ge(ada_row_v, 1)
            dve.wait_ge(ada_row_a, 1)
            open_sub(CONV)
            dve.wait_ge(pads, 1)
            for k in range(2, 18):
                m = (k - 4) // 2
                if k % 2 == 0 and 0 <= m < 6 and m % 3:
                    h = m // 3
                    dve.wait_ge(w_used, weight_count(n + 2 * m + 1))
                    if m % 3 == 1:
                        dve.wait_ge(evac_a, h + 1)
                        for b in range(2):
                            u = dve.tensor_tensor(u_pad[:, 2 * b:2 * b + 2, :, 1:GRID_W + 1],
                                                  ps[:, 2 + b, :].rearrange("p (a r c) -> p a r c", a=2, r=4),
                                                  gate_c[:, 2 * b:2 * b + 2, :].rearrange("p a (r c) -> p a r c", r=4), ALU.mult)
                        u.then_inc(evac_v, 1)
                        dve.wait_ge(evac_v, 2 * h + 1)
                        for i, tp in enumerate((1, 0, 2)):
                            for c in range(CCT):
                                wt = C_CONVW + tp * KT + 4 * h + c
                                o = conv_acc[:, c, :].rearrange("p (r c) -> p r c", r=4)
                                src = u_pad[:, c, :, tp:tp + GRID_W]
                                if i == 0:
                                    o = dve.tensor_scalar(o, src, par[:, wt:wt + 1], None, ALU.mult)
                                else:
                                    dve.wait_ge(tap, 12 * h + 4 * (i - 1) + c + 1)
                                    o = dve.scalar_tensor_tensor(o, src, par[:, wt:wt + 1], o, ALU.mult, ALU.add)
                                o.then_inc(tap, 1)
                    else:
                        dve.wait_ge(tap, 12 * h + 12)
                        if h:
                            dve.wait_ge(yT_hi_ok, h)
                        dve.tensor_tensor(conv_y.rearrange("p a b -> p (a b)"), ps[:, 4:6, :].rearrange("p b n -> p (b n)"),
                                          conv_acc.rearrange("p a b -> p (a b)"), ALU.mult).then_inc(evac_v, 1)
                        dve.wait_ge(yT_hi_ok, h + 1)
                        dve.tensor_tensor(yT_lo[:, 4 * h:4 * h + 4, :], conv_y, yT_hi[:, 4 * h:4 * h + 4, :].bitcast(F32),
                                          ALU.subtract).then_inc(yT_ok, 1)
                split(n + k)
            dve.wait_ge(ada_ps, 5)
            dve.wait_ge(g2_row_landed, 16)
            dve.scalar_tensor_tensor(rows[:, 0, :], ps[:, 0:2, :].rearrange("p b n -> p (b n)"), 1.0, rows[:, 0, :],
                                     ALU.add, ALU.mult).then_inc(ada_row_v, 1)
            dve.wait_ge(ada_row_v, 2)
            dve.wait_ge(ada_row_a, 4)
            close(CONV)

            def attention(items, first_item, p, bias_of, sink, idle):
                def scaled(i):
                    item = first_item + i
                    c = 4 * item
                    bank = 2 * (i % 2)
                    dve.wait_ge(s_ps, item + 1)
                    dve.scalar_tensor_tensor(p[:, i % 2, :, :], ps[:, bank:bank + 2, 0:384], DH ** -0.5, bias_of(i),
                                             ALU.mult, ALU.add).then_inc(s_sb, 1)
                    dve.wait_ge(s_sb, item + 1)
                    for b in range(2):
                        d = p[:, i % 2, :, 0:P] if b == 0 else p[:, i % 2, :, P:3 * P]
                        mx = dve.tensor_reduce(soft[:, 0, c + 2 * b:c + 2 * b + 2], d, AX_X, ALU.max)
                        if b == 1:
                            link(mx)
                    if sink is not None:
                        s4 = sink(i)
                        link(dve.tensor_tensor(soft[:, 4, c:c + 4].rearrange("p (b g) -> p b g", b=2),
                                               soft[:, 0, c:c + 4].rearrange("p (b g) -> p b g", b=2), s4, ALU.max))
                        link(dve.tensor_tensor(soft[:, 2, c:c + 4].rearrange("p (b g) -> p b g", b=2), s4,
                                               soft[:, 4, c:c + 4].rearrange("p (b g) -> p b g", b=2), ALU.subtract))
                        dve.tensor_scalar(soft[:, 1, c:c + 4], soft[:, 4, c:c + 4], -1.0, None, ALU.mult).then_inc(m_ok, 1)
                    else:
                        dve.tensor_scalar(soft[:, 1, c:c + 4], soft[:, 0, c:c + 4], -1.0, None, ALU.mult).then_inc(m_ok, 1)

                def normed(i):
                    item = first_item + i
                    c = 4 * item
                    dve.wait_ge(e_done, item + 1)
                    z = soft[:, 3, c:c + 4]
                    if sink is not None:
                        link(dve.tensor_tensor(soft[:, 6, c:c + 4], z, soft[:, 5, c:c + 4], ALU.add))
                        z = soft[:, 6, c:c + 4]
                    link(dve.reciprocal(soft[:, 7, c:c + 4], z))
                    for b in range(2):
                        for g in range(2):
                            d = p[:, i % 2, g, 0:P] if b == 0 else p[:, i % 2, g, P:3 * P]
                            a = c + 2 * b + g
                            q = dve.tensor_scalar(d, d, soft[:, 7, a:a + 1], None, ALU.mult)
                    q.then_inc(p_done, 1)

                def out_lo(i):
                    item = first_item + i
                    dve.wait_ge(oT_hi_ok, item + 1)
                    dve.tensor_tensor(yT_lo[:, out_kt + i, :], ps[:, 6 + i % 2, 0:SEQ], yT_hi[:, out_kt + i, :].bitcast(F32),
                                      ALU.subtract).then_inc(oT_ok, 1)

                out_kt = 4 if sink is not None else 0
                pT = pT_ab if sink is not None else pT_fox
                scaled(0)
                for i in range(items):
                    if i + 1 < items:
                        scaled(i + 1)
                    idle(3 * i)
                    normed(i)
                    idle(3 * i + 1)
                    if i:
                        out_lo(i - 1)
                    dve.wait_ge(pT_psd, first_item + i + 1)
                    dve.tensor_copy(pT[:, i % 2, 1, :], ps[:, 5, 0:384]).then_inc(pT_okV, 1)
                    idle(3 * i + 2)
                out_lo(items - 1)

            if last_sub >= FFN0:
                open_sub(FFN0)
                ffn(FFN0)
            if last_sub >= FFN1:
                close(FFN0)
                for t in range(TOKT):
                    r = reciprocal_root(FINAL_EVENT, t)
                    dve.scalar_tensor_tensor(x[:, t, :], x[:, t, :], r, rows[:, 1, :], ALU.mult, ALU.mult).then_inc(x_new, 1)
                open_sub(FFN1)
                ffn(FFN1)
            if last_sub >= AB:
                close(FFN1)
                open_sub(AB)
                n = BASE[AB]
                done = [0]

                def taps(count):
                    for tp in range(done[0], min(done[0] + count, CONV_K)):
                        for c in range(CCT):
                            wt = cw31[:, tp * CCT + c:tp * CCT + c + 1]
                            src = a_pad[:, c, tp:tp + SEQ]
                            if tp == 0:
                                o = dve.tensor_scalar(acc31[:, c, :], src, wt, par[:, C_CB + c:C_CB + c + 1], ALU.mult, ALU.add)
                            else:
                                dve.wait_ge(tap, 24 + CCT * (tp - 1) + c + 1)
                                o = dve.scalar_tensor_tensor(acc31[:, c, :], src, wt, acc31[:, c, :], ALU.mult, ALU.add)
                            o.then_inc(tap, 1)
                    done[0] = min(done[0] + count, CONV_K)

                for k in range(2, 10):
                    if k == 7:
                        dve.wait_ge(evac_a, 3)
                        dve.wait_ge(pads, 2)
                        dve.tensor_tensor(a_pad[:, :, CONV_K - 1:], ps[:, 0:2, :].rearrange("p b (a c) -> p (b a) c", a=2), sig,
                                          ALU.mult).then_inc(evac_v, 1)
                    split(n + k)
                    if k >= 7:
                        dve.wait_ge(evac_v, 5)
                        taps(3)
                dve.wait_ge(bias_built, 1)
                dve.wait_ge(misc_landed, 48)
                sink_v = sinks[:, :].rearrange("p (c g) -> p c g", g=2)
                attention(4, 0, p_ab,
                          lambda i: alibi[:, 2 * i:2 * i + 2, :],
                          lambda i: sink_v[:, i:i + 1, :].to_broadcast([P, 2, 2]), lambda j: taps(1))
                taps(CONV_K)
                dve.wait_ge(tap, 24 + CCT * CONV_K)
                dve.tensor_copy(warm[:, 23:24], acc31[:, 0, 0:1]).then_inc(conv_done, 1)
                for t in range(TOKT):
                    dve.wait_ge(ln_ps, t + 1)
                    link(dve.bn_stats(soft[:, 0, 50 + 6 * t:56 + 6 * t], ps[:, t, :]))
                    dve.bn_aggr(zf[:, 7, 8 * t:8 * t + 2], soft[:, 0, 50 + 6 * t:56 + 6 * t]).then_inc(ln_stat, 1)
                for t in range(TOKT):
                    dve.wait_ge(ln_std, t + 1)
                    link(dve.reciprocal(zf[:, 7, 8 * t + 3:8 * t + 4], zf[:, 7, 8 * t + 2:8 * t + 3]))
                    dve.tensor_scalar(ln_y[:, t, :], ps[:, t, :], zf[:, 7, 8 * t:8 * t + 1], zf[:, 7, 8 * t + 3:8 * t + 4],
                                      ALU.subtract, ALU.mult).then_inc(ln_out, 1)
                dve.wait_ge(yT_hi_ok, 3)
                dve.tensor_tensor(yT_lo[:, 0:4, :], ab_y, yT_hi[:, 0:4, :].bitcast(F32), ALU.subtract).then_inc(yT_ok, 1)
                for k in range(10, 13):
                    split(n + k)
            if last_sub >= FFN2:
                close(AB)
                open_sub(FFN2)
                ffn(FFN2)
            if last_sub >= FFN3:
                close(FFN2)
                open_sub(FFN3)
                dve.tensor_copy(zf_hi[:, :, :], zf_raw[:, :, :]).then_inc(zf_ok, 1)
                dve.wait_ge(zf_ok, 1)
                dve.tensor_tensor(zf_lo[:, :, :], zf_raw[:, :, :], zf_hi[:, :, :].bitcast(F32), ALU.subtract).then_inc(zf_ok, 1)
                ffn(FFN3)
            if last_sub >= FOX:
                close(FFN3)
                open_sub(FOX)
                n = BASE[FOX]
                split(n + 2)
                dve.wait_ge(zf_p, 1)
                for t in range(TOKT):
                    o = dve.tensor_tensor(zf[:, 0, t * 16:(t + 1) * 16], ps[:, 6, t * 16:(t + 1) * 16], b_f[:, :], ALU.add)
                link(o)
                dve.scalar_tensor_tensor(zf[:, 1, :], zf[:, 0, :], -1.0, zf[:, 0, :], ALU.mult, ALU.max).then_inc(zf_z, 1)
                link(dve.tensor_scalar(zf[:, 4, :], zf[:, 0, :], 0.0, None, ALU.min))
                dve.wait_ge(zf_e, 2)
                dve.tensor_tensor(zf[:, 5, :], zf[:, 4, :], zf[:, 3, :], ALU.subtract).then_inc(zf_v, 1)
                for k in range(3, 15):
                    split(n + k)

                def fox_bias(i):
                    dve.wait_ge(d_ok, i + 1)
                    return decay[:, 2 * i:2 * i + 2, :]

                attention(8, 4, p_fox, fox_bias, None, lambda j: None)
                for k in range(15, 18):
                    split(n + k)
            if last_sub >= FFN4:
                close(FOX)
                open_sub(FFN4)
                ffn(FFN4)
            if last_sub > CONV:
                close(last_sub)

        @block.gpsimd
        def _(pool):
            step = [0]

            def link(ins):
                step[0] += 1
                ins.then_inc(pool_chain, 1)
                pool.wait_ge(pool_chain, step[0])

            pool.memset(ada_sum0, 0.0).then_inc(ada0_cleared, 1)
            pool.memset(eps[:, :], EPS)
            pool.memset(ones[:, :], 1.0)
            link(pool.memset(ident[:, :], 0.0))
            link(pool.affine_select(out=ident[:, :], in_=ident[:, :], compare_op=ALU.not_equal, fill=1.0, base=0,
                                    pattern=[[-1, P]], channel_multiplier=1))
            pool.affine_select(out=upper[:, :], in_=ones[:, :], compare_op=ALU.is_ge, fill=0.0, base=0,
                               pattern=[[1, P]], channel_multiplier=-1).then_inc(consts, 1)
            pool.memset(u_pad[:, :, :, 0:1], 0.0)
            pool.memset(u_pad[:, :, :, GRID_W + 1:GRID_W + 2], 0.0).then_inc(pads, 1)

            rest = len(ADA_SECTIONS) * 4

            def load_ada(r):
                section, k = ADA_SECTIONS[r // 4], 2 * (r % 4)
                pool.dma_start(ada_raw[:, r % ADA_REST_SLOTS, :, :], ada_w[:, k:k + 2, section * D:(section + 1) * D])\
                    .then_inc(ada_landed[r % ADA_REST_SLOTS], 16)

            pool.wait_ge(raw_done, ADA_FIRST - 3)
            for r in range(ADA_REST_SLOTS):
                load_ada(r)
            for i, section in enumerate(ADA_SECTIONS):
                acc = ada_acc if i % 2 else tmp[:, 1, :]
                if i != 1:
                    pool.wait_ge(ada_ps, 2 if i == 0 else i + 1)
                link(pool.memset(acc, 0.0))
                pool.dma_start(acc[0:1, :], w["ada_b"][:, section * D:(section + 1) * D]).then_inc(ada_b_landed, 16)
                pool.wait_ge(ada_b_landed, 16 * (i + 1))
                for u in range(4):
                    r = 4 * i + u
                    pool.wait_ge(ada_scaled, r + 1)
                    if r:
                        pool.wait_ge(ada_added, r)
                    link(pool.tensor_tensor(acc, ada_raw[:, r % ADA_REST_SLOTS, 0, :], acc, ALU.add))
                    pool.tensor_tensor(acc, ada_raw[:, r % ADA_REST_SLOTS, 1, :], acc, ALU.add).then_inc(ada_added, 1)
                    pool.wait_ge(ada_added, r + 1)
                    if r + ADA_REST_SLOTS < rest:
                        load_ada(r + ADA_REST_SLOTS)
                if i == 1:
                    pool.wait_ge(xn_done, 2)
                    pool.dma_start(rows[:, 0, :], w["norm2_g"].to_broadcast([P, D])).then_inc(g2_row_landed, 16)
            if last_sub >= AB:
                pool.wait_ge(ada_ps, 6)
                pool.wait_ge(x_new, 1)
                pool.memset(a_pad[:, :, 0:CONV_K - 1], 0.0).then_inc(pads, 1)
                dist_i = pT_ab[:, 0, 0, :].bitcast(mybir.dt.int32)
                dist = pT_ab[:, 0, 1, :]
                pool.iota(dist_i[:, 0:P], pattern=[[-1, P]], base=0, channel_multiplier=1)
                link(pool.iota(dist_i[:, P:3 * P], pattern=[[-1, 2 * P]], base=P, channel_multiplier=1))
                link(pool.tensor_copy(dist, dist_i))
                for h in range(SWA_HQ):
                    slope = 2.0 ** (-8.0 * (h + 1) / SWA_HQ)
                    b0, b1 = alibi[:, h, 0:P], alibi[:, h, P:3 * P]
                    link(pool.tensor_scalar(alibi[:, h, :], dist, -slope, None, ALU.mult))
                    link(pool.affine_select(out=b1, in_=b1, compare_op=ALU.is_ge, fill=NEG, base=P,
                                            pattern=[[-1, 2 * P]], channel_multiplier=1))
                    pool.affine_select(out=b0, in_=b0, compare_op=ALU.is_ge, fill=NEG, base=0,
                                       pattern=[[-1, P]], channel_multiplier=1)
                    a = pool.affine_select(out=b1, in_=b1, compare_op=ALU.is_ge, fill=NEG, base=-1,
                                           pattern=[[1, 2 * P]], channel_multiplier=-1)
                a.then_inc(bias_built, 1)
            if last_sub >= FOX:
                for i in range(FOX_H // 2):
                    pool.wait_ge(d_raw, i + 1)
                    for h in (2 * i, 2 * i + 1):
                        d = decay[:, h, :].rearrange("p (k s) -> p k s", k=3)[:, 0::2, :]
                        a = pool.affine_select(out=d, in_=d, compare_op=ALU.is_ge, fill=NEG, base=0,
                                               pattern=[[0, 2], [-1, P]], channel_multiplier=1)
                    a.then_inc(d_ok, 1)


_INS = ["x", "c", "ada_w", "ada_b", "norm1_g", "norm2_g", "conv_w_in", "conv_w", "conv_w_out", "ffn_w_in", "ffn_w_out",
        "final_g", "norm_g_2", "ffn_w_gate_2", "ffn_w_up_2", "ffn_w_down_2", "ab_w_in_2", "conv_w_2", "conv_b_2",
        "conv_ln_g_2", "conv_ln_b_2", "swa_sinks_2", "ab_w_out_2", "fox_w_in_2", "fox_b_f_2", "fox_w_out_2"]


def kernel(**inputs):
    import numpy as np
    from concourse import bacc
    from concourse.bass_utils import run_bass_kernel_spmd

    nc = bacc.Bacc("TRN2", target_bir_lowering=False, num_devices=1)
    arrays, args = {}, {}
    for name in _INS:
        a = np.ascontiguousarray(inputs[name])
        arrays[f"in_{name}"] = a
        args[name] = nc.dram_tensor(f"in_{name}", a.shape, mybir.dt.from_np(a.dtype), kind="ExternalInput").ap()
    out = nc.dram_tensor("out", (1, SEQ, D), F32, kind="ExternalOutput").ap()
    block_program(nc, out, **args)
    r = run_bass_kernel_spmd(nc, [arrays], core_ids=[0])
    return r.results[0]["out"]
```

```python
from contextlib import ExitStack

import concourse.bass as bass
from concourse import mybir

ALU = mybir.AluOpType
ACT = mybir.ActivationFunctionType
F32 = mybir.dt.float32
F32R = mybir.dt.float32r
AX_X = mybir.AxisListType.X

P = 128
SEQ = 256
TOKT = SEQ // P
D = 1024
KT = D // P
EPS = 1e-6
NEG = -1e30
SLOT = 2048
NSLOT = 3

FF = 2816
FCH = 256
NCH = FF // FCH
FFN_UNITS = 3 * NCH

ADA_FIRST = 8
ADA_REST_SLOTS = 3
ADA_SECTIONS = (2, 3, 4, 5)

CONV_CH = 512
CONV_K = 31
CCT = CONV_CH // P
DH = 64
SWA_HQ = 8
SWA_HKV = 2
SWA_G = SWA_HQ // SWA_HKV
FOX_H = 16
GRID_W = 64
AB_IN = 1792

CONV, FFN0, FFN1, AB, FFN2, FFN3, FOX, FFN4 = range(8)
UNITS = {CONV: 16, AB: 11, FOX: 16}
BASE = {}
_n = ADA_FIRST
for _s in range(8):
    BASE[_s] = _n
    _n += UNITS.get(_s, FFN_UNITS)
TOTAL = _n

C_COND, C_CONVW, C_CB, C_LNG, C_LNB, C_PRE = 0, 8, 32, 36, 40, 44
N_PAR = C_PRE + 4 * 8
N_CW31 = CONV_K * CCT


NORMED = (CONV, FFN0, AB, FOX)
FOLDED = (FFN1, FFN2, FFN3, FFN4)


def x_count(b, t, h):
    return 4 * b + 2 * t + h + 1


def xn_count(s, t):
    return 2 * NORMED.index(s) + t + 1


def x_event(s):
    return s if s < 2 else s + 1


FINAL_EVENT = 2
STAT_Y = 18


def rows_count(b):
    return 16 * sum(1 + (i + 1 in NORMED) for i in range(FFN0, b + 1))


def gain_column(n):
    for i, s in enumerate(FOLDED):
        o = n - BASE[s]
        if 0 <= o < FFN_UNITS - 1 and (o < 2 or o % 3 != 1):
            second = o == 1 or (o > 1 and o % 3 == 0)
            return C_PRE + 8 * i + (4 if second else 0)
    return None


def block_program(nc, out, last_sub=FFN4, **w):
    x_d = w["x"].rearrange("b (t p) d -> p (b t) d", p=P)
    out_d = out.rearrange("b (t p) d -> p (b t) d", p=P)
    ada_w = w["ada_w"].rearrange("l (kt p) n -> p (l kt) n", p=P)
    conv_in = w["conv_w_in"].rearrange("l (kt p) n -> p (l kt) n", p=P)
    conv_out = w["conv_w_out"].rearrange("l (kt p) n -> p (l kt) n", p=P)
    ab_in = w["ab_w_in_2"].rearrange("l (kt p) n -> p (l kt) n", p=P)
    ab_out = w["ab_w_out_2"].rearrange("l (kt p) n -> p (l kt) n", p=P)
    fox_in = w["fox_w_in_2"].rearrange("l (kt p) n -> p (l kt) n", p=P)
    fox_out = w["fox_w_out_2"].rearrange("l (kt p) n -> p (l kt) n", p=P)

    def ffn_weights(s):
        if s == FFN0:
            both = w["ffn_w_in"].rearrange("l (kt p) n -> p (l kt) n", p=P)
            return both[:, :, 0:FF], both[:, :, FF:2 * FF], \
                w["ffn_w_out"].rearrange("l (kt p) n -> p (l kt) n", p=P)
        layer, half = {FFN1: (0, 0), FFN2: (0, 1), FFN3: (1, 0), FFN4: (1, 1)}[s]
        return (w["ffn_w_gate_2"][layer, half].rearrange("(kt p) n -> p kt n", p=P),
                w["ffn_w_up_2"][layer, half].rearrange("(kt p) n -> p kt n", p=P),
                w["ffn_w_down_2"][layer, half].rearrange("(kt p) n -> p kt n", p=P))

    def norm_row(layer, i):
        return w["norm_g_2"][layer, i:i + 1, :].to_broadcast([P, D])

    PRE_ROW = {FFN1: (0, 0), AB: (0, 2), FFN2: (0, 4), FFN3: (1, 0), FOX: (1, 2), FFN4: (1, 4)}
    POST_ROW = {FFN1: (0, 1), AB: (0, 3), FFN2: (0, 5), FFN3: (1, 1), FOX: (1, 3), FFN4: (1, 5)}

    with ExitStack() as ctx:
        def sb(name, shape, dt=F32):
            return ctx.enter_context(nc.sbuf_tensor(name, shape, dt))

        def sem(name):
            return ctx.enter_context(nc.semaphore(name))

        ps = ctx.enter_context(nc.psum_tensor("ps", [P, 8, 512], F32))
        raw = sb("raw", [P, NSLOT, SLOT])
        w_hi = sb("w_hi", [P, NSLOT, SLOT], F32R)
        w_lo = sb("w_lo", [P, NSLOT, SLOT], F32R)
        x = sb("x_sb", [P, TOKT, D])
        tmp = sb("tmp", [P, TOKT, D])
        xn = sb("xn", [P, TOKT, D])
        xT_hi = sb("xT_hi", [P, KT, SEQ], F32R)
        xT_lo = sb("xT_lo", [P, KT, SEQ], F32R)
        yT_hi = sb("yT_hi", [P, KT, SEQ], F32R)
        yT_lo = sb("yT_lo", [P, KT, SEQ], F32R)
        sil = sb("sil", [P, TOKT, FCH])
        hid = sb("hid", [P, TOKT, FCH])
        hT_hi = sb("hT_hi", [P, 2, SEQ], F32R)
        hT_lo = sb("hT_lo", [P, 2, SEQ], F32R)
        rows = sb("rows", [P, 4, D])
        ident = sb("ident", [P, P])
        ones = sb("ones", [P, P])
        upper = sb("upper", [P, P])
        par_rows = sb("par_rows", [P, 2, P])
        par = sb("par", [P, N_PAR])
        cw31 = sb("cw31", [P, N_CW31])
        cond = sb("cond", [P, KT])
        eps = sb("eps", [P, 1])
        warm = sb("warm", [P, 24])
        stat = sb("stat", [P, 3, 32])
        sinks = sb("sinks", [P, SWA_HQ])
        b_f = sb("b_f", [P, FOX_H])
        soft = sb("soft", [P, 8, 64])
        zf = sb("zf", [P, 8, 2 * FOX_H])
        zf_hi = sb("zf_hi", [P, KT, FOX_H], F32R)
        zf_lo = sb("zf_lo", [P, KT, FOX_H], F32R)
        zf_raw = sb("zf_raw", [P, KT, FOX_H])
        cT = sb("cT", [FOX_H, SEQ])
        arena = sb("arena", [P, 11776])

        def part(at, *shape):
            n = 1
            for k in shape:
                n *= k
            assert at + n <= 11776
            ap = arena[:, at:at + n]
            if len(shape) == 1:
                return ap
            names = "abcd"[:len(shape)]
            return ap.rearrange(f"p ({' '.join(names)}) -> p {' '.join(names)}",
                                **dict(zip(names[1:], shape[1:])))

        ada_raw = part(0, ADA_REST_SLOTS, 2, D)
        ada_acc = part(6144, D)
        gate_c = part(7168, CCT, SEQ)
        u_pad = part(8192, CCT, SEQ // GRID_W, GRID_W + 2)
        conv_acc = part(9248, CCT, SEQ)
        conv_y = part(10272, CCT, SEQ)
        alibi = part(0, SWA_HQ, 384)
        a_pad = part(3072, CCT, SEQ + CONV_K - 1)
        sig = part(4216, CCT, SEQ)
        acc31 = part(5240, CCT, SEQ)
        q_ab = part(6264, CCT, SEQ)
        k_ab = part(7288, SWA_HKV, SEQ)
        v_ab = part(7800, TOKT, P)
        p_ab = part(8056, 2, 2, 384)
        pT_ab = part(9592, 2, 2, 384)
        ln_y = part(8056, TOKT, CONV_CH)
        ab_y = part(9592, CCT, SEQ)
        q_fox = part(0, KT, SEQ)
        k_fox = part(2048, KT, SEQ)
        decay = part(4096, FOX_H, 384)
        pT_fox = part(10240, 2, 2, 384)
        v_fox = tmp
        p_fox = xn[:, :, :].rearrange("p t d -> p (t d)")[:, 0:1536].rearrange(
            "p (b h s) -> p b h s", b=2, h=2)
        q_of = {AB: q_ab, FOX: q_fox}
        p_of = {AB: p_ab, FOX: p_fox}
        pT_of = {AB: pT_ab, FOX: pT_fox}
        ada_sum0 = tmp[:, :, :].rearrange("p t d -> p (t d)")

        landed = [sem(f"landed{i}") for i in range(NSLOT)]
        hi_ready = sem("hi_ready")
        raw_done = sem("raw_done")
        w_used = sem("w_used")
        x_landed = sem("x_landed")
        par_landed = sem("par_landed")
        bias_landed = sem("bias_landed")
        row_g1_landed = sem("row_g1_landed")
        misc_landed = sem("misc_landed")
        consts = sem("consts")
        par_ps = sem("par_ps")
        par_ready = sem("par_ready")
        cond_ready = sem("cond_ready")
        ada_landed = [sem(f"ada_landed{i}") for i in range(ADA_REST_SLOTS)]
        ada_b_landed = sem("ada_b_landed")
        ada_scaled = sem("ada_scaled")
        ada_added = sem("ada_added")
        ada_cleared = sem("ada_cleared")
        ada_ps = sem("ada_ps")
        ada_row_a = sem("ada_row_a")
        ada_row_v = sem("ada_row_v")
        ada0_cleared = sem("ada0_cleared")
        g2_row_landed = sem("g2_row_landed")
        y_tok0 = sem("y_tok0")
        y_sq = sem("y_sq")
        y_std = sem("y_std")
        y_rstd = sem("y_rstd")
        x_sq = sem("x_sq")
        x_std = sem("x_std")
        x_rstd = sem("x_rstd")
        x_mid = sem("x_mid")
        t_done = sem("t_done")
        x_new = sem("x_new")
        xn_part = sem("xn_part")
        xn_done = sem("xn_done")
        xT_ps = sem("xT_ps")
        xT_hi_ok = sem("xT_hi_ok")
        xT_ok = sem("xT_ok")
        rows_landed = sem("rows_landed")
        out_landed = sem("out_landed")
        up_tok0 = sem("up_tok0")
        sil_done = sem("sil_done")
        hid_done = sem("hid_done")
        hT_ps = sem("hT_ps")
        hT_hi_ok = sem("hT_hi_ok")
        hT_ok = sem("hT_ok")
        evac_a = sem("evac_a")
        evac_v = sem("evac_v")
        pads = sem("pads")
        tap = sem("tap")
        conv_done = sem("conv_done")
        yT_hi_ok = sem("yT_hi_ok")
        yT_ok = sem("yT_ok")
        bias_built = sem("bias_built")
        k_landed = sem("k_landed")
        ln_ps = sem("ln_ps")
        ln_stat = sem("ln_stat")
        ln_std = sem("ln_std")
        ln_out = sem("ln_out")
        lnT_ps = sem("lnT_ps")
        ab_y_ok = sem("ab_y_ok")
        s_ps = sem("s_ps")
        s_sb = sem("s_sb")
        m_chain = sem("m_chain")
        m_ok = sem("m_ok")
        e_done = sem("e_done")
        p_done = sem("p_done")
        pT_psd = sem("pT_psd")
        pT_okA = sem("pT_okA")
        pT_okV = sem("pT_okV")
        o_ps = sem("o_ps")
        oT_hi_ok = sem("oT_hi_ok")
        oT_ok = sem("oT_ok")
        zf_ok = sem("zf_ok")
        zf_v = sem("zf_v")
        zf_a = sem("zf_a")
        zf_p = sem("zf_p")
        zf_z = sem("zf_z")
        zf_e = sem("zf_e")
        pool_chain = sem("pool_chain")
        d_ps = sem("d_ps")
        d_raw_a = sem("d_raw_a")
        d_raw_v = sem("d_raw_v")
        d_ok = sem("d_ok")

        def slot_of(n):
            return n % NSLOT

        def weight_count(n):
            return n - ADA_FIRST + 1

        def y_unit(b):
            return BASE[b] + UNITS.get(b, FFN_UNITS) - 1

        first_item = {AB: 0, FOX: 4}
        out_kt = {AB: 4, FOX: 0}

        def item_bank(i):
            return 2 * ((i + 1) % 2)

        def ffn_index(s):
            return (FFN0, FFN1, FFN2, FFN3, FFN4).index(s)

        block = ctx.enter_context(nc.Block())

        @block.sync
        def _(sp):
            def load(n, j, dst_src):
                if not (isinstance(j, int) and n + NSLOT * j < NSLOT):
                    sp.wait_ge(raw_done, n - NSLOT + 1 + NSLOT * j)
                assert len(dst_src) == 2
                for dst, src in dst_src:
                    sp.dma_start(dst, src).then_inc(landed[slot_of(n)], 16)

            def columns(n, wd, k0, c0, width, kts=4):
                dst = raw[:, slot_of(n), 0:kts * width].rearrange("p (k c) -> p k c", k=kts)
                h = kts // 2
                return [(dst[:, i:i + h, :], wd[:, k0 + i:k0 + i + h, c0:c0 + width]) for i in (0, h)]

            def pair_rows(n, wd, k):
                dst = raw[:, slot_of(n), :].rearrange("p (k c) -> p k c", k=2)
                return [(dst[:, i:i + 1, :], wd[:, bass.ds(k + i, 1), :]) for i in range(2)]

            def up_unit(n, gate, up, k0, c0):
                dst = raw[:, slot_of(n), :].rearrange("p (k h c) -> p k h c", k=4, h=2)
                return [(dst[:, :, i, :], wd[:, k0:k0 + 4, bass.ds(c0, FCH)]) for i, wd in enumerate((gate, up))]

            def load_rows(s):
                if s in NORMED:
                    sp.wait_ge(xn_done, xn_count(s, 1))
                sp.wait_ge(x_new, x_count(s - 1, 1, 1))
                post = w["final_g"].rearrange("(a d) -> a d", a=1).to_broadcast([P, D]) if s == FFN0 \
                    else norm_row(*POST_ROW[s])
                sp.dma_start(rows[:, 1, :], post).then_inc(rows_landed, 16)
                if s + 1 in NORMED:
                    sp.dma_start(rows[:, 0, :], norm_row(*PRE_ROW[s + 1])).then_inc(rows_landed, 16)

            def load_ffn(s):
                gate, up, down = ffn_weights(s)
                n = BASE[s]
                load(n, 0, up_unit(n, gate, up, 0, 0))
                load(n + 1, 0, up_unit(n + 1, gate, up, 4, 0))
                with sp.Fori(1, NCH) as j:
                    load(n - 1, j, up_unit(n - 1, gate, up, 0, j * FCH))
                    load(n, j, up_unit(n, gate, up, 4, j * FCH))
                    load(n + 1, j, pair_rows(n + 1, down, j * 2 - 2))
                load_rows(s)
                load(n + FFN_UNITS - 1, 0, pair_rows(n + FFN_UNITS - 1, down, 2 * NCH - 2))

            sp.dma_start(par_rows[C_COND:C_COND + 8, 0, :], w["c"].rearrange("b (r q) -> (b r) q", q=P)).then_inc(par_landed, 16)
            sp.dma_start(par_rows[C_CONVW:C_CONVW + 24, 0, :], w["conv_w"].rearrange("l k (r q) -> (l k r) q", q=P)).then_inc(par_landed, 16)
            sp.dma_start(par_rows[C_CB:C_CB + 4, 0, :], w["conv_b_2"].rearrange("l (r q) -> (l r) q", q=P)).then_inc(par_landed, 16)
            sp.dma_start(par_rows[C_LNG:C_LNG + 4, 0, :], w["conv_ln_g_2"].rearrange("l (r q) -> (l r) q", q=P)).then_inc(par_landed, 16)
            sp.dma_start(par_rows[C_LNB:C_LNB + 4, 0, :], w["conv_ln_b_2"].rearrange("l (r q) -> (l r) q", q=P)).then_inc(par_landed, 16)
            for i, s in enumerate(FOLDED):
                layer, row = PRE_ROW[s]
                sp.dma_start(par_rows[C_PRE + 8 * i:C_PRE + 8 * i + 8, 0, :],
                             w["norm_g_2"][layer, row, :].rearrange("(r q) -> r q", q=P)).then_inc(par_landed, 16)
            sp.dma_start(par_rows[0:N_CW31, 1, :], w["conv_w_2"].rearrange("l k (r q) -> (l k r) q", q=P)).then_inc(par_landed, 16)
            sp.wait_ge(ada0_cleared, 1)
            sp.dma_start(ada_sum0[0:1, :], w["ada_b"][:, 0:2 * D]).then_inc(bias_landed, 16)
            for n in range(ADA_FIRST):
                load(n, 0, [(raw[:, slot_of(n), h * D:(h + 1) * D], ada_w[:, n, h * D:(h + 1) * D]) for h in range(2)])
                if n == 0:
                    sp.dma_start(x[:, :, :], x_d).then_inc(x_landed, 16)
                    sp.dma_start(rows[:, 0, :], w["norm1_g"].to_broadcast([P, D])).then_inc(row_g1_landed, 16)
            n = BASE[CONV]
            for half in range(2):
                for section in (1, 2, 0):
                    for k0 in (0, 4):
                        load(n, 0, columns(n, conv_in, k0, section * D + half * 512, 512))
                        n += 1
            for k in range(0, KT, 2):
                load(n, 0, pair_rows(n, conv_out, k))
                n += 1
            sp.dma_start(sinks[:, :], w["swa_sinks_2"].to_broadcast([P, SWA_HQ])).then_inc(misc_landed, 16)
            sp.dma_start(b_f[:, :], w["fox_b_f_2"].to_broadcast([P, FOX_H])).then_inc(misc_landed, 16)
            sp.dma_start(zf_raw[:, :, :], fox_in[:, :, 3 * D:3 * D + FOX_H]).then_inc(misc_landed, 16)
            if last_sub >= FFN0:
                load_ffn(FFN0)
            if last_sub >= FFN1:
                load_ffn(FFN1)
            if last_sub >= AB:
                n = BASE[AB]
                for c0 in (0, CONV_CH):
                    for k0 in (0, 4):
                        load(n, 0, columns(n, ab_in, k0, c0, 512))
                        n += 1
                for k0 in (0, 4):
                    load(n, 0, columns(n, ab_in, k0, 2 * CONV_CH, 512))
                    n += 1
                load(n, 0, columns(n, ab_in, 0, 1536, 256, kts=8))
                n += 1
                load_rows(AB)
                for k in (4, 6, 0, 2):
                    load(n, 0, pair_rows(n, ab_out, k))
                    n += 1
            if last_sub >= FFN2:
                load_ffn(FFN2)
            if last_sub >= FFN3:
                load_ffn(FFN3)
            if last_sub >= FOX:
                n = BASE[FOX]
                for c0 in (2 * D, 2 * D + 512):
                    for k0 in (0, 4):
                        load(n, 0, columns(n, fox_in, k0, c0, 512))
                        n += 1
                for c0 in range(0, D, 256):
                    for section in (0, 1):
                        load(n, 0, columns(n, fox_in, 0, section * D + c0, 256, kts=8))
                        n += 1
                load_rows(FOX)
                for k in range(0, KT, 2):
                    load(n, 0, pair_rows(n, fox_out, k))
                    n += 1
            if last_sub >= FFN4:
                load_ffn(FFN4)
            for t in range(TOKT):
                for h in range(2):
                    sp.wait_ge(x_new, x_count(last_sub, t, h))
                    c = slice(h * 512, (h + 1) * 512)
                    sp.dma_start(out_d[:, t, c], x[:, t, c]).then_inc(out_landed, 16)
            sp.wait_ge(out_landed, 16 * 2 * TOKT)

        @block.tensor
        def _(pe):
            def product(o, a_hi, a_lo, b_hi, b_lo, first, last):
                pe.matmul(o, a_hi, b_lo, start=first, stop=False, skip_group_check=True)
                pe.matmul(o, a_hi, b_hi, start=False, stop=False, skip_group_check=True)
                return pe.matmul(o, a_lo, b_hi, start=False, stop=last, skip_group_check=True)

            def unit(n, j=0):
                pe.wait_ge(raw_done, n + 1 + NSLOT * j)
                return w_hi[:, slot_of(n), :], w_lo[:, slot_of(n), :]

            def tok(t):
                return slice(t * P, (t + 1) * P)

            def turn_x(s, t):
                if s in NORMED:
                    pe.wait_ge(xn_done, xn_count(s, t))
                for h in range(2):
                    if s in FOLDED:
                        pe.wait_ge(x_new, x_count(s - 1, t, h))
                    for k in range(4):
                        tr = pe.transpose(ps[:, 2 * t + h, tok(k)], (xn if s in NORMED else x)[:, t, tok(4 * h + k)], ident[:, :])
                    tr.then_inc(xT_ps, 1)

            def up_part(n, k0, t, j=0):
                hi, lo = unit(n, j)
                for k in range(4):
                    c = slice(k * 512, (k + 1) * 512)
                    mm = product(ps[:, t, :], xT_hi[:, k0 + k, tok(t)], xT_lo[:, k0 + k, tok(t)], hi[:, c], lo[:, c],
                                 k0 + k == 0, k0 + k == KT - 1)
                return mm

            def turn_hid(s, j):
                for f in range(2):
                    for t in range(TOKT):
                        tr = pe.transpose(ps[:, 2, f * SEQ + t * P:f * SEQ + (t + 1) * P], hid[:, t, tok(f)], ident[:, :])
                tr.then_inc(hT_ps, 1)

            def down_part(n, aT_hi, aT_lo, k0, t, first, last, j=0, ks=(0, 1)):
                hi, lo = unit(n, j)
                for k in ks:
                    for h in range(2):
                        c = slice(k * D + h * 512, k * D + (h + 1) * 512)
                        mm = product(ps[:, 4 + 2 * t + h, :], aT_hi[:, k0 + k, tok(t)], aT_lo[:, k0 + k, tok(t)],
                                     hi[:, c], lo[:, c], first and k == 0, last and k == 1)
                return mm

            def ffn(s):
                f, n = ffn_index(s), BASE[s]
                turn_x(s, 0)
                pe.wait_ge(xT_ok, 4 * s + 1)
                up_part(n, 0, 0)
                turn_x(s, 1)
                pe.wait_ge(xT_ok, 4 * s + 2)
                up_part(n + 1, 4, 0).then_inc(up_tok0, 1)
                pe.wait_ge(xT_ok, 4 * s + 3)
                up_part(n, 0, 1).then_inc(w_used, 1)
                pe.wait_ge(xT_ok, 4 * s + 4)
                up_part(n + 1, 4, 1).then_inc(w_used, 1)

                def chunk(n_a, j_hid, j, first):
                    pe.wait_ge(hid_done, 2 * (NCH * f + j_hid + 1))
                    up_part(n_a, 0, 0, j)
                    up_part(n_a, 0, 1, j).then_inc(w_used, 1)
                    turn_hid(s, j_hid)
                    up_part(n_a + 1, 4, 0, j).then_inc(up_tok0, 1)
                    up_part(n_a + 1, 4, 1, j).then_inc(w_used, 1)
                    pe.wait_ge(hT_ok, NCH * f + j_hid + 1)
                    down_part(n_a + 2, hT_hi, hT_lo, 0, 0, first, False, j)
                    down_part(n_a + 2, hT_hi, hT_lo, 0, 1, first, False, j).then_inc(w_used, 1)

                chunk(n + 2, 0, 0, True)
                with pe.Fori(1, NCH - 2) as i:
                    chunk(n + 2, i, i, False)
                last = n + FFN_UNITS - 1
                pe.wait_ge(hid_done, 2 * (NCH * f + NCH - 1))
                up_part(last - 3, 0, 0)
                up_part(last - 3, 0, 1).then_inc(w_used, 1)
                turn_hid(s, NCH - 2)
                up_part(last - 2, 4, 0).then_inc(up_tok0, 1)
                up_part(last - 2, 4, 1).then_inc(w_used, 1)
                pe.wait_ge(hT_ok, NCH * (f + 1) - 1)
                down_part(last - 1, hT_hi, hT_lo, 0, 0, False, False, ks=(0,))
                pe.wait_ge(hid_done, 2 * NCH * (f + 1))
                turn_hid(s, NCH - 1)
                down_part(last - 1, hT_hi, hT_lo, 0, 0, False, False, ks=(1,))
                down_part(last - 1, hT_hi, hT_lo, 0, 1, False, False).then_inc(w_used, 1)
                pe.wait_ge(hT_ok, NCH * (f + 1))
                down_part(last, yT_hi, yT_lo, 0, 0, False, True).then_inc(y_tok0, 1)
                down_part(last, yT_hi, yT_lo, 0, 1, False, True).then_inc(w_used, 1)

            def channel_chunk(n, bank):
                for u in range(2):
                    hi, lo = unit(n + u)
                    for k in range(4):
                        for c in range(4):
                            w_k = [v[:, k * 512 + c * P:k * 512 + (c + 1) * P] for v in (hi, lo)]
                            mm = product(ps[:, bank + c // 2, (c % 2) * SEQ:(c % 2 + 1) * SEQ], *w_k,
                                         xT_hi[:, 4 * u + k, :], xT_lo[:, 4 * u + k, :],
                                         u == 0 and k == 0 and c % 2 == 0, u == 1 and k == 3)
                    mm.then_inc(w_used, 1)

            def token_chunk(n, bank):
                for u in range(2):
                    hi, lo = unit(n + u)
                    for t in range(TOKT):
                        for k in range(4):
                            c = slice(k * 512, (k + 1) * 512)
                            mm = product(ps[:, bank + t, :], xT_hi[:, 4 * u + k, tok(t)], xT_lo[:, 4 * u + k, tok(t)],
                                         hi[:, c], lo[:, c], u == 0 and k == 0, u == 1 and k == 3)
                    mm.then_inc(w_used, 1)

            def row_everywhere(banks, acc):
                for h in range(2):
                    mm = pe.matmul(ps[:, banks + h, :], ones[:, :], acc[:, h * 512:(h + 1) * 512], start=True, stop=True)
                mm.then_inc(ada_ps, 1)

            def key(s, i):
                return k_ab[:, i // 2, :] if s == AB else k_fox[:, i, :]

            def value(s, i, g, b):
                c = i // 2 * DH if s == AB else (2 * i + g) * DH
                return (v_ab if s == AB else v_fox)[:, b, c:c + DH]

            def scores(s, i):
                if i >= 2:
                    pe.wait_ge(oT_ok, first_item[s] + i - 1)
                q = q_of[s]
                for g in range(2):
                    r = slice(g * DH, (g + 1) * DH)
                    pe.matmul(ps[:, item_bank(i) + g, 0:P], q[r, i, 0:P], key(s, i)[r, 0:P], start=True, stop=True)
                for g in range(2):
                    r = slice(g * DH, (g + 1) * DH)
                    mm = pe.matmul(ps[:, item_bank(i) + g, P:3 * P], q[r, i, P:SEQ], key(s, i)[r, :], start=True, stop=True)
                mm.then_inc(s_ps, 1)

            def turn_probs(s, i):
                pe.wait_ge(p_done, first_item[s] + i + 1)
                for g in range(2):
                    for b in range(3):
                        tr = pe.transpose(ps[:, item_bank(i) + g, tok(b)], p_of[s][:, i % 2, g, tok(b)], ident[:, :])
                tr.then_inc(pT_psd, 1)

            def head_outputs(s, i):
                pe.wait_ge(pT_okA, first_item[s] + i + 1)
                pe.wait_ge(pT_okV, first_item[s] + i + 1)
                for g in range(2):
                    pT = pT_of[s][:, i % 2, g, :]
                    r = slice(g * DH, (g + 1) * DH)
                    o_bank = item_bank(i)
                    pe.matmul(ps[r, o_bank, 0:P], value(s, i, g, 0), pT[:, 0:P], start=True, stop=True)
                    pe.matmul(ps[r, o_bank, P:SEQ], value(s, i, g, 0), pT[:, P:2 * P], start=True, stop=False)
                    mm = pe.matmul(ps[r, o_bank, P:SEQ], value(s, i, g, 1), pT[:, 2 * P:3 * P], start=False, stop=True)
                mm.then_inc(o_ps, 1)

            pe.wait_ge(consts, 1)
            pe.wait_ge(par_landed, 160)
            pe.transpose(ps[:, 6, 0:N_PAR], par_rows[0:N_PAR, 0, :], ident[0:N_PAR, 0:N_PAR])
            pe.transpose(ps[:, 7, 0:N_CW31], par_rows[0:N_CW31, 1, :], ident[0:N_CW31, 0:N_CW31]).then_inc(par_ps, 1)
            pe.wait_ge(raw_done, ADA_FIRST)
            row_everywhere(0, ada_sum0[:, 0:D])
            row_everywhere(2, ada_sum0[:, D:2 * D])

            for t in range(TOKT):
                turn_x(CONV, t)
            pe.wait_ge(xT_ok, 4)
            n = BASE[CONV]
            pe.wait_ge(par_ready, 3)
            for m in range(6):
                if m == 3:
                    pe.wait_ge(evac_a, 1)
                if m > 3:
                    pe.wait_ge(evac_v, m - 3)
                channel_chunk(n + 2 * m, 2 * (m % 3))
                if m == 2:
                    pe.wait_ge(ada_added, 4)
                    row_everywhere(6, tmp[:, 1, :])
                if m == 4:
                    pe.wait_ge(ada_added, 8)
                    pe.wait_ge(ada_row_a, 2)
                    row_everywhere(6, ada_acc)
            pe.wait_ge(evac_v, 4)
            pe.wait_ge(ada_row_a, 3)
            for i in range(4):
                pe.wait_ge(yT_ok, i // 2 + 1)
                first, last = i == 0, i == 3
                mm = down_part(n + 12 + i, yT_hi, yT_lo, 2 * i, 0, first, last)
                if last:
                    mm.then_inc(y_tok0, 1)
                down_part(n + 12 + i, yT_hi, yT_lo, 2 * i, 1, first, last).then_inc(w_used, 1)
                if i == 2:
                    pe.wait_ge(ada_added, 12)
                    row_everywhere(0, tmp[:, 1, :])
            pe.wait_ge(ada_added, 16)
            row_everywhere(2, ada_acc)

            def mixer_out(s, n, order, waits):
                for i, k0 in enumerate(order):
                    pe.wait_ge(*waits[i])
                    first, last = i == 0, i == len(order) - 1
                    mm = down_part(n + i, yT_hi, yT_lo, k0, 0, first, last)
                    if last:
                        mm.then_inc(y_tok0, 1)
                    down_part(n + i, yT_hi, yT_lo, k0, 1, first, last).then_inc(w_used, 1)

            if last_sub >= FFN0:
                ffn(FFN0)
            if last_sub >= FFN1:
                ffn(FFN1)
            if last_sub >= AB:
                for t in range(TOKT):
                    turn_x(AB, t)
                pe.wait_ge(xT_ok, 4 * AB + 4)
                n = BASE[AB]
                channel_chunk(n, 0)
                channel_chunk(n + 2, 2)
                channel_chunk(n + 4, 4)
                hi, lo = unit(n + 6)
                for k in range(KT):
                    product(ps[:, 6, 0:SEQ], hi[:, k * 256:k * 256 + P], lo[:, k * 256:k * 256 + P], xT_hi[:, k, :], xT_lo[:, k, :],
                            k == 0, k == KT - 1)
                for t in range(TOKT):
                    for k in range(KT):
                        c = slice(k * 256 + P, (k + 1) * 256)
                        mm = product(ps[:, 7, tok(t)], xT_hi[:, k, tok(t)], xT_lo[:, k, tok(t)], hi[:, c], lo[:, c],
                                     k == 0, k == KT - 1)
                mm.then_inc(w_used, 1)
                pe.wait_ge(evac_v, 5)
                pe.wait_ge(evac_a, 7)
                pe.wait_ge(k_landed, 32)
                scores(AB, 0)
                scores(AB, 1)
                for i in range(4):
                    turn_probs(AB, i)
                    head_outputs(AB, i)
                    if i + 2 < 4:
                        scores(AB, i + 2)
                pe.wait_ge(oT_ok, 4)
                pe.wait_ge(conv_done, 1)
                for t in range(TOKT):
                    for c in range(CCT):
                        tr = pe.transpose(ps[:, t, tok(c)], acc31[:, c, tok(t)], ident[:, :])
                    tr.then_inc(ln_ps, 1)
                for t in range(TOKT):
                    pe.wait_ge(ln_out, t + 1)
                    for c in range(CCT):
                        tr = pe.transpose(ps[:, 2 + c // 2, (c % 2) * SEQ + t * P:(c % 2) * SEQ + (t + 1) * P],
                                          ln_y[:, t, tok(c)], ident[:, :])
                    tr.then_inc(lnT_ps, 1)
                mixer_out(AB, n + 7, (4, 6, 0, 2), [(oT_ok, 4), (oT_ok, 4), (yT_ok, 3), (yT_ok, 3)])
            if last_sub >= FFN2:
                ffn(FFN2)
            if last_sub >= FFN3:
                ffn(FFN3)
            if last_sub >= FOX:
                n = BASE[FOX]
                logf = zf[:, 5, :]
                c_tok = zf[:, 6, :]

                def value_part(u, t):
                    hi, lo = unit(n + u)
                    for k in range(4):
                        c = slice(k * 512, (k + 1) * 512)
                        kt = 4 * (u % 2) + k
                        mm = product(ps[:, 4 + 2 * (u // 2) + t, :], xT_hi[:, kt, tok(t)], xT_lo[:, kt, tok(t)],
                                     hi[:, c], lo[:, c], kt == 0, kt == KT - 1)
                    if t == 1:
                        mm.then_inc(w_used, 1)

                def head_part(u, h):
                    hi, lo = unit(n + u)
                    if h == 0:
                        pe.wait_ge(evac_a, 7 + (1 if u < 6 else 2 if u < 8 else u - 5))
                    for k in range(4 * h, 4 * h + 4):
                        for c in range(2):
                            w_k = [v[:, k * 256 + c * P:k * 256 + (c + 1) * P] for v in (hi, lo)]
                            mm = product(ps[:, 4 + u % 4, c * SEQ:(c + 1) * SEQ], *w_k, xT_hi[:, k, :], xT_lo[:, k, :],
                                         k == 0 and c == 0, k == KT - 1)
                    if h == 1:
                        mm.then_inc(w_used, 1)

                def distance_rows(i):
                    if i >= 2:
                        pe.wait_ge(d_raw_v if i % 2 else d_raw_a, i // 2)
                    for g in range(2):
                        h = 2 * i + g
                        mm = pe.matmul(ps[:, i % 2, g * SEQ:(g + 1) * SEQ],
                                       ident[0:FOX_H, h:h + 1].to_broadcast([FOX_H, P]), cT[:, :], start=True, stop=True)
                    mm.then_inc(d_ps, 1)

                turn_x(FOX, 0)
                pe.wait_ge(xT_ok, 4 * FOX + 1)
                value_part(0, 0)
                turn_x(FOX, 1)
                pe.wait_ge(xT_ok, 4 * FOX + 2)
                value_part(1, 0)
                pe.wait_ge(xT_ok, 4 * FOX + 3)
                value_part(0, 1)
                pe.wait_ge(xT_ok, 4 * FOX + 4)
                pe.wait_ge(zf_ok, 2)
                for t in range(TOKT):
                    for k in range(KT):
                        mm = product(ps[:, 0, t * FOX_H:(t + 1) * FOX_H], xT_hi[:, k, tok(t)], xT_lo[:, k, tok(t)],
                                     zf_hi[:, k, :], zf_lo[:, k, :], k == 0, k == KT - 1)
                mm.then_inc(zf_p, 1)
                value_part(1, 1)
                value_part(2, 0)
                pe.wait_ge(zf_v, 1)
                pe.matmul(ps[:, 0, 64:80], upper[:, :], logf[:, 0:16], start=True, stop=True)
                pe.matmul(ps[:, 0, 80:96], upper[:, :], logf[:, 16:32], start=True, stop=False)
                pe.matmul(ps[:, 0, 80:96], ones[:, :], logf[:, 0:16], start=False, stop=True).then_inc(zf_p, 1)
                value_part(2, 1)
                pe.wait_ge(zf_a, 1)
                for t in range(TOKT):
                    tr = pe.transpose(ps[0:FOX_H, 0, P + t * P:P + (t + 1) * P], c_tok[:, t * 16:(t + 1) * 16], ident[:, :])
                tr.then_inc(zf_p, 1)
                value_part(3, 0)
                pe.wait_ge(zf_a, 2)
                distance_rows(0)
                distance_rows(1)
                value_part(3, 1)
                head_part(4, 0)
                distance_rows(2)
                distance_rows(3)
                head_part(4, 1)
                distance_rows(4)
                distance_rows(5)
                head_part(5, 0)
                distance_rows(6)
                distance_rows(7)
                head_part(5, 1)

                def out_part(u, t):
                    pe.wait_ge(oT_ok, 4 + 2 * (u - 12) + 2)
                    mm = down_part(n + u, yT_hi, yT_lo, 2 * (u - 12), t, u == 12, u == 15)
                    if t == 1:
                        mm.then_inc(w_used, 1)
                    elif u == 15:
                        mm.then_inc(y_tok0, 1)

                for i in range(FOX_H // 2 + 1):
                    part_of = head_part if i < 6 else out_part
                    if i:
                        turn_probs(FOX, i - 1)
                    if i < FOX_H // 2:
                        if i == 1:
                            pe.wait_ge(d_raw_a, 4)
                            pe.wait_ge(d_raw_v, 4)
                        pe.wait_ge(evac_a, 7 + 2 + 2 * (i // 2 + 1))
                        scores(FOX, i)
                    if i == 6:
                        pe.wait_ge(evac_a, 7 + 10)
                    part_of(6 + i, 0)
                    if i:
                        head_outputs(FOX, i - 1)
                    part_of(6 + i, 1)
                out_part(15, 0)
                out_part(15, 1)
            if last_sub >= FFN4:
                ffn(FFN4)

        @block.scalar
        def _(act):
            warmed = [0]

            def warm_up(func):
                c = warmed[0]
                warmed[0] += 1
                act.activation(warm[:, c:c + 1], eps[:, 0:1], func)

            def split(n, j=0, wait_used=True):
                v = weight_count(n) - 1
                if n >= TOTAL or n >= limit:
                    return
                act.wait_ge(landed[slot_of(n)], 32 * (n // NSLOT + 1 + j) if isinstance(j, int) else j * 32 + 32 * (n // NSLOT + 1))
                if not (isinstance(j, int) and v + NSLOT * j < NSLOT):
                    act.wait_ge(w_used, v - NSLOT + 1 + NSLOT * j)
                g = gain_column(n)
                if g is None:
                    act.activation(w_hi[:, slot_of(n), :], raw[:, slot_of(n), :], ACT.Copy).then_inc(hi_ready, 1)
                else:
                    for k in range(4):
                        c = slice(k * 512, (k + 1) * 512)
                        a = act.activation(w_hi[:, slot_of(n), c], raw[:, slot_of(n), c], ACT.Copy, scale=par[:, g + k:g + k + 1])
                    a.then_inc(hi_ready, 1)

            limit = y_unit(last_sub) + 1

            def square_root(c, src, junk, sq, std, count):
                act.activation(junk, src, ACT.Square, scale=D ** -0.5, accum_out=stat[:, 0, c:c + 1]).then_inc(sq, 1)
                act.wait_ge(sq, count)
                act.activation(stat[:, 1, c:c + 1], stat[:, 0, c:c + 1], ACT.Sqrt, bias=eps[:, 0:1]).then_inc(std, 1)

            def root_y(b, t):
                act.wait_ge(w_used if t else y_tok0, weight_count(y_unit(b)) if t else b + 1)
                e = 2 * (b - FFN1) + t
                square_root(STAT_Y + e, ps[:, 4 + 2 * t:6 + 2 * t, :].rearrange("p b n -> p (b n)"), xn[:, t, :],
                            y_sq, y_std, e + 1)

            def root_x(e, t):
                square_root(2 * e + t, x[:, t, :], (tmp if e else xn)[:, t, :], x_sq, x_std, 2 * e + t + 1)

            def turned_hi(s, t):
                for h in range(2):
                    act.wait_ge(xT_ps, 4 * s + 2 * t + h + 1)
                    act.activation(xT_hi[:, 4 * h:4 * h + 4, t * P:(t + 1) * P],
                                   ps[:, 2 * t + h, :].rearrange("p (k c) -> p k c", k=4), ACT.Copy).then_inc(xT_hi_ok, 1)

            def between(b, func=None):
                s = b + 1
                warm_up(ACT.Sqrt)

                def before(t):
                    act.wait_ge(x_new, x_count(b, t, 1))
                    root_x(x_event(s), t)

                def after(t):
                    if b == FFN0:
                        act.wait_ge(x_mid, t + 1)
                        root_x(FINAL_EVENT, t)
                    elif b > FFN0:
                        root_y(b, t)

                if s in FOLDED:
                    after(0)
                    turned_hi(s, 0)
                    after(1)
                    before(0)
                    turned_hi(s, 1)
                    before(1)
                elif s in NORMED:
                    after(0)
                    before(0)
                    after(1)
                    turned_hi(s, 0)
                    before(1)
                    turned_hi(s, 1)
                else:
                    after(0)
                    after(1)
                if func is not None:
                    warm_up(func)

            def ffn(s):
                f, n = ffn_index(s), BASE[s]
                v = weight_count(n)

                def gates(j):
                    for t in range(TOKT):
                        if t == 0:
                            act.wait_ge(up_tok0, NCH * f + 1 + j)
                        else:
                            act.wait_ge(w_used, v + 1 if isinstance(j, int) and j == 0 else v + 3 * j)
                        c = 2 * x_event(s) + t
                        act.activation(sil[:, t, :], ps[:, t, 0:FCH], ACT.Silu,
                                       scale=stat[:, 2, c:c + 1] if s in FOLDED else 1.0).then_inc(sil_done, 1)

                def turned(j, dst):
                    act.wait_ge(hT_ps, NCH * f + 1 + j)
                    act.activation(dst, ps[:, 2, :].rearrange("p (f c) -> p f c", f=2), ACT.Copy).then_inc(hT_hi_ok, 1)

                def chunk(j):
                    split(n + 2, j)
                    gates(j)
                    split(n + 3, j)
                    split(n + 4, j)
                    turned(j, hT_hi[:, :, :])

                if s in FOLDED:
                    act.wait_ge(x_rstd, 2 * x_event(s) + 2)
                chunk(0)
                with act.Fori(1, NCH - 1) as j:
                    chunk(j)
                split(n + FFN_UNITS - 1)
                gates(NCH - 1)
                turned(NCH - 1, yT_hi[:, 0:2, :])
                split(n + FFN_UNITS)
                split(n + FFN_UNITS + 1)

            act.wait_ge(par_ps, 1)
            act.wait_ge(consts, 1)
            act.activation(cond[:, :], ps[:, 6, C_COND:C_COND + KT], ACT.Silu).then_inc(par_ready, 1)
            act.activation(par[:, :], ps[:, 6, 0:N_PAR], ACT.Copy).then_inc(par_ready, 1)
            act.activation(cw31[:, :], ps[:, 7, 0:N_CW31], ACT.Copy).then_inc(par_ready, 1)
            act.wait_ge(par_ready, 3)
            act.wait_ge(x_landed, 16)
            for t in range(TOKT):
                root_x(0, t)
            split(BASE[CONV])
            split(BASE[CONV] + 1)
            act.wait_ge(ada_ps, 1)
            act.activation(rows[:, 3, :], ps[:, 0:2, :].rearrange("p b n -> p (b n)"), ACT.Copy).then_inc(ada_row_a, 1)
            for t in range(TOKT):
                turned_hi(CONV, t)

            def ada_scale(r):
                act.wait_ge(ada_landed[r % ADA_REST_SLOTS], 16 * (r // ADA_REST_SLOTS + 1))
                for i in range(2):
                    k = 2 * (r % 4) + i
                    a = act.activation(ada_raw[:, r % ADA_REST_SLOTS, i, :], ada_raw[:, r % ADA_REST_SLOTS, i, :], ACT.Copy,
                                       scale=cond[:, k:k + 1])
                a.then_inc(ada_scaled, 1)

            n = BASE[CONV]
            for k in range(2, 18):
                m = (k - 4) // 2
                if k % 2 == 0 and 0 <= m < 6:
                    act.wait_ge(w_used, weight_count(n + 2 * m + 1))
                    if m % 3 == 0:
                        if m == 3:
                            act.wait_ge(evac_v, 1)
                        act.activation(gate_c[:, :, :].rearrange("p a b -> p (a b)"),
                                       ps[:, 0:2, :].rearrange("p b n -> p (b n)"), ACT.Copy).then_inc(evac_a, 1)
                    if m % 3 == 2:
                        h = m // 3
                        act.wait_ge(evac_v, 2 * h + 2)
                        act.activation(yT_hi[:, 4 * h:4 * h + 4, :], conv_y[:, :, :], ACT.Copy).then_inc(yT_hi_ok, 1)
                split(n + k)
                ada_scale(k - 2)
                if k == 9:
                    act.wait_ge(ada_ps, 3)
                    act.activation(rows[:, 1, :], ps[:, 6:8, :].rearrange("p b n -> p (b n)"), ACT.Copy).then_inc(ada_row_a, 1)
                if k == 13:
                    act.wait_ge(ada_ps, 4)
                    act.activation(rows[:, 3, :], ps[:, 6:8, :].rearrange("p b n -> p (b n)"), ACT.Copy).then_inc(ada_row_a, 1)
            act.wait_ge(ada_ps, 6)
            act.activation(rows[:, 2, :], ps[:, 2:4, :].rearrange("p b n -> p (b n)"), ACT.Copy).then_inc(ada_row_a, 1)

            def exps(s, i):
                item = first_item[s] + i
                c = 4 * item
                act.wait_ge(m_ok, item + 1)
                for b in range(2):
                    for g in range(2):
                        a = c + 2 * b + g
                        d = p_of[s][:, i % 2, g, 0:P] if b == 0 else p_of[s][:, i % 2, g, P:3 * P]
                        e = act.activation(d, d, ACT.Exp, bias=soft[:, 1, a:a + 1], accum_out=soft[:, 3, a:a + 1])
                if s == AB:
                    e = act.activation(soft[:, 5, c:c + 4], soft[:, 2, c:c + 4], ACT.Exp)
                e.then_inc(e_done, 1)

            def probs_out(s, i):
                act.wait_ge(pT_psd, first_item[s] + i + 1)
                act.activation(pT_of[s][:, i % 2, 0, :], ps[:, item_bank(i), 0:384], ACT.Copy).then_inc(pT_okA, 1)

            def outputs_hi(s, i):
                act.wait_ge(o_ps, first_item[s] + i + 1)
                act.activation(yT_hi[:, out_kt[s] + i, :], ps[:, item_bank(i), 0:SEQ], ACT.Copy).then_inc(oT_hi_ok, 1)

            if last_sub >= FFN0:
                between(CONV, ACT.Silu)
                ffn(FFN0)
            if last_sub >= FFN1:
                between(FFN0, ACT.Silu)
                ffn(FFN1)
            if last_sub >= AB:
                between(FFN1, ACT.Sigmoid)
                n = BASE[AB]
                for k in range(2, 10):
                    if k == 7:
                        act.wait_ge(w_used, weight_count(n + 3))
                        act.activation(sig.rearrange("p a b -> p (a b)"), ps[:, 2:4, :].rearrange("p b n -> p (b n)"),
                                       ACT.Sigmoid).then_inc(evac_a, 1)
                    if k == 9:
                        act.wait_ge(w_used, weight_count(n + 5))
                        act.activation(q_ab.rearrange("p a b -> p (a b)"), ps[:, 4:6, :].rearrange("p b n -> p (b n)"),
                                       ACT.Copy).then_inc(evac_a, 1)
                        act.wait_ge(w_used, weight_count(n + 6))
                        for g in range(SWA_HKV):
                            r = slice(g * DH, (g + 1) * DH)
                            act.activation(k_ab[r, g, :], ps[r, 6, 0:SEQ], ACT.Copy).then_inc(evac_a, 1)
                        act.wait_ge(evac_a, 6)
                        act.dma_start(k_ab[DH:P, 0, :], k_ab[0:DH, 0, :]).then_inc(k_landed, 16)
                        act.dma_start(k_ab[0:DH, 1, :], k_ab[DH:P, 1, :]).then_inc(k_landed, 16)
                        act.activation(v_ab.rearrange("p a b -> p (a b)"), ps[:, 7, 0:SEQ], ACT.Copy).then_inc(evac_a, 1)
                    split(n + k)
                exps(AB, 0)
                for i in range(4):
                    if i + 1 < 4:
                        exps(AB, i + 1)
                    probs_out(AB, i)
                    outputs_hi(AB, i)
                warm_up(ACT.Sqrt)
                for t in range(TOKT):
                    act.wait_ge(ln_stat, t + 1)
                    act.activation(zf[:, 7, 8 * t + 2:8 * t + 3], zf[:, 7, 8 * t + 1:8 * t + 2], ACT.Sqrt, bias=eps[:, 0:1]).then_inc(ln_std, 1)
                warm_up(ACT.Silu)
                act.wait_ge(lnT_ps, 2)
                for c in range(CCT):
                    a = act.activation(ab_y[:, c, :], ps[:, 2 + c // 2, (c % 2) * SEQ:(c % 2 + 1) * SEQ], ACT.Silu,
                                       scale=par[:, C_LNG + c:C_LNG + c + 1], bias=par[:, C_LNB + c:C_LNB + c + 1])
                a.then_inc(ab_y_ok, 1)
                act.wait_ge(ab_y_ok, 1)
                act.activation(yT_hi[:, 0:4, :], ab_y, ACT.Copy).then_inc(yT_hi_ok, 1)
                for k in range(10, 13):
                    split(n + k)
            if last_sub >= FFN2:
                between(AB, ACT.Silu)
                ffn(FFN2)
            if last_sub >= FFN3:
                between(FFN2, ACT.Silu)
                ffn(FFN3)
            if last_sub >= FOX:
                between(FFN3, ACT.Exp)
                n = BASE[FOX]
                split(n + 2)
                act.wait_ge(zf_z, 1)
                act.activation(zf[:, 2, :], zf[:, 1, :], ACT.Exp, scale=-1.0).then_inc(zf_e, 1)
                act.wait_ge(zf_e, 1)
                act.activation(zf[:, 3, :], zf[:, 2, :], ACT.Ln, bias=1.0).then_inc(zf_e, 1)

                def distances(i):
                    act.wait_ge(d_ps, i + 1)
                    for g in range(2):
                        h = 2 * i + g
                        src = ps[:, 0, g * SEQ:(g + 1) * SEQ]
                        act.activation(decay[:, h, 0:P], src[:, 0:P], ACT.Identity, bias=zf[:, 6, h:h + 1])
                        a = act.activation(decay[:, h, P:3 * P], src, ACT.Identity, bias=zf[:, 6, 16 + h:17 + h])
                    a.then_inc(d_raw_a, 1)

                def values_out(h):
                    act.wait_ge(w_used, weight_count(n + 2 * h + 1))
                    act.activation(v_fox[:, :, h * 512:(h + 1) * 512], ps[:, 4 + 2 * h:6 + 2 * h, :], ACT.Copy).then_inc(evac_a, 1)

                def heads_out(u):
                    act.wait_ge(w_used, weight_count(n + u))
                    i = 2 * ((u - 4) // 2)
                    act.activation((k_fox if u % 2 else q_fox)[:, i:i + 2, :],
                                   ps[:, 4 + u % 4, :].rearrange("p (a c) -> p a c", a=2), ACT.Copy).then_inc(evac_a, 1)

                split(n + 3)
                values_out(0)
                split(n + 4)
                act.wait_ge(zf_p, 2)
                act.activation(zf[:, 6, :], ps[:, 0, 64:96], ACT.Copy).then_inc(zf_a, 1)
                act.wait_ge(zf_p, 3)
                act.activation(cT[:, :], ps[0:FOX_H, 0, P:P + SEQ], ACT.Copy, scale=-1.0).then_inc(zf_a, 1)
                split(n + 5)
                act.wait_ge(zf_a, 1)
                distances(0)
                values_out(1)
                split(n + 6)
                distances(2)
                heads_out(4)
                split(n + 7)
                distances(4)
                distances(6)
                for i in range(FOX_H // 2):
                    if i < 7:
                        heads_out(5 + i)
                    if i:
                        probs_out(FOX, i - 1)
                    split(n + 8 + i)
                    exps(FOX, i)
                    if i:
                        outputs_hi(FOX, i - 1)
                probs_out(FOX, 7)
                split(n + 16)
                outputs_hi(FOX, 7)
                split(n + 17)
            if last_sub >= FFN4:
                between(FOX, ACT.Silu)
                ffn(FFN4)
            if last_sub > FFN0:
                between(last_sub)

        @block.vector
        def _(dve):
            limit = y_unit(last_sub) + 1
            chained = [0]

            def link(ins):
                chained[0] += 1
                ins.then_inc(m_chain, 1)
                dve.wait_ge(m_chain, chained[0])

            def split(n, j=0):
                if n >= limit:
                    return
                dve.wait_ge(hi_ready, weight_count(n) + NSLOT * j)
                g = gain_column(n)
                if g is None:
                    dve.tensor_tensor(w_lo[:, slot_of(n), :], raw[:, slot_of(n), :], w_hi[:, slot_of(n), :].bitcast(F32),
                                      ALU.subtract).then_inc(raw_done, 1)
                else:
                    for k in range(4):
                        c = slice(k * 512, (k + 1) * 512)
                        o = dve.scalar_tensor_tensor(w_lo[:, slot_of(n), c], raw[:, slot_of(n), c], par[:, g + k:g + k + 1],
                                                     w_hi[:, slot_of(n), c].bitcast(F32), ALU.mult, ALU.subtract)
                    o.then_inc(raw_done, 1)

            def reciprocal_root(c, std, rstd, count):
                dve.wait_ge(std, count)
                dve.reciprocal(stat[:, 2, c:c + 1], stat[:, 1, c:c + 1]).then_inc(rstd, 1)
                dve.wait_ge(rstd, count)
                return stat[:, 2, c:c + 1]

            def rms_x(e, t):
                return reciprocal_root(2 * e + t, x_std, x_rstd, 2 * e + t + 1)

            def output(t):
                return ps[:, 4 + 2 * t:6 + 2 * t, :].rearrange("p b n -> p (b n)")

            def residual(b, t):
                if b <= FFN0:
                    dve.wait_ge(w_used if t else y_tok0, weight_count(y_unit(b)) if t else b + 1)
                    dve.tensor_tensor(tmp[:, t, :], output(t), rows[:, 2 if b else 1, :], ALU.mult).then_inc(t_done, 1)
                    scale = 1.0
                else:
                    e = 2 * (b - FFN1) + t
                    r = reciprocal_root(STAT_Y + e, y_std, y_rstd, e + 1)
                    dve.scalar_tensor_tensor(tmp[:, t, :], output(t), r, rows[:, 1, :], ALU.mult, ALU.mult).then_inc(t_done, 1)
                    scale = 1.0 if b in (AB, FOX) else 0.5
                dve.wait_ge(t_done, 2 * b + t + 1)
                for h in range(2):
                    c = slice(h * 512, (h + 1) * 512)
                    o = dve.scalar_tensor_tensor(x[:, t, c], tmp[:, t, c], scale, x[:, t, c], ALU.mult, ALU.add)
                    if b != FFN0:
                        o.then_inc(x_new, 1)
                if b == FFN0:
                    o.then_inc(x_mid, 1)
                    r = rms_x(FINAL_EVENT, t)
                    for h in range(2):
                        c = slice(h * 512, (h + 1) * 512)
                        dve.scalar_tensor_tensor(x[:, t, c], x[:, t, c], r, rows[:, 1, c], ALU.mult, ALU.mult).then_inc(x_new, 1)

            def norm_x(s, t):
                r = rms_x(x_event(s), t)
                o = dve.scalar_tensor_tensor(xn[:, t, :], x[:, t, :], r, rows[:, 0, :], ALU.mult, ALU.mult)
                if s <= FFN0:
                    o.then_inc(xn_part, 1)
                    dve.wait_ge(xn_part, 2 * s + t + 1)
                    o = dve.tensor_tensor(xn[:, t, :], xn[:, t, :], rows[:, 3, :], ALU.add)
                o.then_inc(xn_done, 1)

            def turned_lo(s, t):
                for h in range(2):
                    at = xT_lo[:, 4 * h:4 * h + 4, t * P:(t + 1) * P]
                    dve.wait_ge(xT_hi_ok, 4 * s + 2 * t + h + 1)
                    dve.tensor_tensor(at, ps[:, 2 * t + h, :].rearrange("p (k c) -> p k c", k=4),
                                      xT_hi[:, 4 * h:4 * h + 4, t * P:(t + 1) * P].bitcast(F32), ALU.subtract).then_inc(xT_ok, 1)

            def between(b):
                s = b + 1
                if b > CONV:
                    dve.wait_ge(rows_landed, rows_count(b))
                if s in FOLDED:
                    residual(b, 0)
                    turned_lo(s, 0)
                    residual(b, 1)
                    rms_x(x_event(s), 0)
                    turned_lo(s, 1)
                    rms_x(x_event(s), 1)
                elif s in NORMED:
                    residual(b, 0)
                    norm_x(s, 0)
                    residual(b, 1)
                    turned_lo(s, 0)
                    norm_x(s, 1)
                    turned_lo(s, 1)
                else:
                    residual(b, 0)
                    residual(b, 1)

            def ffn(s):
                f, n = ffn_index(s), BASE[s]

                def hidden(j):
                    for t in range(TOKT):
                        dve.wait_ge(sil_done, 2 * NCH * f + t + 1 + 2 * j)
                        up = ps[:, t, FCH:2 * FCH]
                        if s in FOLDED:
                            c = 2 * x_event(s) + t
                            o = dve.scalar_tensor_tensor(hid[:, t, :], up, stat[:, 2, c:c + 1], sil[:, t, :], ALU.mult, ALU.mult)
                        else:
                            o = dve.tensor_tensor(hid[:, t, :], up, sil[:, t, :], ALU.mult)
                        o.then_inc(hid_done, 1)

                def turned(j, dst, hi):
                    dve.wait_ge(hT_hi_ok, NCH * f + 1 + j)
                    dve.tensor_tensor(dst, ps[:, 2, :].rearrange("p (f c) -> p f c", f=2), hi.bitcast(F32),
                                      ALU.subtract).then_inc(hT_ok, 1)

                def chunk(j):
                    split(n + 2, j)
                    hidden(j)
                    split(n + 3, j)
                    split(n + 4, j)
                    turned(j, hT_lo[:, :, :], hT_hi[:, :, :])

                chunk(0)
                with dve.Fori(1, NCH - 1) as j:
                    chunk(j)
                split(n + FFN_UNITS - 1)
                hidden(NCH - 1)
                turned(NCH - 1, yT_lo[:, 0:2, :], yT_hi[:, 0:2, :])
                split(n + FFN_UNITS)
                split(n + FFN_UNITS + 1)

            dve.wait_ge(par_ready, 1)
            dve.wait_ge(bias_landed, 16)
            for k in range(KT):
                dve.wait_ge(landed[slot_of(k)], 32 * (k // NSLOT + 1))
                if k:
                    dve.wait_ge(raw_done, k)
                dve.scalar_tensor_tensor(ada_sum0, raw[:, slot_of(k), :], cond[:, k:k + 1], ada_sum0, ALU.mult, ALU.add)\
                    .then_inc(raw_done, 1)
            n = BASE[CONV]
            split(n)
            split(n + 1)
            dve.wait_ge(ada_ps, 2)
            dve.wait_ge(row_g1_landed, 16)
            dve.scalar_tensor_tensor(rows[:, 0, :], ps[:, 2:4, :].rearrange("p b n -> p (b n)"), 1.0, rows[:, 0, :],
                                     ALU.add, ALU.mult).then_inc(ada_row_v, 1)
            dve.wait_ge(ada_row_v, 1)
            dve.wait_ge(ada_row_a, 1)
            for t in range(TOKT):
                norm_x(CONV, t)
            for t in range(TOKT):
                turned_lo(CONV, t)
            dve.wait_ge(pads, 1)
            for k in range(2, 18):
                m = (k - 4) // 2
                if k % 2 == 0 and 0 <= m < 6 and m % 3:
                    h = m // 3
                    dve.wait_ge(w_used, weight_count(n + 2 * m + 1))
                    if m % 3 == 1:
                        dve.wait_ge(evac_a, h + 1)
                        for b in range(2):
                            u = dve.tensor_tensor(u_pad[:, 2 * b:2 * b + 2, :, 1:GRID_W + 1],
                                                  ps[:, 2 + b, :].rearrange("p (a r c) -> p a r c", a=2, r=4),
                                                  gate_c[:, 2 * b:2 * b + 2, :].rearrange("p a (r c) -> p a r c", r=4), ALU.mult)
                        u.then_inc(evac_v, 1)
                        dve.wait_ge(evac_v, 2 * h + 1)
                        for i, tp in enumerate((1, 0, 2)):
                            for c in range(CCT):
                                wt = C_CONVW + tp * KT + 4 * h + c
                                o = conv_acc[:, c, :].rearrange("p (r c) -> p r c", r=4)
                                src = u_pad[:, c, :, tp:tp + GRID_W]
                                if i == 0:
                                    o = dve.tensor_scalar(o, src, par[:, wt:wt + 1], None, ALU.mult)
                                else:
                                    dve.wait_ge(tap, 12 * h + 4 * (i - 1) + c + 1)
                                    o = dve.scalar_tensor_tensor(o, src, par[:, wt:wt + 1], o, ALU.mult, ALU.add)
                                o.then_inc(tap, 1)
                    else:
                        dve.wait_ge(tap, 12 * h + 12)
                        if h:
                            dve.wait_ge(yT_hi_ok, h)
                        dve.tensor_tensor(conv_y.rearrange("p a b -> p (a b)"), ps[:, 4:6, :].rearrange("p b n -> p (b n)"),
                                          conv_acc.rearrange("p a b -> p (a b)"), ALU.mult).then_inc(evac_v, 1)
                        dve.wait_ge(yT_hi_ok, h + 1)
                        dve.tensor_tensor(yT_lo[:, 4 * h:4 * h + 4, :], conv_y, yT_hi[:, 4 * h:4 * h + 4, :].bitcast(F32),
                                          ALU.subtract).then_inc(yT_ok, 1)
                split(n + k)
            dve.wait_ge(ada_ps, 5)
            dve.wait_ge(g2_row_landed, 16)
            dve.scalar_tensor_tensor(rows[:, 0, :], ps[:, 0:2, :].rearrange("p b n -> p (b n)"), 1.0, rows[:, 0, :],
                                     ALU.add, ALU.mult).then_inc(ada_row_v, 1)
            dve.wait_ge(ada_row_v, 2)
            dve.wait_ge(ada_row_a, 4)
            between(CONV)

            def scaled(s, i, bias, sink=None):
                item = first_item[s] + i
                c = 4 * item
                p = p_of[s]
                dve.wait_ge(s_ps, item + 1)
                dve.scalar_tensor_tensor(p[:, i % 2, :, :], ps[:, item_bank(i):item_bank(i) + 2, 0:384], DH ** -0.5, bias,
                                         ALU.mult, ALU.add).then_inc(s_sb, 1)
                dve.wait_ge(s_sb, item + 1)
                for b in range(2):
                    d = p[:, i % 2, :, 0:P] if b == 0 else p[:, i % 2, :, P:3 * P]
                    mx = dve.tensor_reduce(soft[:, 0, c + 2 * b:c + 2 * b + 2], d, AX_X, ALU.max)
                    if b == 1:
                        link(mx)
                if sink is not None:
                    link(dve.tensor_tensor(soft[:, 4, c:c + 4].rearrange("p (b g) -> p b g", b=2),
                                           soft[:, 0, c:c + 4].rearrange("p (b g) -> p b g", b=2), sink, ALU.max))
                    link(dve.tensor_tensor(soft[:, 2, c:c + 4].rearrange("p (b g) -> p b g", b=2), sink,
                                           soft[:, 4, c:c + 4].rearrange("p (b g) -> p b g", b=2), ALU.subtract))
                dve.tensor_scalar(soft[:, 1, c:c + 4], soft[:, 0 if sink is None else 4, c:c + 4], -1.0, None,
                                  ALU.mult).then_inc(m_ok, 1)

            def normed(s, i):
                item = first_item[s] + i
                c = 4 * item
                dve.wait_ge(e_done, item + 1)
                z = soft[:, 3, c:c + 4]
                if s == AB:
                    link(dve.tensor_tensor(soft[:, 6, c:c + 4], z, soft[:, 5, c:c + 4], ALU.add))
                    z = soft[:, 6, c:c + 4]
                link(dve.reciprocal(soft[:, 7, c:c + 4], z))
                for b in range(2):
                    for g in range(2):
                        d = p_of[s][:, i % 2, g, 0:P] if b == 0 else p_of[s][:, i % 2, g, P:3 * P]
                        a = c + 2 * b + g
                        q = dve.tensor_scalar(d, d, soft[:, 7, a:a + 1], None, ALU.mult)
                q.then_inc(p_done, 1)

            def probs_out(s, i):
                dve.wait_ge(pT_psd, first_item[s] + i + 1)
                dve.tensor_copy(pT_of[s][:, i % 2, 1, :], ps[:, item_bank(i) + 1, 0:384]).then_inc(pT_okV, 1)

            def outputs_lo(s, i):
                dve.wait_ge(oT_hi_ok, first_item[s] + i + 1)
                dve.tensor_tensor(yT_lo[:, out_kt[s] + i, :], ps[:, item_bank(i), 0:SEQ],
                                  yT_hi[:, out_kt[s] + i, :].bitcast(F32), ALU.subtract).then_inc(oT_ok, 1)

            if last_sub >= FFN0:
                ffn(FFN0)
            if last_sub >= FFN1:
                between(FFN0)
                ffn(FFN1)
            if last_sub >= AB:
                between(FFN1)
                n = BASE[AB]
                done = [0]

                def taps(count):
                    for tp in range(done[0], min(done[0] + count, CONV_K)):
                        for c in range(CCT):
                            wt = cw31[:, tp * CCT + c:tp * CCT + c + 1]
                            src = a_pad[:, c, tp:tp + SEQ]
                            if tp == 0:
                                o = dve.tensor_scalar(acc31[:, c, :], src, wt, par[:, C_CB + c:C_CB + c + 1], ALU.mult, ALU.add)
                            else:
                                dve.wait_ge(tap, 24 + CCT * (tp - 1) + c + 1)
                                o = dve.scalar_tensor_tensor(acc31[:, c, :], src, wt, acc31[:, c, :], ALU.mult, ALU.add)
                            o.then_inc(tap, 1)
                    done[0] = min(done[0] + count, CONV_K)

                for k in range(2, 10):
                    if k == 7:
                        dve.wait_ge(evac_a, 3)
                        dve.wait_ge(pads, 2)
                        dve.tensor_tensor(a_pad[:, :, CONV_K - 1:], ps[:, 0:2, :].rearrange("p b (a c) -> p (b a) c", a=2), sig,
                                          ALU.mult).then_inc(evac_v, 1)
                    split(n + k)
                    if k >= 7:
                        dve.wait_ge(evac_v, 5)
                        taps(3)
                dve.wait_ge(bias_built, 1)
                dve.wait_ge(misc_landed, 48)
                sink_v = sinks[:, :].rearrange("p (c g) -> p c g", g=2)

                def ab_scaled(i):
                    scaled(AB, i, alibi[:, 2 * i:2 * i + 2, :], sink_v[:, i:i + 1, :].to_broadcast([P, 2, 2]))

                ab_scaled(0)
                for i in range(4):
                    if i + 1 < 4:
                        ab_scaled(i + 1)
                    taps(1)
                    normed(AB, i)
                    taps(1)
                    probs_out(AB, i)
                    taps(1)
                    outputs_lo(AB, i)
                taps(CONV_K)
                dve.wait_ge(tap, 24 + CCT * CONV_K)
                dve.tensor_copy(warm[:, 23:24], acc31[:, 0, 0:1]).then_inc(conv_done, 1)
                for t in range(TOKT):
                    dve.wait_ge(ln_ps, t + 1)
                    link(dve.bn_stats(soft[:, 0, 50 + 6 * t:56 + 6 * t], ps[:, t, :]))
                    dve.bn_aggr(zf[:, 7, 8 * t:8 * t + 2], soft[:, 0, 50 + 6 * t:56 + 6 * t]).then_inc(ln_stat, 1)
                for t in range(TOKT):
                    dve.wait_ge(ln_std, t + 1)
                    link(dve.reciprocal(zf[:, 7, 8 * t + 3:8 * t + 4], zf[:, 7, 8 * t + 2:8 * t + 3]))
                    dve.tensor_scalar(ln_y[:, t, :], ps[:, t, :], zf[:, 7, 8 * t:8 * t + 1], zf[:, 7, 8 * t + 3:8 * t + 4],
                                      ALU.subtract, ALU.mult).then_inc(ln_out, 1)
                dve.wait_ge(yT_hi_ok, 3)
                dve.tensor_tensor(yT_lo[:, 0:4, :], ab_y, yT_hi[:, 0:4, :].bitcast(F32), ALU.subtract).then_inc(yT_ok, 1)
                for k in range(10, 13):
                    split(n + k)
            if last_sub >= FFN2:
                between(AB)
                ffn(FFN2)
            if last_sub >= FFN3:
                between(FFN2)
                dve.tensor_copy(zf_hi[:, :, :], zf_raw[:, :, :]).then_inc(zf_ok, 1)
                dve.wait_ge(zf_ok, 1)
                dve.tensor_tensor(zf_lo[:, :, :], zf_raw[:, :, :], zf_hi[:, :, :].bitcast(F32), ALU.subtract).then_inc(zf_ok, 1)
                ffn(FFN3)
            if last_sub >= FOX:
                between(FFN3)
                n = BASE[FOX]
                split(n + 2)
                dve.wait_ge(zf_p, 1)
                for t in range(TOKT):
                    o = dve.tensor_tensor(zf[:, 0, t * 16:(t + 1) * 16], ps[:, 0, t * 16:(t + 1) * 16], b_f[:, :], ALU.add)
                link(o)
                dve.scalar_tensor_tensor(zf[:, 1, :], zf[:, 0, :], -1.0, zf[:, 0, :], ALU.mult, ALU.max).then_inc(zf_z, 1)
                link(dve.tensor_scalar(zf[:, 4, :], zf[:, 0, :], 0.0, None, ALU.min))
                dve.wait_ge(zf_e, 2)
                dve.tensor_tensor(zf[:, 5, :], zf[:, 4, :], zf[:, 3, :], ALU.subtract).then_inc(zf_v, 1)

                def distances(i):
                    dve.wait_ge(d_ps, i + 1)
                    for g in range(2):
                        h = 2 * i + g
                        src = ps[:, 1, g * SEQ:(g + 1) * SEQ]
                        dve.tensor_scalar(decay[:, h, 0:P], src[:, 0:P], zf[:, 6, h:h + 1], None, ALU.add)
                        o = dve.tensor_scalar(decay[:, h, P:3 * P], src, zf[:, 6, 16 + h:17 + h], None, ALU.add)
                    o.then_inc(d_raw_v, 1)

                split(n + 3)
                split(n + 4)
                split(n + 5)
                distances(1)
                split(n + 6)
                distances(3)
                split(n + 7)
                distances(5)
                distances(7)
                for i in range(FOX_H // 2):
                    if i:
                        probs_out(FOX, i - 1)
                    dve.wait_ge(d_ok, i + 1)
                    scaled(FOX, i, decay[:, 2 * i:2 * i + 2, :])
                    split(n + 8 + i)
                    normed(FOX, i)
                    if i:
                        outputs_lo(FOX, i - 1)
                probs_out(FOX, 7)
                split(n + 16)
                outputs_lo(FOX, 7)
                split(n + 17)
            if last_sub >= FFN4:
                between(FOX)
                ffn(FFN4)
            if last_sub > CONV:
                between(last_sub)

        @block.gpsimd
        def _(pool):
            step = [0]

            def link(ins):
                step[0] += 1
                ins.then_inc(pool_chain, 1)
                pool.wait_ge(pool_chain, step[0])

            pool.memset(ada_sum0, 0.0).then_inc(ada0_cleared, 1)
            pool.memset(eps[:, :], EPS)
            pool.memset(ones[:, :], 1.0)
            link(pool.memset(ident[:, :], 0.0))
            link(pool.affine_select(out=ident[:, :], in_=ident[:, :], compare_op=ALU.not_equal, fill=1.0, base=0,
                                    pattern=[[-1, P]], channel_multiplier=1))
            pool.affine_select(out=upper[:, :], in_=ones[:, :], compare_op=ALU.is_ge, fill=0.0, base=0,
                               pattern=[[1, P]], channel_multiplier=-1).then_inc(consts, 1)
            pool.memset(u_pad[:, :, :, 0:1], 0.0)
            pool.memset(u_pad[:, :, :, GRID_W + 1:GRID_W + 2], 0.0).then_inc(pads, 1)

            rest = len(ADA_SECTIONS) * 4

            def load_ada(r):
                section, k = ADA_SECTIONS[r // 4], 2 * (r % 4)
                pool.dma_start(ada_raw[:, r % ADA_REST_SLOTS, :, :], ada_w[:, k:k + 2, section * D:(section + 1) * D])\
                    .then_inc(ada_landed[r % ADA_REST_SLOTS], 16)

            pool.wait_ge(raw_done, ADA_FIRST - 3)
            for r in range(ADA_REST_SLOTS):
                load_ada(r)
            for i, section in enumerate(ADA_SECTIONS):
                acc = ada_acc if i % 2 else tmp[:, 1, :]
                if i != 1:
                    pool.wait_ge(ada_ps, 2 if i == 0 else i + 1)
                link(pool.memset(acc, 0.0))
                pool.dma_start(acc[0:1, :], w["ada_b"][:, section * D:(section + 1) * D]).then_inc(ada_b_landed, 16)
                pool.wait_ge(ada_b_landed, 16 * (i + 1))
                for u in range(4):
                    r = 4 * i + u
                    pool.wait_ge(ada_scaled, r + 1)
                    if r:
                        pool.wait_ge(ada_added, r)
                    link(pool.tensor_tensor(acc, ada_raw[:, r % ADA_REST_SLOTS, 0, :], acc, ALU.add))
                    pool.tensor_tensor(acc, ada_raw[:, r % ADA_REST_SLOTS, 1, :], acc, ALU.add).then_inc(ada_added, 1)
                    pool.wait_ge(ada_added, r + 1)
                    if r + ADA_REST_SLOTS < rest:
                        load_ada(r + ADA_REST_SLOTS)
                if i == 1:
                    pool.wait_ge(xn_done, 2)
                    pool.dma_start(rows[:, 0, :], w["norm2_g"].to_broadcast([P, D])).then_inc(g2_row_landed, 16)
            if last_sub >= AB:
                pool.wait_ge(ada_ps, 6)
                pool.wait_ge(x_new, x_count(CONV, 0, 0))
                pool.memset(a_pad[:, :, 0:CONV_K - 1], 0.0).then_inc(pads, 1)
                dist_i = pT_ab[:, 0, 0, :].bitcast(mybir.dt.int32)
                dist = pT_ab[:, 0, 1, :]
                pool.iota(dist_i[:, 0:P], pattern=[[-1, P]], base=0, channel_multiplier=1)
                link(pool.iota(dist_i[:, P:3 * P], pattern=[[-1, 2 * P]], base=P, channel_multiplier=1))
                link(pool.tensor_copy(dist, dist_i))
                for h in range(SWA_HQ):
                    slope = 2.0 ** (-8.0 * (h + 1) / SWA_HQ)
                    b0, b1 = alibi[:, h, 0:P], alibi[:, h, P:3 * P]
                    link(pool.tensor_scalar(alibi[:, h, :], dist, -slope, None, ALU.mult))
                    link(pool.affine_select(out=b1, in_=b1, compare_op=ALU.is_ge, fill=NEG, base=P,
                                            pattern=[[-1, 2 * P]], channel_multiplier=1))
                    pool.affine_select(out=b0, in_=b0, compare_op=ALU.is_ge, fill=NEG, base=0,
                                       pattern=[[-1, P]], channel_multiplier=1)
                    a = pool.affine_select(out=b1, in_=b1, compare_op=ALU.is_ge, fill=NEG, base=-1,
                                           pattern=[[1, 2 * P]], channel_multiplier=-1)
                a.then_inc(bias_built, 1)
            if last_sub >= FOX:
                for i in range(FOX_H // 2):
                    pool.wait_ge(d_raw_v if i % 2 else d_raw_a, i // 2 + 1)
                    for h in (2 * i, 2 * i + 1):
                        d = decay[:, h, :].rearrange("p (k s) -> p k s", k=3)[:, 0::2, :]
                        a = pool.affine_select(out=d, in_=d, compare_op=ALU.is_ge, fill=NEG, base=0,
                                               pattern=[[0, 2], [-1, P]], channel_multiplier=1)
                    a.then_inc(d_ok, 1)


_INS = ["x", "c", "ada_w", "ada_b", "norm1_g", "norm2_g", "conv_w_in", "conv_w", "conv_w_out", "ffn_w_in", "ffn_w_out",
        "final_g", "norm_g_2", "ffn_w_gate_2", "ffn_w_up_2", "ffn_w_down_2", "ab_w_in_2", "conv_w_2", "conv_b_2",
        "conv_ln_g_2", "conv_ln_b_2", "swa_sinks_2", "ab_w_out_2", "fox_w_in_2", "fox_b_f_2", "fox_w_out_2"]


def kernel(**inputs):
    import numpy as np
    from concourse import bacc
    from concourse.bass_utils import run_bass_kernel_spmd

    nc = bacc.Bacc("TRN2", target_bir_lowering=False, num_devices=1)
    arrays, args = {}, {}
    for name in _INS:
        a = np.ascontiguousarray(inputs[name])
        arrays[f"in_{name}"] = a
        args[name] = nc.dram_tensor(f"in_{name}", a.shape, mybir.dt.from_np(a.dtype), kind="ExternalInput").ap()
    out = nc.dram_tensor("out", (1, SEQ, D), F32, kind="ExternalOutput").ap()
    block_program(nc, out, **args)
    r = run_bass_kernel_spmd(nc, [arrays], core_ids=[0])
    return r.results[0]["out"]
```

```python
from contextlib import ExitStack

import concourse.bass as bass
from concourse import mybir

ALU = mybir.AluOpType
ACT = mybir.ActivationFunctionType
F32 = mybir.dt.float32
F32R = mybir.dt.float32r
AX_X = mybir.AxisListType.X

P = 128
SEQ = 256
TOKT = SEQ // P
D = 1024
KT = D // P
EPS = 1e-6
NEG = -1e30
SLOT = 2048
NSLOT = 3

FF = 2816
FCH = 256
NCH = FF // FCH
FFN_UNITS = 3 * NCH

ADA_FIRST = 8
GATE1, SHIFT2, SCALE2, GATE2 = 2, 3, 4, 5
ADA_V = (GATE1, SCALE2)
ADA_P = (SHIFT2, GATE2)
ADA_CH = KT // 2

CONV_CH = 512
CONV_K = 31
CCT = CONV_CH // P
DH = 64
SWA_HQ = 8
SWA_HKV = 2
FOX_H = 16
GRID_W = 64

CONV, FFN0, FFN1, AB, FFN2, FFN3, FOX, FFN4 = range(8)
UNITS = {CONV: 16, AB: 11, FOX: 16}
BASE = {}
_n = ADA_FIRST
for _s in range(8):
    BASE[_s] = _n
    _n += UNITS.get(_s, FFN_UNITS)
TOTAL = _n

C_CONVW, C_CB, C_LNG, C_LNB, C_PRE = 0, 24, 28, 32, 36
C_G1 = C_PRE + 4 * 8
N_PAR = C_G1 + 8
N_CW31 = CONV_K * CCT

POOL_C1 = 15
V_TAPS = [(k, c) for k in range(CONV_K) for c in (0, 1) if c == 0 or k < CONV_K - POOL_C1]
A_TAPS = [(k, c) for k in range(CONV_K) for c in (2, 1) if c == 2 or k >= CONV_K - POOL_C1]
PE_TAPS = (0, 7, 3, 3, 3, 3, 3, 3, 3, 3)
RING = 4


NORMED = (CONV, FFN0, AB, FOX)
FOLDED = (FFN1, FFN2, FFN3, FFN4)
FFNS = (FFN0,) + FOLDED


def x_count(b, t, h):
    return 4 * b + 2 * t + h + 1


def xn_count(s, t):
    return 2 * NORMED.index(s) + t + 1


def x_event(s):
    return s if s < 2 else s + 1


FINAL_EVENT = 2
STAT_Y = 18


def rows_count(b):
    return 16 * sum(1 + (i + 1 in NORMED) for i in range(FFN0, b + 1))


WARM_TURNED, WARM_FOLDED, WARM_FINAL, WARM_NORMED = 4, 5, 12, 18

LATE = [BASE[s] + 1 for s in range(FFN0, FFN4 + 1)]


def gain_column(n):
    for i, s in enumerate(FOLDED):
        o = n - BASE[s]
        if 0 <= o < FFN_UNITS - 1 and (o < 2 or o % 3 != 1):
            second = o == 1 or (o > 1 and o % 3 == 0)
            return C_PRE + 8 * i + (4 if second else 0)
    return None


def block_program(nc, out, **w):
    x_d = w["x"].rearrange("b (t p) d -> p (b t) d", p=P)
    out_d = out.rearrange("b (t p) d -> p (b t) d", p=P)
    ada_w = w["ada_w"].rearrange("l (kt p) n -> p (l kt) n", p=P)
    conv_in = w["conv_w_in"].rearrange("l (kt p) n -> p (l kt) n", p=P)
    conv_out = w["conv_w_out"].rearrange("l (kt p) n -> p (l kt) n", p=P)
    ab_in = w["ab_w_in_2"].rearrange("l (kt p) n -> p (l kt) n", p=P)
    ab_out = w["ab_w_out_2"].rearrange("l (kt p) n -> p (l kt) n", p=P)
    fox_in = w["fox_w_in_2"].rearrange("l (kt p) n -> p (l kt) n", p=P)
    fox_out = w["fox_w_out_2"].rearrange("l (kt p) n -> p (l kt) n", p=P)

    def ffn_weights(s):
        if s == FFN0:
            both = w["ffn_w_in"].rearrange("l (kt p) n -> p (l kt) n", p=P)
            return both[:, :, 0:FF], both[:, :, FF:2 * FF], \
                w["ffn_w_out"].rearrange("l (kt p) n -> p (l kt) n", p=P)
        layer, half = {FFN1: (0, 0), FFN2: (0, 1), FFN3: (1, 0), FFN4: (1, 1)}[s]
        return (w["ffn_w_gate_2"][layer, half].rearrange("(kt p) n -> p kt n", p=P),
                w["ffn_w_up_2"][layer, half].rearrange("(kt p) n -> p kt n", p=P),
                w["ffn_w_down_2"][layer, half].rearrange("(kt p) n -> p kt n", p=P))

    def norm_row(layer, i):
        return w["norm_g_2"][layer, i:i + 1, :].to_broadcast([P, D])

    PRE_ROW = {FFN1: (0, 0), AB: (0, 2), FFN2: (0, 4), FFN3: (1, 0), FOX: (1, 2), FFN4: (1, 4)}
    POST_ROW = {FFN1: (0, 1), AB: (0, 3), FFN2: (0, 5), FFN3: (1, 1), FOX: (1, 3), FFN4: (1, 5)}

    with ExitStack() as ctx:
        def sb(name, shape, dt=F32):
            return ctx.enter_context(nc.sbuf_tensor(name, shape, dt))

        def sem(name):
            return ctx.enter_context(nc.semaphore(name))

        ps = ctx.enter_context(nc.psum_tensor("ps", [P, 8, 512], F32))
        raw = sb("raw", [P, NSLOT, SLOT])
        w_hi = sb("w_hi", [P, NSLOT, SLOT], F32R)
        w_lo = sb("w_lo", [P, NSLOT, SLOT], F32R)
        x = sb("x_sb", [P, TOKT, D])
        tmp = sb("tmp", [P, TOKT, D])
        xn = sb("xn", [P, TOKT, D])
        xT_hi = sb("xT_hi", [P, KT, SEQ], F32R)
        xT_lo = sb("xT_lo", [P, KT, SEQ], F32R)
        yT_hi = sb("yT_hi", [P, KT, SEQ], F32R)
        yT_lo = sb("yT_lo", [P, KT, SEQ], F32R)
        sil = sb("sil", [P, TOKT, FCH])
        hid = sb("hid", [P, TOKT, FCH])
        hT_hi = sb("hT_hi", [P, 2, SEQ], F32R)
        hT_lo = sb("hT_lo", [P, 2, SEQ], F32R)
        rows = sb("rows", [P, 4, D])
        ident = sb("ident", [P, P])
        ones = sb("ones", [P, P])
        upper = sb("upper", [P, P])
        par_rows = sb("par_rows", [P, 2, P])
        par = sb("par", [P, N_PAR])
        cw31 = sb("cw31", [P, N_CW31])
        cond = sb("cond", [P, KT])
        eps = sb("eps", [P, 1])
        warm = sb("warm", [P, 28])
        mod = sb("mod", [P, 2, KT])
        stat = sb("stat", [P, 3, 32])
        sinks = sb("sinks", [P, SWA_HQ])
        b_f = sb("b_f", [P, FOX_H])
        soft = sb("soft", [P, 8, 64])
        zf = sb("zf", [P, 8, 2 * FOX_H])
        zf_hi = sb("zf_hi", [P, KT, FOX_H], F32R)
        zf_lo = sb("zf_lo", [P, KT, FOX_H], F32R)
        zf_raw = sb("zf_raw", [P, KT, FOX_H])
        cT = sb("cT", [FOX_H, SEQ])
        arena = sb("arena", [P, 11776])

        def part(at, *shape):
            n = 1
            for k in shape:
                n *= k
            assert at + n <= 11776
            ap = arena[:, at:at + n]
            if len(shape) == 1:
                return ap
            names = "abcd"[:len(shape)]
            return ap.rearrange(f"p ({' '.join(names)}) -> p {' '.join(names)}",
                                **dict(zip(names[1:], shape[1:])))

        ada_v_raw = part(0, 2, 2, D)
        ada_p_raw = [part(4096, 2, D), xn[:, :, :]]
        ada_acc = part(6144, D)
        cond_rows = part(7168, P)[0:KT, :]
        gate_c = part(7168, CCT, SEQ)
        u_pad = part(8192, CCT, SEQ // GRID_W, GRID_W + 2)
        conv_acc = part(9248, CCT, SEQ)
        conv_y = part(10272, CCT, SEQ)
        xnT = part(9248, KT, SEQ)
        alibi = part(0, SWA_HQ, 384)
        a_pad = part(3072, CCT, SEQ + CONV_K - 1)
        sig = part(4216, TOKT, CONV_CH)
        acc31 = part(5240, CCT, SEQ)
        q_ab = part(6264, CCT, SEQ)
        k_ab = part(7288, SWA_HKV, SEQ)
        v_ab = part(7800, TOKT, P)
        acc_p = part(11128, SEQ)
        diag = [(xn, tmp)[k // 16][:, :, :].rearrange("p t d -> p (t d)")[:, k % 16 * P:(k % 16 + 1) * P]
                for k in range(CONV_K)]
        ring = [b[:, t, :] for b in (sil, hid) for t in range(TOKT)]
        p_ab = part(8056, 2, 2, 384)
        pT_ab = part(9592, 2, 2, 384)
        ln_y = part(8056, TOKT, CONV_CH)
        ab_y = part(9592, CCT, SEQ)
        q_fox = part(0, KT, SEQ)
        k_fox = part(2048, KT, SEQ)
        decay = part(4096, FOX_H, 384)
        pT_fox = part(10240, 2, 2, 384)
        v_fox = tmp
        p_fox = xn[:, :, :].rearrange("p t d -> p (t d)")[:, 0:1536].rearrange(
            "p (b h s) -> p b h s", b=2, h=2)
        q_of = {AB: q_ab, FOX: q_fox}
        p_of = {AB: p_ab, FOX: p_fox}
        pT_of = {AB: pT_ab, FOX: pT_fox}
        ada_sum0 = tmp[:, :, :].rearrange("p t d -> p (t d)")

        landed = [sem(f"landed{i}") for i in range(NSLOT)]
        hi_ready = sem("hi_ready")
        hi_piece = sem("hi_piece")
        raw_done = sem("raw_done")
        w_used = sem("w_used")
        x_landed = sem("x_landed")
        par_landed = sem("par_landed")
        bias_landed = sem("bias_landed")
        mod_ps = sem("mod_ps")
        mod_ok = sem("mod_ok")
        xnT_ok = sem("xnT_ok")
        misc_landed = sem("misc_landed")
        consts = sem("consts")
        c_landed = sem("c_landed")
        c_ps = sem("c_ps")
        par_ps = sem("par_ps")
        par_ready = sem("par_ready")
        cond_ready = sem("cond_ready")
        ada_v_landed = [sem(f"ada_v_landed{i}") for i in range(2)]
        ada_v_bias = sem("ada_v_bias")
        ada_v_add = sem("ada_v_add")
        ada_p_landed = [sem(f"ada_p_landed{i}") for i in range(2)]
        ada_p_bias = sem("ada_p_bias")
        ada_p_done = sem("ada_p_done")
        ada_ps = sem("ada_ps")
        ada_row_a = sem("ada_row_a")
        ada_row_v = sem("ada_row_v")
        ada0_cleared = sem("ada0_cleared")
        g2_row_landed = sem("g2_row_landed")
        y_tok0 = sem("y_tok0")
        y_sq = sem("y_sq")
        y_std = sem("y_std")
        y_rstd = sem("y_rstd")
        x_sq = sem("x_sq")
        x_std = sem("x_std")
        x_rstd = sem("x_rstd")
        x_mid = sem("x_mid")
        t_done = sem("t_done")
        x_new = sem("x_new")
        xn_part = sem("xn_part")
        xn_done = sem("xn_done")
        xT_ps = sem("xT_ps")
        xT_hi_ok = sem("xT_hi_ok")
        xT_ok = sem("xT_ok")
        rows_landed = sem("rows_landed")
        out_landed = sem("out_landed")
        up_tok0 = sem("up_tok0")
        sil_done = sem("sil_done")
        hid_done = sem("hid_done")
        hT_ps = sem("hT_ps")
        hT_hi_ok = sem("hT_hi_ok")
        hT_ok = sem("hT_ok")
        evac_a = sem("evac_a")
        evac_v = sem("evac_v")
        pads = sem("pads")
        tap = sem("tap")
        a_tok0 = sem("a_tok0")
        glu_ps = sem("glu_ps")
        diag_ok = sem("diag_ok")
        prod_a = sem("prod_a")
        sum_p = sem("sum_p")
        conv_pe = sem("conv_pe")
        conv_done = sem("conv_done")
        yT_hi_ok = sem("yT_hi_ok")
        yT_ok = sem("yT_ok")
        bias_built = sem("bias_built")
        k_landed = sem("k_landed")
        ln_ps = sem("ln_ps")
        ln_stat = sem("ln_stat")
        ln_std = sem("ln_std")
        ln_out = sem("ln_out")
        lnT_ps = sem("lnT_ps")
        ab_y_ok = sem("ab_y_ok")
        s_ps = sem("s_ps")
        s_sb = sem("s_sb")
        m_chain = sem("m_chain")
        m_ok = sem("m_ok")
        e_done = sem("e_done")
        p_done = sem("p_done")
        pT_psd = sem("pT_psd")
        pT_okA = sem("pT_okA")
        pT_okV = sem("pT_okV")
        o_ps = sem("o_ps")
        oT_hi_ok = sem("oT_hi_ok")
        oT_ok = sem("oT_ok")
        zf_ok = sem("zf_ok")
        zf_v = sem("zf_v")
        zf_a = sem("zf_a")
        zf_p = sem("zf_p")
        zf_z = sem("zf_z")
        zf_e = sem("zf_e")
        pool_chain = sem("pool_chain")
        d_ps = sem("d_ps")
        d_raw_a = sem("d_raw_a")
        d_raw_v = sem("d_raw_v")
        d_ok = sem("d_ok")

        def slot_of(n):
            return n % NSLOT

        def weight_count(n):
            return n - ADA_FIRST + 1

        def y_unit(b):
            return BASE[b] + UNITS.get(b, FFN_UNITS) - 1

        first_item = {AB: 0, FOX: 4}
        out_kt = {AB: 4, FOX: 0}

        def item_bank(i):
            return 2 * ((i + 1) % 2)

        CONV_BANK = (6, 2, 4, 6, 2, 4)

        EVAC_AB = 11

        def ffn_index(s):
            return (FFN0, FFN1, FFN2, FFN3, FFN4).index(s)

        block = ctx.enter_context(nc.Block())

        @block.sync
        def _(sp):
            def load(n, j, dst_src):
                if not (isinstance(j, int) and n + NSLOT * j < NSLOT):
                    sp.wait_ge(raw_done, n - NSLOT + 1 + NSLOT * j)
                assert len(dst_src) == 2
                for dst, src in dst_src:
                    sp.dma_start(dst, src).then_inc(landed[slot_of(n)], 16)

            def columns(n, wd, k0, c0, width, kts=4):
                dst = raw[:, slot_of(n), 0:kts * width].rearrange("p (k c) -> p k c", k=kts)
                h = kts // 2
                return [(dst[:, i:i + h, :], wd[:, k0 + i:k0 + i + h, c0:c0 + width]) for i in (0, h)]

            def pair_rows(n, wd, k):
                dst = raw[:, slot_of(n), :].rearrange("p (k c) -> p k c", k=2)
                return [(dst[:, i:i + 1, :], wd[:, bass.ds(k + i, 1), :]) for i in range(2)]

            def up_unit(n, gate, up, k0, c0):
                dst = raw[:, slot_of(n), :].rearrange("p (k h c) -> p k h c", k=4, h=2)
                return [(dst[:, :, i, :], wd[:, k0:k0 + 4, bass.ds(c0, FCH)]) for i, wd in enumerate((gate, up))]

            def load_rows(s):
                if s in NORMED:
                    sp.wait_ge(xn_done, xn_count(s, 1))
                sp.wait_ge(x_new, x_count(s - 1, 1, 1))
                post = w["final_g"].rearrange("(a d) -> a d", a=1).to_broadcast([P, D]) if s == FFN0 \
                    else norm_row(*POST_ROW[s])
                sp.dma_start(rows[:, 1, :], post).then_inc(rows_landed, 16)
                if s + 1 in NORMED:
                    sp.dma_start(rows[:, 0, :], norm_row(*PRE_ROW[s + 1])).then_inc(rows_landed, 16)

            def load_ffn(s):
                gate, up, down = ffn_weights(s)
                n = BASE[s]
                load(n, 0, up_unit(n, gate, up, 0, 0))
                load(n + 1, 0, up_unit(n + 1, gate, up, 4, 0))
                with sp.Fori(1, NCH) as j:
                    load(n - 1, j, up_unit(n - 1, gate, up, 0, j * FCH))
                    load(n, j, up_unit(n, gate, up, 4, j * FCH))
                    load(n + 1, j, pair_rows(n + 1, down, j * 2 - 2))
                load_rows(s)
                load(n + FFN_UNITS - 1, 0, pair_rows(n + FFN_UNITS - 1, down, 2 * NCH - 2))

            for n in range(ADA_FIRST):
                load(n, 0, [(raw[:, slot_of(n), h * D:(h + 1) * D], ada_w[:, n, h * D:(h + 1) * D]) for h in range(2)])
                if n == 3:
                    sp.dma_start(x[:, :, :], x_d).then_inc(x_landed, 16)
            n = BASE[CONV]

            def load_ada_v(q):
                if not 0 <= q < 2 * ADA_CH:
                    return
                if q >= 2:
                    sp.wait_ge(ada_v_add, 2 * (q - 1))
                c0, k = ADA_V[q // ADA_CH] * D, 2 * (q % ADA_CH)
                sp.dma_start(ada_v_raw[:, q % 2, :, :], ada_w[:, k:k + 2, c0:c0 + D]).then_inc(ada_v_landed[q % 2], 16)

            for half in range(2):
                for section in (1, 2, 0):
                    for k0 in (0, 4):
                        load(n, 0, columns(n, conv_in, k0, section * D + half * 512, 512))
                        load_ada_v(n - BASE[CONV] - 3)
                        n += 1
            sp.dma_start(rows[:, 0, :], w["norm2_g"].to_broadcast([P, D])).then_inc(g2_row_landed, 16)
            for k in range(0, KT, 2):
                load(n, 0, pair_rows(n, conv_out, k))
                n += 1
            sp.dma_start(sinks[:, :], w["swa_sinks_2"].to_broadcast([P, SWA_HQ])).then_inc(misc_landed, 16)
            sp.dma_start(b_f[:, :], w["fox_b_f_2"].to_broadcast([P, FOX_H])).then_inc(misc_landed, 16)
            sp.dma_start(zf_raw[:, :, :], fox_in[:, :, 3 * D:3 * D + FOX_H]).then_inc(misc_landed, 16)
            load_ffn(FFN0)
            load_ffn(FFN1)
            n = BASE[AB]
            for c0 in (CONV_CH, 0):
                for k0 in (0, 4):
                    load(n, 0, columns(n, ab_in, k0, c0, 512))
                    n += 1
            for c0 in (1536, 2 * CONV_CH, 2 * CONV_CH + 256):
                load(n, 0, columns(n, ab_in, 0, c0, 256, kts=8))
                n += 1
            load_rows(AB)
            for k in (4, 6, 0, 2):
                load(n, 0, pair_rows(n, ab_out, k))
                n += 1
            load_ffn(FFN2)
            load_ffn(FFN3)
            n = BASE[FOX]
            for c0 in (2 * D, 2 * D + 512):
                for k0 in (0, 4):
                    load(n, 0, columns(n, fox_in, k0, c0, 512))
                    n += 1
            for c0 in range(0, D, 256):
                for section in (0, 1):
                    load(n, 0, columns(n, fox_in, 0, section * D + c0, 256, kts=8))
                    n += 1
            load_rows(FOX)
            for k in range(0, KT, 2):
                load(n, 0, pair_rows(n, fox_out, k))
                n += 1
            load_ffn(FFN4)
            for t in range(TOKT):
                for h in range(2):
                    sp.wait_ge(x_new, x_count(FFN4, t, h))
                    c = slice(h * 512, (h + 1) * 512)
                    sp.dma_start(out_d[:, t, c], x[:, t, c]).then_inc(out_landed, 16)
            sp.wait_ge(out_landed, 16 * 2 * TOKT)

        @block.tensor
        def _(pe):
            def product(o, a_hi, a_lo, b_hi, b_lo, first, last):
                pe.matmul(o, a_hi, b_lo, start=first, stop=False, skip_group_check=True)
                pe.matmul(o, a_hi, b_hi, start=False, stop=False, skip_group_check=True)
                return pe.matmul(o, a_lo, b_hi, start=False, stop=last, skip_group_check=True)

            def unit(n, j=0):
                pe.wait_ge(raw_done, n + 1 + NSLOT * j)
                return w_hi[:, slot_of(n), :], w_lo[:, slot_of(n), :]

            def tok(t):
                return slice(t * P, (t + 1) * P)

            def turn_x(s, t):
                if s in NORMED:
                    pe.wait_ge(xn_done, xn_count(s, t))
                for h in range(2):
                    if s in FOLDED:
                        pe.wait_ge(x_new, x_count(s - 1, t, h))
                    for k in range(4):
                        tr = pe.transpose(ps[:, 2 * t + h, tok(k)], (xn if s in NORMED else x)[:, t, tok(4 * h + k)], ident[:, :])
                    tr.then_inc(xT_ps, 1)

            def keep_warm(count, bank=3):
                for _ in range(count):
                    pe.matmul(ps[:, bank, 0:P], ones[:, :], ones[:, :], start=True, stop=True)

            def up_part(n, k0, t, j=0):
                hi, lo = unit(n, j)
                for k in range(4):
                    c = slice(k * 512, (k + 1) * 512)
                    mm = product(ps[:, t, :], xT_hi[:, k0 + k, tok(t)], xT_lo[:, k0 + k, tok(t)], hi[:, c], lo[:, c],
                                 k0 + k == 0, k0 + k == KT - 1)
                return mm

            def turn_hid(s, j):
                for f in range(2):
                    for t in range(TOKT):
                        tr = pe.transpose(ps[:, 2, f * SEQ + t * P:f * SEQ + (t + 1) * P], hid[:, t, tok(f)], ident[:, :])
                tr.then_inc(hT_ps, 1)

            def down_part(n, aT_hi, aT_lo, k0, t, first, last, j=0, ks=(0, 1)):
                hi, lo = unit(n, j)
                for k in ks:
                    for h in range(2):
                        c = slice(k * D + h * 512, k * D + (h + 1) * 512)
                        mm = product(ps[:, 4 + 2 * t + h, :], aT_hi[:, k0 + k, tok(t)], aT_lo[:, k0 + k, tok(t)],
                                     hi[:, c], lo[:, c], first and k == 0, last and k == 1)
                return mm

            def ffn(s):
                f, n = ffn_index(s), BASE[s]
                turn_x(s, 0)
                keep_warm(WARM_TURNED)
                pe.wait_ge(xT_ok, 4 * s + 1)
                up_part(n, 0, 0)
                turn_x(s, 1)
                pe.wait_ge(xT_ok, 4 * s + 2)
                up_part(n + 1, 4, 0).then_inc(up_tok0, 1)
                pe.wait_ge(xT_ok, 4 * s + 3)
                up_part(n, 0, 1).then_inc(w_used, 1)
                pe.wait_ge(xT_ok, 4 * s + 4)
                up_part(n + 1, 4, 1).then_inc(w_used, 1)

                def gate_row(h):
                    pe.matmul(ps[:, 3, :], ones[:, :], ada_acc[:, h * 512:(h + 1) * 512], start=True, stop=True).then_inc(ada_ps, 1)

                def chunk(n_a, j_hid, j, first):
                    pe.wait_ge(hid_done, 2 * NCH * f + 1 + 2 * j_hid)
                    up_part(n_a, 0, 0, j)
                    pe.wait_ge(hid_done, 2 * NCH * f + 2 + 2 * j_hid)
                    up_part(n_a, 0, 1, j).then_inc(w_used, 1)
                    turn_hid(s, j_hid)
                    up_part(n_a + 1, 4, 0, j).then_inc(up_tok0, 1)
                    up_part(n_a + 1, 4, 1, j).then_inc(w_used, 1)
                    pe.wait_ge(hT_ok, NCH * f + j_hid + 1)
                    down_part(n_a + 2, hT_hi, hT_lo, 0, 0, first, False, j)
                    down_part(n_a + 2, hT_hi, hT_lo, 0, 1, first, False, j).then_inc(w_used, 1)

                chunk(n + 2, 0, 0, True)
                with pe.Fori(1, NCH - 2) as i:
                    chunk(n + 2, i, i, False)
                last = n + FFN_UNITS - 1
                if s == FFN0:
                    pe.wait_ge(ada_p_done, 2 * ADA_CH)
                    gate_row(0)
                pe.wait_ge(hid_done, 2 * (NCH * f + NCH - 1) - 1)
                up_part(last - 3, 0, 0)
                pe.wait_ge(hid_done, 2 * (NCH * f + NCH - 1))
                up_part(last - 3, 0, 1).then_inc(w_used, 1)
                turn_hid(s, NCH - 2)
                up_part(last - 2, 4, 0).then_inc(up_tok0, 1)
                up_part(last - 2, 4, 1).then_inc(w_used, 1)
                if s == FFN0:
                    pe.wait_ge(ada_row_a, 3)
                    gate_row(1)
                pe.wait_ge(hT_ok, NCH * (f + 1) - 1)
                down_part(last - 1, hT_hi, hT_lo, 0, 0, False, False, ks=(0,))
                pe.wait_ge(hid_done, 2 * NCH * (f + 1))
                turn_hid(s, NCH - 1)
                down_part(last - 1, hT_hi, hT_lo, 0, 0, False, False, ks=(1,))
                down_part(last - 1, hT_hi, hT_lo, 0, 1, False, False).then_inc(w_used, 1)
                pe.wait_ge(hT_ok, NCH * (f + 1))
                down_part(last, yT_hi, yT_lo, 0, 0, False, True).then_inc(y_tok0, 1)
                down_part(last, yT_hi, yT_lo, 0, 1, False, True).then_inc(w_used, 1)
                if s != FFN4:
                    keep_warm(WARM_FOLDED if s + 1 in FOLDED and s > FFN0 else WARM_FINAL if s == FFN0 else WARM_NORMED)

            def channel_chunk(n, bank, ready=False):
                for u in range(2):
                    hi, lo = unit(n + u)
                    for k in range(4):
                        if ready and k % 2 == 0:
                            pe.wait_ge(xT_ok, 2 * u + k // 2 + 1)
                        for c in range(4):
                            w_k = [v[:, k * 512 + c * P:k * 512 + (c + 1) * P] for v in (hi, lo)]
                            mm = product(ps[:, bank + c // 2, (c % 2) * SEQ:(c % 2 + 1) * SEQ], *w_k,
                                         xT_hi[:, 4 * u + k, :], xT_lo[:, 4 * u + k, :],
                                         u == 0 and k == 0 and c % 2 == 0, u == 1 and k == 3)
                    mm.then_inc(w_used, 1)

            def token_part(n, second, bank, t):
                hi, lo = unit(n)
                for k in range(4):
                    c = slice(k * 512, (k + 1) * 512)
                    kt = 4 * second + k
                    mm = product(ps[:, bank, :], xT_hi[:, kt, tok(t)], xT_lo[:, kt, tok(t)], hi[:, c], lo[:, c],
                                 kt == 0, kt == KT - 1)
                return mm

            def pair_part(n, h, bank):
                hi, lo = unit(n)
                for k in range(4 * h, 4 * h + 4):
                    for c in range(2):
                        w_k = [v[:, k * 256 + c * P:k * 256 + (c + 1) * P] for v in (hi, lo)]
                        mm = product(ps[:, bank, c * SEQ:(c + 1) * SEQ], *w_k, xT_hi[:, k, :], xT_lo[:, k, :],
                                     k == 0 and c == 0, k == KT - 1)
                if h == 1:
                    mm.then_inc(w_used, 1)

            def row_everywhere(banks, acc):
                for h in range(2):
                    mm = pe.matmul(ps[:, banks + h, :], ones[:, :], acc[:, h * 512:(h + 1) * 512], start=True, stop=True)
                mm.then_inc(ada_ps, 1)

            def key(s, i):
                return k_ab[:, i // 2, :] if s == AB else k_fox[:, i, :]

            def value(s, i, g, b):
                c = i // 2 * DH if s == AB else (2 * i + g) * DH
                return (v_ab if s == AB else v_fox)[:, b, c:c + DH]

            def scores(s, i):
                if i >= 2:
                    pe.wait_ge(oT_ok, first_item[s] + i - 1)
                q = q_of[s]
                for g in range(2):
                    r = slice(g * DH, (g + 1) * DH)
                    pe.matmul(ps[:, item_bank(i) + g, 0:P], q[r, i, 0:P], key(s, i)[r, 0:P], start=True, stop=True)
                for g in range(2):
                    r = slice(g * DH, (g + 1) * DH)
                    mm = pe.matmul(ps[:, item_bank(i) + g, P:3 * P], q[r, i, P:SEQ], key(s, i)[r, :], start=True, stop=True)
                mm.then_inc(s_ps, 1)

            def turn_probs(s, i):
                pe.wait_ge(p_done, first_item[s] + i + 1)
                for g in range(2):
                    for b in range(3):
                        tr = pe.transpose(ps[:, item_bank(i) + g, tok(b)], p_of[s][:, i % 2, g, tok(b)], ident[:, :])
                tr.then_inc(pT_psd, 1)

            def head_outputs(s, i):
                pe.wait_ge(pT_okA, first_item[s] + i + 1)
                pe.wait_ge(pT_okV, first_item[s] + i + 1)
                for g in range(2):
                    pT = pT_of[s][:, i % 2, g, :]
                    r = slice(g * DH, (g + 1) * DH)
                    o_bank = item_bank(i)
                    pe.matmul(ps[r, o_bank, 0:P], value(s, i, g, 0), pT[:, 0:P], start=True, stop=True)
                    pe.matmul(ps[r, o_bank, P:SEQ], value(s, i, g, 0), pT[:, P:2 * P], start=True, stop=False)
                    mm = pe.matmul(ps[r, o_bank, P:SEQ], value(s, i, g, 1), pT[:, 2 * P:3 * P], start=False, stop=True)
                mm.then_inc(o_ps, 1)

            pe.wait_ge(consts, 1)
            pe.wait_ge(c_landed, 16)
            pe.transpose(ps[:, 5, 0:KT], cond_rows[:, :], ident[0:KT, 0:KT]).then_inc(c_ps, 1)
            pe.wait_ge(par_landed, 160)
            pe.transpose(ps[:, 6, 0:N_PAR], par_rows[0:N_PAR, 0, :], ident[0:N_PAR, 0:N_PAR])
            pe.transpose(ps[:, 7, 0:N_CW31], par_rows[0:N_CW31, 1, :], ident[0:N_CW31, 0:N_CW31]).then_inc(par_ps, 1)
            for t in range(TOKT):
                pe.wait_ge(xn_done, t + 1)
                for k in range(KT):
                    tr = pe.transpose(ps[:, k // 2, (k % 2) * SEQ + t * P:(k % 2) * SEQ + (t + 1) * P], xn[:, t, tok(k)], ident[:, :])
                    if t == 1 and k % 2:
                        tr.then_inc(xT_ps, 1)
            pe.wait_ge(raw_done, ADA_FIRST)
            for h in range(2):
                for part_k in (4 * h, KT + 4 * h):
                    for k in range(part_k, part_k + 4):
                        mm = pe.matmul(ps[:, 4 + h, k:k + 1], ada_sum0[:, k * P:(k + 1) * P], ones[:, 0:1], start=True, stop=True)
                mm.then_inc(mod_ps, 1)

            n = BASE[CONV]
            pe.wait_ge(par_ready, 3)
            for m in range(6):
                if m == 3:
                    pe.wait_ge(evac_a, 1)
                if m > 3:
                    pe.wait_ge(evac_v, m - 3)
                channel_chunk(n + 2 * m, CONV_BANK[m], ready=m == 0)
                if m == 3:
                    pe.wait_ge(ada_v_add, 2 * ADA_CH)
                    row_everywhere(0, tmp[:, 0, :])
            pe.wait_ge(ada_row_a, 1)
            pe.wait_ge(ada_v_add, 4 * ADA_CH)
            row_everywhere(0, tmp[:, 1, :])
            pe.wait_ge(evac_v, 4)
            pe.wait_ge(evac_a, 2)
            for i in range(4):
                pe.wait_ge(yT_ok, i // 2 + 1)
                first, last = i == 0, i == 3
                mm = down_part(n + 12 + i, yT_hi, yT_lo, 2 * i, 0, first, last)
                if last:
                    mm.then_inc(y_tok0, 1)
                down_part(n + 12 + i, yT_hi, yT_lo, 2 * i, 1, first, last).then_inc(w_used, 1)
                if i == 2:
                    pe.wait_ge(ada_p_done, ADA_CH)
                    row_everywhere(2, ada_acc)

            ffn(FFN0)
            ffn(FFN1)
            n = BASE[AB]
            turn_x(AB, 0)
            keep_warm(WARM_TURNED)
            pe.wait_ge(xT_ok, 4 * AB + 1)
            token_part(n, 0, 4, 0)
            turn_x(AB, 1)
            pe.wait_ge(xT_ok, 4 * AB + 2)
            token_part(n + 1, 1, 4, 0)
            pe.wait_ge(xT_ok, 4 * AB + 3)
            token_part(n, 0, 5, 1).then_inc(w_used, 1)
            pe.wait_ge(xT_ok, 4 * AB + 4)
            token_part(n + 1, 1, 5, 1).then_inc(w_used, 1)
            token_part(n + 2, 0, 6, 0)
            token_part(n + 3, 1, 6, 0).then_inc(a_tok0, 1)
            token_part(n + 2, 0, 7, 1).then_inc(w_used, 1)

            def turn_glu(t):
                pe.wait_ge(evac_v, 5 + t)
                for c in range(CCT):
                    tr = pe.transpose(ps[:, t, tok(c)], sig[:, t, tok(c)], ident[:, :])
                tr.then_inc(glu_ps, 1)

            turn_glu(0)
            token_part(n + 3, 1, 7, 1).then_inc(w_used, 1)
            hi, lo = unit(n + 4)
            for k in range(KT):
                product(ps[:, 2, 0:SEQ], hi[:, k * 256:k * 256 + P], lo[:, k * 256:k * 256 + P], xT_hi[:, k, :], xT_lo[:, k, :],
                        k == 0, k == KT - 1)
            turn_glu(1)
            for t in range(TOKT):
                for k in range(KT):
                    c = slice(k * 256 + P, (k + 1) * 256)
                    mm = product(ps[:, 3, tok(t)], xT_hi[:, k, tok(t)], xT_lo[:, k, tok(t)], hi[:, c], lo[:, c],
                                 k == 0, k == KT - 1)
            mm.then_inc(w_used, 1)
            pair_part(n + 5, 0, 4)
            pair_part(n + 5, 1, 4)

            def long_conv(k0, k1):
                for k in range(k0, min(k1, CONV_K)):
                    mm = pe.matmul(ps[:, 6, 0:SEQ], diag[k], a_pad[:, 3, k:k + SEQ], start=k == 0, stop=k == CONV_K - 1)
                if k1 >= CONV_K > k0:
                    mm.then_inc(conv_pe, 1)

            def beside(i):
                if i == 0:
                    pair_part(n + 6, 0, 5)
                elif i == 1:
                    pair_part(n + 6, 1, 5)
                if i:
                    long_conv(sum(PE_TAPS[:i]), sum(PE_TAPS[:i + 1]))

            pe.wait_ge(evac_a, 9)
            pe.wait_ge(k_landed, 32)
            pe.wait_ge(diag_ok, 1)
            for i in range(5):
                if i:
                    turn_probs(AB, i - 1)
                if i == 2:
                    pe.wait_ge(evac_a, 10)
                if i < 4:
                    scores(AB, i)
                beside(2 * i)
                if i:
                    head_outputs(AB, i - 1)
                beside(2 * i + 1)
            pe.wait_ge(oT_ok, 4)
            down_part(n + 7, yT_hi, yT_lo, 4, 0, True, False)
            pe.wait_ge(evac_a, 11)
            pe.wait_ge(conv_done, 1)
            for t in range(TOKT):
                for c in range(CCT):
                    tr = pe.transpose(ps[:, t, tok(c)], acc31[:, c, tok(t)], ident[:, :])
                tr.then_inc(ln_ps, 1)

            def out_unit(u, kt):
                first, last = False, u == 10
                mm = down_part(n + u, yT_hi, yT_lo, kt, 0, first, last)
                if last:
                    mm.then_inc(y_tok0, 1)
                down_part(n + u, yT_hi, yT_lo, kt, 1, first, last).then_inc(w_used, 1)

            down_part(n + 7, yT_hi, yT_lo, 4, 1, True, False).then_inc(w_used, 1)
            for t in range(TOKT):
                pe.wait_ge(ln_out, t + 1)
                for c in range(CCT):
                    tr = pe.transpose(ps[:, 2 + c // 2, (c % 2) * SEQ + t * P:(c % 2) * SEQ + (t + 1) * P],
                                      ln_y[:, t, tok(c)], ident[:, :])
                tr.then_inc(lnT_ps, 1)
            out_unit(8, 6)
            pe.wait_ge(yT_ok, 3)
            out_unit(9, 0)
            out_unit(10, 2)
            ffn(FFN2)
            ffn(FFN3)
            n = BASE[FOX]
            logf = zf[:, 5, :]
            c_tok = zf[:, 6, :]

            def value_part(u, t):
                mm = token_part(n + u, u % 2, 4 + 2 * (u // 2) + t, t)
                if t == 1:
                    mm.then_inc(w_used, 1)

            def head_part(u, h):
                if h == 0:
                    pe.wait_ge(evac_a, EVAC_AB + (1 if u < 6 else 2 if u < 8 else u - 5))
                pair_part(n + u, h, 4 + u % 4)

            def distance_rows(i):
                if i >= 2:
                    pe.wait_ge(d_raw_v if i % 2 else d_raw_a, i // 2)
                for g in range(2):
                    h = 2 * i + g
                    mm = pe.matmul(ps[:, i % 2, g * SEQ:(g + 1) * SEQ],
                                   ident[0:FOX_H, h:h + 1].to_broadcast([FOX_H, P]), cT[:, :], start=True, stop=True)
                mm.then_inc(d_ps, 1)

            turn_x(FOX, 0)
            keep_warm(WARM_TURNED)
            pe.wait_ge(xT_ok, 4 * FOX + 1)
            value_part(0, 0)
            turn_x(FOX, 1)
            pe.wait_ge(xT_ok, 4 * FOX + 2)
            value_part(1, 0)
            pe.wait_ge(xT_ok, 4 * FOX + 3)
            value_part(0, 1)
            pe.wait_ge(xT_ok, 4 * FOX + 4)
            pe.wait_ge(zf_ok, 2)
            for t in range(TOKT):
                for k in range(KT):
                    mm = product(ps[:, 0, t * FOX_H:(t + 1) * FOX_H], xT_hi[:, k, tok(t)], xT_lo[:, k, tok(t)],
                                 zf_hi[:, k, :], zf_lo[:, k, :], k == 0, k == KT - 1)
            mm.then_inc(zf_p, 1)
            value_part(1, 1)
            value_part(2, 0)
            pe.wait_ge(zf_v, 1)
            pe.matmul(ps[:, 0, 64:80], upper[:, :], logf[:, 0:16], start=True, stop=True)
            pe.matmul(ps[:, 0, 80:96], upper[:, :], logf[:, 16:32], start=True, stop=False)
            pe.matmul(ps[:, 0, 80:96], ones[:, :], logf[:, 0:16], start=False, stop=True).then_inc(zf_p, 1)
            value_part(2, 1)
            pe.wait_ge(zf_a, 1)
            for t in range(TOKT):
                tr = pe.transpose(ps[0:FOX_H, 0, P + t * P:P + (t + 1) * P], c_tok[:, t * 16:(t + 1) * 16], ident[:, :])
            tr.then_inc(zf_p, 1)
            value_part(3, 0)
            pe.wait_ge(zf_a, 2)
            distance_rows(0)
            distance_rows(1)
            value_part(3, 1)
            head_part(4, 0)
            distance_rows(2)
            distance_rows(3)
            head_part(4, 1)
            distance_rows(4)
            distance_rows(5)
            head_part(5, 0)
            distance_rows(6)
            distance_rows(7)
            head_part(5, 1)

            def out_part(u, t):
                pe.wait_ge(oT_ok, 4 + 2 * (u - 12) + 2)
                mm = down_part(n + u, yT_hi, yT_lo, 2 * (u - 12), t, u == 12, u == 15)
                if t == 1:
                    mm.then_inc(w_used, 1)
                elif u == 15:
                    mm.then_inc(y_tok0, 1)

            for i in range(FOX_H // 2 + 1):
                part_of = head_part if i < 6 else out_part
                if i:
                    turn_probs(FOX, i - 1)
                if i < FOX_H // 2:
                    if i == 1:
                        pe.wait_ge(d_raw_a, 4)
                        pe.wait_ge(d_raw_v, 4)
                    pe.wait_ge(evac_a, EVAC_AB + 2 + 2 * (i // 2 + 1))
                    scores(FOX, i)
                if i == 6:
                    pe.wait_ge(evac_a, EVAC_AB + 10)
                part_of(6 + i, 0)
                if i:
                    head_outputs(FOX, i - 1)
                part_of(6 + i, 1)
            out_part(15, 0)
            out_part(15, 1)
            ffn(FFN4)

        @block.scalar
        def _(act):
            warmed = [0]

            def warm_up(func):
                c = warmed[0]
                warmed[0] += 1
                act.activation(warm[:, c:c + 1], eps[:, 0:1], func)

            def split(n, j=0, wait_used=True):
                v = weight_count(n) - 1
                if n >= TOTAL:
                    return
                act.wait_ge(landed[slot_of(n)], 32 * (n // NSLOT + 1 + j) if isinstance(j, int) else j * 32 + 32 * (n // NSLOT + 1))
                if not (isinstance(j, int) and v + NSLOT * j < NSLOT):
                    act.wait_ge(w_used, v - NSLOT + 1 + NSLOT * j)
                g = gain_column(n)
                if g is None:
                    act.activation(w_hi[:, slot_of(n), :], raw[:, slot_of(n), :], ACT.Copy).then_inc(hi_ready, 1)
                else:
                    for k in range(4):
                        c = slice(k * 512, (k + 1) * 512)
                        a = act.activation(w_hi[:, slot_of(n), c], raw[:, slot_of(n), c], ACT.Copy, scale=par[:, g + k:g + k + 1])
                    a.then_inc(hi_ready, 1)

            def split_late(n):
                if n >= TOTAL:
                    return
                act.wait_ge(landed[slot_of(n)], 32 * (n // NSLOT + 1))
                act.wait_ge(w_used, weight_count(n) - NSLOT)
                g = gain_column(n)
                for k in range(4):
                    c = slice(k * 512, (k + 1) * 512)
                    act.activation(w_hi[:, slot_of(n), c], raw[:, slot_of(n), c], ACT.Copy,
                                   scale=1.0 if g is None else par[:, g + k:g + k + 1]).then_inc(hi_ready if k == 3 else hi_piece, 1)

            def square_root(c, src, junk, sq, std, count):
                act.activation(junk, src, ACT.Square, scale=D ** -0.5, accum_out=stat[:, 0, c:c + 1]).then_inc(sq, 1)
                act.wait_ge(sq, count)
                act.activation(stat[:, 1, c:c + 1], stat[:, 0, c:c + 1], ACT.Sqrt, bias=eps[:, 0:1]).then_inc(std, 1)

            def root_y(b, t):
                act.wait_ge(w_used if t else y_tok0, weight_count(y_unit(b)) if t else b + 1)
                e = 2 * (b - FFN1) + t
                square_root(STAT_Y + e, ps[:, 4 + 2 * t:6 + 2 * t, :].rearrange("p b n -> p (b n)"), xn[:, t, :],
                            y_sq, y_std, e + 1)

            def root_x(e, t):
                square_root(2 * e + t, x[:, t, :], (tmp if e else xn)[:, t, :], x_sq, x_std, 2 * e + t + 1)

            def turned_hi(s, t):
                for h in range(2):
                    act.wait_ge(xT_ps, 4 * s + 2 * t + h + 1)
                    act.activation(xT_hi[:, 4 * h:4 * h + 4, t * P:(t + 1) * P],
                                   ps[:, 2 * t + h, :].rearrange("p (k c) -> p k c", k=4), ACT.Copy).then_inc(xT_hi_ok, 1)

            def between(b, func=None):
                s = b + 1
                if b not in FFNS:
                    warm_up(ACT.Sqrt)

                def before(t):
                    act.wait_ge(x_new, x_count(b, t, 1))
                    root_x(x_event(s), t)

                def after(t):
                    if b == FFN0:
                        act.wait_ge(x_mid, t + 1)
                        root_x(FINAL_EVENT, t)
                    elif b > FFN0:
                        root_y(b, t)

                if s in FOLDED:
                    after(0)
                    turned_hi(s, 0)
                    after(1)
                    before(0)
                    split(BASE[s] + 2)
                    turned_hi(s, 1)
                    before(1)
                elif s in NORMED:
                    after(0)
                    before(0)
                    after(1)
                    turned_hi(s, 0)
                    before(1)
                    split(BASE[s] + 2)
                    turned_hi(s, 1)
                else:
                    after(0)
                    after(1)
                if func is not None:
                    warm_up(func)

            def ffn(s):
                f, n = ffn_index(s), BASE[s]
                v = weight_count(n)

                def gates(j):
                    for t in range(TOKT):
                        if t == 0:
                            act.wait_ge(up_tok0, NCH * f + 1 + j)
                        else:
                            act.wait_ge(w_used, v + 1 if isinstance(j, int) and j == 0 else v + 3 * j)
                        c = 2 * x_event(s) + t
                        act.activation(sil[:, t, :], ps[:, t, 0:FCH], ACT.Silu,
                                       scale=stat[:, 2, c:c + 1] if s in FOLDED else 1.0).then_inc(sil_done, 1)

                def turned(j, dst):
                    act.wait_ge(hT_ps, NCH * f + 1 + j)
                    act.activation(dst, ps[:, 2, :].rearrange("p (f c) -> p f c", f=2), ACT.Copy).then_inc(hT_hi_ok, 1)

                def chunk(j):
                    if not (isinstance(j, int) and j == 0):
                        split(n + 2, j)
                    gates(j)
                    split(n + 3, j)
                    split(n + 4, j)
                    turned(j, hT_hi[:, :, :])

                if s in FOLDED:
                    act.wait_ge(x_rstd, 2 * x_event(s) + 2)
                chunk(0)
                with act.Fori(1, NCH - 1) as j:
                    chunk(j)

                def gate_row(h):
                    act.wait_ge(ada_ps, 4 + h)
                    act.activation(rows[:, 2, h * 512:(h + 1) * 512], ps[:, 3, :], ACT.Copy).then_inc(ada_row_a, 1)

                if s == FFN0:
                    gate_row(0)
                split(n + FFN_UNITS - 1)
                gates(NCH - 1)
                if s == FFN0:
                    gate_row(1)
                warm_up(ACT.Sqrt)
                turned(NCH - 1, yT_hi[:, 0:2, :])
                split(n + FFN_UNITS)
                split_late(n + FFN_UNITS + 1)

            act.dma_start(cond_rows[:, :], w["c"].rearrange("b (r q) -> (b r) q", q=P)).then_inc(c_landed, 16)
            act.wait_ge(ada0_cleared, 1)
            act.dma_start(ada_sum0[0:1, :], w["ada_b"][:, 0:2 * D]).then_inc(bias_landed, 16)
            warm_up(ACT.Silu)
            act.wait_ge(c_ps, 1)
            act.activation(cond[:, :], ps[:, 5, 0:KT], ACT.Silu).then_inc(par_ready, 1)
            act.dma_start(par_rows[C_CONVW:C_CONVW + 24, 0, :], w["conv_w"].rearrange("l k (r q) -> (l k r) q", q=P)).then_inc(par_landed, 16)
            act.dma_start(par_rows[C_CB:C_CB + 4, 0, :], w["conv_b_2"].rearrange("l (r q) -> (l r) q", q=P)).then_inc(par_landed, 16)
            act.dma_start(par_rows[C_LNG:C_LNG + 4, 0, :], w["conv_ln_g_2"].rearrange("l (r q) -> (l r) q", q=P)).then_inc(par_landed, 16)
            act.dma_start(par_rows[C_LNB:C_LNB + 4, 0, :], w["conv_ln_b_2"].rearrange("l (r q) -> (l r) q", q=P)).then_inc(par_landed, 16)
            for i, s in enumerate(FOLDED):
                layer, row = PRE_ROW[s]
                act.dma_start(par_rows[C_PRE + 8 * i:C_PRE + 8 * i + 8, 0, :],
                             w["norm_g_2"][layer, row, :].rearrange("(r q) -> r q", q=P)).then_inc(par_landed, 16)
            act.dma_start(par_rows[0:N_CW31, 1, :], w["conv_w_2"].rearrange("l k (r q) -> (l k r) q", q=P)).then_inc(par_landed, 16)
            act.dma_start(par_rows[C_G1:C_G1 + 8, 0, :], w["norm1_g"].rearrange("l (r q) -> (l r) q", q=P)).then_inc(par_landed, 16)
            act.wait_ge(par_ps, 1)
            act.wait_ge(consts, 1)
            act.activation(par[:, :], ps[:, 6, 0:N_PAR], ACT.Copy).then_inc(par_ready, 1)
            act.activation(cw31[:, :], ps[:, 7, 0:N_CW31], ACT.Copy).then_inc(par_ready, 1)
            act.wait_ge(par_ready, 3)
            act.wait_ge(x_landed, 16)
            for t in range(TOKT):
                root_x(0, t)
            split(BASE[CONV])
            for k in range(0, KT, 2):
                act.wait_ge(xnT_ok, k // 2 + 1)
                act.activation(xT_hi[:, k:k + 2, :], xnT[:, k:k + 2, :], ACT.Copy).then_inc(xT_hi_ok, 1)
                if k == 0:
                    split(BASE[CONV] + 1)

            n = BASE[CONV]
            for k in range(2, 18):
                m = (k - 4) // 2
                if k % 2 == 0 and 0 <= m < 6:
                    act.wait_ge(w_used, weight_count(n + 2 * m + 1))
                    if m % 3 == 0:
                        if m == 3:
                            act.wait_ge(evac_v, 1)
                        act.activation(gate_c[:, :, :].rearrange("p a b -> p (a b)"),
                                       ps[:, 6:8, :].rearrange("p b n -> p (b n)"), ACT.Copy).then_inc(evac_a, 1)
                    if m % 3 == 2:
                        h = m // 3
                        act.wait_ge(evac_v, 2 * h + 2)
                        act.activation(yT_hi[:, 4 * h:4 * h + 4, :], conv_y[:, :, :], ACT.Copy).then_inc(yT_hi_ok, 1)
                if k < 17:
                    split(n + k)
                else:
                    split_late(n + k)
                if k == 11:
                    act.wait_ge(ada_ps, 1)
                    act.activation(rows[:, 1, :], ps[:, 0:2, :].rearrange("p b n -> p (b n)"), ACT.Copy).then_inc(ada_row_a, 1)
            act.wait_ge(ada_ps, 3)
            act.activation(rows[:, 3, :], ps[:, 2:4, :].rearrange("p b n -> p (b n)"), ACT.Copy).then_inc(ada_row_a, 1)

            def exps(s, i):
                item = first_item[s] + i
                c = 4 * item
                act.wait_ge(m_ok, item + 1)
                for b in range(2):
                    for g in range(2):
                        a = c + 2 * b + g
                        d = p_of[s][:, i % 2, g, 0:P] if b == 0 else p_of[s][:, i % 2, g, P:3 * P]
                        e = act.activation(d, d, ACT.Exp, bias=soft[:, 1, a:a + 1], accum_out=soft[:, 3, a:a + 1])
                if s == AB:
                    e = act.activation(soft[:, 5, c:c + 4], soft[:, 2, c:c + 4], ACT.Exp)
                e.then_inc(e_done, 1)

            def probs_out(s, i):
                act.wait_ge(pT_psd, first_item[s] + i + 1)
                act.activation(pT_of[s][:, i % 2, 0, :], ps[:, item_bank(i), 0:384], ACT.Copy).then_inc(pT_okA, 1)

            def outputs_hi(s, i):
                act.wait_ge(o_ps, first_item[s] + i + 1)
                act.activation(yT_hi[:, out_kt[s] + i, :], ps[:, item_bank(i), 0:SEQ], ACT.Copy).then_inc(oT_hi_ok, 1)

            between(CONV, ACT.Silu)
            ffn(FFN0)
            between(FFN0, ACT.Silu)
            ffn(FFN1)
            between(FFN1, ACT.Sigmoid)
            n = BASE[AB]
            multiplied = [0]

            def multiply(count):
                for m in range(multiplied[0], min(multiplied[0] + count, len(A_TAPS))):
                    k, c = A_TAPS[m]
                    if m >= RING:
                        act.wait_ge(sum_p, m - RING + 1)
                    w_kc = cw31[:, k * CCT + c:k * CCT + c + 1]
                    bias = par[:, C_CB + c:C_CB + c + 1] if k == 0 else 0.0
                    act.activation(ring[m % RING], a_pad[:, c, k:k + SEQ], ACT.Identity, scale=w_kc, bias=bias).then_inc(prod_a, 1)
                multiplied[0] = min(multiplied[0] + count, len(A_TAPS))

            def padded(t):
                act.wait_ge(glu_ps, t + 1)
                act.activation(a_pad[:, :, CONV_K - 1 + t * P:CONV_K - 1 + (t + 1) * P],
                               ps[:, t, :].rearrange("p (c n) -> p c n", c=CCT), ACT.Copy).then_inc(evac_a, 1)

            def queries_out(u):
                act.wait_ge(w_used, weight_count(n + u))
                i = 2 * (u - 5)
                act.activation(q_ab[:, i:i + 2, :], ps[:, u - 1, :].rearrange("p (a c) -> p a c", a=2),
                               ACT.Copy).then_inc(evac_a, 1)

            split(n + 3)
            act.wait_ge(w_used, weight_count(n + 1))
            act.activation(sig.rearrange("p a b -> p (a b)"), ps[:, 4:6, :].rearrange("p b n -> p (b n)"),
                           ACT.Sigmoid).then_inc(evac_a, 1)
            warm_up(ACT.Exp)
            split(n + 4)
            split(n + 5)
            act.wait_ge(pads, 2)
            padded(0)
            split(n + 6)
            padded(1)
            act.wait_ge(evac_a, 5)
            multiply(10)
            act.wait_ge(w_used, weight_count(n + 4))
            for g in range(SWA_HKV):
                r = slice(g * DH, (g + 1) * DH)
                act.activation(k_ab[r, g, :], ps[r, 2, 0:SEQ], ACT.Copy).then_inc(evac_a, 1)
            act.wait_ge(evac_a, 7)
            act.dma_start(k_ab[DH:P, 0, :], k_ab[0:DH, 0, :]).then_inc(k_landed, 16)
            act.dma_start(k_ab[0:DH, 1, :], k_ab[DH:P, 1, :]).then_inc(k_landed, 16)
            act.activation(v_ab.rearrange("p a b -> p (a b)"), ps[:, 3, 0:SEQ], ACT.Copy).then_inc(evac_a, 1)
            queries_out(5)
            split(n + 7)
            for i in range(5):
                if i == 1:
                    queries_out(6)
                if i:
                    probs_out(AB, i - 1)
                multiply(2)
                if i < 4:
                    exps(AB, i)
                multiply(2)
                if i:
                    outputs_hi(AB, i - 1)
                if i < 2:
                    split(n + 8 + i)
                multiply(3)
            multiply(len(A_TAPS))
            act.wait_ge(conv_pe, 1)
            act.activation(acc31[:, 3, :], ps[:, 6, 0:SEQ], ACT.Identity, bias=par[:, C_CB + 3:C_CB + 4]).then_inc(evac_a, 1)
            warm_up(ACT.Sqrt)
            for t in range(TOKT):
                act.wait_ge(ln_stat, t + 1)
                act.activation(zf[:, 7, 8 * t + 2:8 * t + 3], zf[:, 7, 8 * t + 1:8 * t + 2], ACT.Sqrt, bias=eps[:, 0:1]).then_inc(ln_std, 1)
            warm_up(ACT.Silu)
            act.wait_ge(lnT_ps, 2)
            for c in range(CCT):
                a = act.activation(ab_y[:, c, :], ps[:, 2 + c // 2, (c % 2) * SEQ:(c % 2 + 1) * SEQ], ACT.Silu,
                                   scale=par[:, C_LNG + c:C_LNG + c + 1], bias=par[:, C_LNB + c:C_LNB + c + 1])
            a.then_inc(ab_y_ok, 1)
            act.wait_ge(ab_y_ok, 1)
            act.activation(yT_hi[:, 0:4, :], ab_y, ACT.Copy).then_inc(yT_hi_ok, 1)
            split(n + 10)
            split(n + 11)
            split_late(n + 12)
            between(AB, ACT.Silu)
            ffn(FFN2)
            between(FFN2, ACT.Silu)
            ffn(FFN3)
            between(FFN3, ACT.Exp)
            n = BASE[FOX]
            act.wait_ge(zf_z, 1)
            act.activation(zf[:, 2, :], zf[:, 1, :], ACT.Exp, scale=-1.0).then_inc(zf_e, 1)
            act.wait_ge(zf_e, 1)
            act.activation(zf[:, 3, :], zf[:, 2, :], ACT.Ln, bias=1.0).then_inc(zf_e, 1)

            def distances(i):
                act.wait_ge(d_ps, i + 1)
                for g in range(2):
                    h = 2 * i + g
                    src = ps[:, 0, g * SEQ:(g + 1) * SEQ]
                    act.activation(decay[:, h, 0:P], src[:, 0:P], ACT.Identity, bias=zf[:, 6, h:h + 1])
                    a = act.activation(decay[:, h, P:3 * P], src, ACT.Identity, bias=zf[:, 6, 16 + h:17 + h])
                a.then_inc(d_raw_a, 1)

            def values_out(h):
                act.wait_ge(w_used, weight_count(n + 2 * h + 1))
                act.activation(v_fox[:, :, h * 512:(h + 1) * 512], ps[:, 4 + 2 * h:6 + 2 * h, :], ACT.Copy).then_inc(evac_a, 1)

            def heads_out(u):
                act.wait_ge(w_used, weight_count(n + u))
                i = 2 * ((u - 4) // 2)
                act.activation((k_fox if u % 2 else q_fox)[:, i:i + 2, :],
                               ps[:, 4 + u % 4, :].rearrange("p (a c) -> p a c", a=2), ACT.Copy).then_inc(evac_a, 1)

            split(n + 3)
            values_out(0)
            split(n + 4)
            act.wait_ge(zf_p, 2)
            act.activation(zf[:, 6, :], ps[:, 0, 64:96], ACT.Copy).then_inc(zf_a, 1)
            act.wait_ge(zf_p, 3)
            act.activation(cT[:, :], ps[0:FOX_H, 0, P:P + SEQ], ACT.Copy, scale=-1.0).then_inc(zf_a, 1)
            split(n + 5)
            act.wait_ge(zf_a, 1)
            distances(0)
            values_out(1)
            split(n + 6)
            distances(2)
            heads_out(4)
            split(n + 7)
            distances(4)
            distances(6)
            for i in range(FOX_H // 2):
                if i < 7:
                    heads_out(5 + i)
                if i:
                    probs_out(FOX, i - 1)
                split(n + 8 + i)
                exps(FOX, i)
                if i:
                    outputs_hi(FOX, i - 1)
            probs_out(FOX, 7)
            split(n + 16)
            outputs_hi(FOX, 7)
            split_late(n + 17)
            between(FOX, ACT.Silu)
            ffn(FFN4)
            between(FFN4)

        @block.vector
        def _(dve):
            chained = [0]

            def link(ins):
                chained[0] += 1
                ins.then_inc(m_chain, 1)
                dve.wait_ge(m_chain, chained[0])

            def split(n, j=0):
                if n >= TOTAL:
                    return
                dve.wait_ge(hi_ready, weight_count(n) + NSLOT * j)
                g = gain_column(n)
                if g is None:
                    dve.tensor_tensor(w_lo[:, slot_of(n), :], raw[:, slot_of(n), :], w_hi[:, slot_of(n), :].bitcast(F32),
                                      ALU.subtract).then_inc(raw_done, 1)
                else:
                    for k in range(4):
                        c = slice(k * 512, (k + 1) * 512)
                        o = dve.scalar_tensor_tensor(w_lo[:, slot_of(n), c], raw[:, slot_of(n), c], par[:, g + k:g + k + 1],
                                                     w_hi[:, slot_of(n), c].bitcast(F32), ALU.mult, ALU.subtract)
                    o.then_inc(raw_done, 1)

            def split_piece(n, pieces):
                if n >= TOTAL:
                    return
                g = gain_column(n)
                for k in pieces:
                    if k == 3:
                        dve.wait_ge(hi_ready, weight_count(n))
                    else:
                        dve.wait_ge(hi_piece, 3 * LATE.index(n) + k + 1)
                    c = slice(k * 512, (k + 1) * 512)
                    lo, v, hi = w_lo[:, slot_of(n), c], raw[:, slot_of(n), c], w_hi[:, slot_of(n), c].bitcast(F32)
                    if g is None:
                        o = dve.tensor_tensor(lo, v, hi, ALU.subtract)
                    else:
                        o = dve.scalar_tensor_tensor(lo, v, par[:, g + k:g + k + 1], hi, ALU.mult, ALU.subtract)
                    if k == 3:
                        o.then_inc(raw_done, 1)

            def reciprocal_root(c, std, rstd, count):
                dve.wait_ge(std, count)
                dve.reciprocal(stat[:, 2, c:c + 1], stat[:, 1, c:c + 1]).then_inc(rstd, 1)
                dve.wait_ge(rstd, count)
                return stat[:, 2, c:c + 1]

            def rms_x(e, t):
                return reciprocal_root(2 * e + t, x_std, x_rstd, 2 * e + t + 1)

            def output(t):
                return ps[:, 4 + 2 * t:6 + 2 * t, :].rearrange("p b n -> p (b n)")

            def residual(b, t):
                if b == FFN0:
                    dve.wait_ge(ada_row_a, 4)
                if b <= FFN0:
                    dve.wait_ge(w_used if t else y_tok0, weight_count(y_unit(b)) if t else b + 1)
                    dve.tensor_tensor(tmp[:, t, :], output(t), rows[:, 2 if b else 1, :], ALU.mult).then_inc(t_done, 1)
                    scale = 1.0
                else:
                    e = 2 * (b - FFN1) + t
                    r = reciprocal_root(STAT_Y + e, y_std, y_rstd, e + 1)
                    dve.scalar_tensor_tensor(tmp[:, t, :], output(t), r, rows[:, 1, :], ALU.mult, ALU.mult).then_inc(t_done, 1)
                    scale = 1.0 if b in (AB, FOX) else 0.5
                dve.wait_ge(t_done, 2 * b + t + 1)
                for h in range(2):
                    c = slice(h * 512, (h + 1) * 512)
                    o = dve.scalar_tensor_tensor(x[:, t, c], tmp[:, t, c], scale, x[:, t, c], ALU.mult, ALU.add)
                    if b != FFN0:
                        o.then_inc(x_new, 1)
                if b == FFN0:
                    o.then_inc(x_mid, 1)
                    r = rms_x(FINAL_EVENT, t)
                    for h in range(2):
                        c = slice(h * 512, (h + 1) * 512)
                        dve.scalar_tensor_tensor(x[:, t, c], x[:, t, c], r, rows[:, 1, c], ALU.mult, ALU.mult).then_inc(x_new, 1)

            def norm_x(s, t):
                r = rms_x(x_event(s), t)
                o = dve.scalar_tensor_tensor(xn[:, t, :], x[:, t, :], r, rows[:, 0, :], ALU.mult, ALU.mult)
                if s == FFN0:
                    o.then_inc(xn_part, 1)
                    dve.wait_ge(xn_part, t + 1)
                    o = dve.tensor_tensor(xn[:, t, :], xn[:, t, :], rows[:, 3, :], ALU.add)
                o.then_inc(xn_done, 1)

            def turned_lo(s, t):
                for h in range(2):
                    at = xT_lo[:, 4 * h:4 * h + 4, t * P:(t + 1) * P]
                    dve.wait_ge(xT_hi_ok, 4 * s + 2 * t + h + 1)
                    dve.tensor_tensor(at, ps[:, 2 * t + h, :].rearrange("p (k c) -> p k c", k=4),
                                      xT_hi[:, 4 * h:4 * h + 4, t * P:(t + 1) * P].bitcast(F32), ALU.subtract).then_inc(xT_ok, 1)

            def between(b):
                s = b + 1
                if b > CONV:
                    dve.wait_ge(rows_landed, rows_count(b))
                if s < 8:
                    split_piece(BASE[s] + 1, (0, 1, 2))
                residual(b, 0)
                if s < 8:
                    split_piece(BASE[s] + 1, (3,))
                if s in FOLDED:
                    turned_lo(s, 0)
                    residual(b, 1)
                    rms_x(x_event(s), 0)
                    turned_lo(s, 1)
                    rms_x(x_event(s), 1)
                elif s in NORMED:
                    norm_x(s, 0)
                    residual(b, 1)
                    turned_lo(s, 0)
                    norm_x(s, 1)
                    turned_lo(s, 1)
                else:
                    residual(b, 1)
                if s < 8:
                    split(BASE[s] + 2)

            def ffn(s):
                f, n = ffn_index(s), BASE[s]

                def hidden(j):
                    for t in range(TOKT):
                        dve.wait_ge(sil_done, 2 * NCH * f + t + 1 + 2 * j)
                        up = ps[:, t, FCH:2 * FCH]
                        if s in FOLDED:
                            c = 2 * x_event(s) + t
                            o = dve.scalar_tensor_tensor(hid[:, t, :], up, stat[:, 2, c:c + 1], sil[:, t, :], ALU.mult, ALU.mult)
                        else:
                            o = dve.tensor_tensor(hid[:, t, :], up, sil[:, t, :], ALU.mult)
                        o.then_inc(hid_done, 1)

                def turned(j, dst, hi):
                    dve.wait_ge(hT_hi_ok, NCH * f + 1 + j)
                    dve.tensor_tensor(dst, ps[:, 2, :].rearrange("p (f c) -> p f c", f=2), hi.bitcast(F32),
                                      ALU.subtract).then_inc(hT_ok, 1)

                def chunk(j):
                    if not (isinstance(j, int) and j == 0):
                        split(n + 2, j)
                    hidden(j)
                    split(n + 3, j)
                    split(n + 4, j)
                    turned(j, hT_lo[:, :, :], hT_hi[:, :, :])

                chunk(0)
                with dve.Fori(1, NCH - 1) as j:
                    chunk(j)
                split(n + FFN_UNITS - 1)
                hidden(NCH - 1)
                turned(NCH - 1, yT_lo[:, 0:2, :], yT_hi[:, 0:2, :])
                split(n + FFN_UNITS)

            dve.wait_ge(par_ready, 1)
            dve.wait_ge(bias_landed, 16)
            for k in range(KT):
                dve.wait_ge(landed[slot_of(k)], 32 * (k // NSLOT + 1))
                if k:
                    dve.wait_ge(raw_done, k)
                dve.scalar_tensor_tensor(ada_sum0, raw[:, slot_of(k), :], cond[:, k:k + 1], ada_sum0, ALU.mult, ALU.add)\
                    .then_inc(raw_done, 1)
                if k in (4, 5):
                    t = k - 4
                    dve.tensor_scalar(xn[:, t, :], x[:, t, :], rms_x(0, t), None, ALU.mult).then_inc(xn_done, 1)
            n = BASE[CONV]
            dve.wait_ge(par_ready, 3)

            def modulation(h):
                dve.wait_ge(mod_ps, h + 1)
                c = slice(4 * h, 4 * h + 4)
                dve.tensor_copy(mod[:, 0, c], ps[:, 4 + h, c])
                dve.scalar_tensor_tensor(mod[:, 1, c], ps[:, 4 + h, KT + 4 * h:KT + 4 * h + 4], 1.0, par[:, C_G1 + 4 * h:C_G1 + 4 * h + 4],
                                         ALU.add, ALU.mult).then_inc(mod_ok, 1)
                dve.wait_ge(mod_ok, h + 1)

            def modulated(b):
                dve.wait_ge(xT_ps, b + 1)
                for i in range(2):
                    k = 2 * b + i
                    o = dve.tensor_scalar(xnT[:, k, :], ps[:, b, i * SEQ:(i + 1) * SEQ], mod[:, 1, k:k + 1], mod[:, 0, k:k + 1],
                                          ALU.mult, ALU.add)
                o.then_inc(xnT_ok, 1)

            modulation(0)
            modulated(0)
            split(n)
            for b in range(KT // 2):
                if b == 1:
                    modulation(1)
                if b + 1 < KT // 2:
                    modulated(b + 1)
                if b == 2:
                    split(n + 1)
                dve.wait_ge(xT_hi_ok, b + 1)
                dve.tensor_tensor(xT_lo[:, 2 * b:2 * b + 2, :], xnT[:, 2 * b:2 * b + 2, :],
                                  xT_hi[:, 2 * b:2 * b + 2, :].bitcast(F32), ALU.subtract).then_inc(xT_ok, 1)

            def ada_chunk(q):
                dve.wait_ge(ada_v_bias, 32)
                dve.wait_ge(ada_v_landed[q % 2], 16 * (q // 2 + 1))
                acc = tmp[:, q // ADA_CH, :]
                for i in range(2):
                    k = 2 * (q % ADA_CH) + i
                    if q or i:
                        dve.wait_ge(ada_v_add, 2 * q + i)
                    o = dve.scalar_tensor_tensor(acc, ada_v_raw[:, q % 2, i, :], cond[:, k:k + 1], acc, ALU.mult, ALU.add)
                    o.then_inc(ada_v_add, 1)

            dve.wait_ge(pads, 1)
            for k in range(2, 18):
                m = (k - 4) // 2
                if k % 2 == 0 and 0 <= m < 6 and m % 3:
                    h = m // 3
                    dve.wait_ge(w_used, weight_count(n + 2 * m + 1))
                    if m % 3 == 1:
                        dve.wait_ge(evac_a, h + 1)
                        for b in range(2):
                            u = dve.tensor_tensor(u_pad[:, 2 * b:2 * b + 2, :, 1:GRID_W + 1],
                                                  ps[:, 2 + b, :].rearrange("p (a r c) -> p a r c", a=2, r=4),
                                                  gate_c[:, 2 * b:2 * b + 2, :].rearrange("p a (r c) -> p a r c", r=4), ALU.mult)
                        u.then_inc(evac_v, 1)
                    else:
                        dve.wait_ge(tap, 12 * h + 12)
                        if h:
                            dve.wait_ge(yT_hi_ok, h)
                        dve.tensor_tensor(conv_y.rearrange("p a b -> p (a b)"), ps[:, 4:6, :].rearrange("p b n -> p (b n)"),
                                          conv_acc.rearrange("p a b -> p (a b)"), ALU.mult).then_inc(evac_v, 1)
                        dve.wait_ge(yT_hi_ok, h + 1)
                        dve.tensor_tensor(yT_lo[:, 4 * h:4 * h + 4, :], conv_y, yT_hi[:, 4 * h:4 * h + 4, :].bitcast(F32),
                                          ALU.subtract).then_inc(yT_ok, 1)
                if k < 17:
                    split(n + k)
                if k in (6, 12):
                    h = (k - 6) // 6
                    dve.wait_ge(evac_v, 2 * h + 1)
                    for i, tp in enumerate((1, 0, 2)):
                        for c in range(CCT):
                            wt = C_CONVW + tp * KT + 4 * h + c
                            o = conv_acc[:, c, :].rearrange("p (r c) -> p r c", r=4)
                            src = u_pad[:, c, :, tp:tp + GRID_W]
                            if i == 0:
                                o = dve.tensor_scalar(o, src, par[:, wt:wt + 1], None, ALU.mult)
                            else:
                                dve.wait_ge(tap, 12 * h + 4 * (i - 1) + c + 1)
                                o = dve.scalar_tensor_tensor(o, src, par[:, wt:wt + 1], o, ALU.mult, ALU.add)
                            o.then_inc(tap, 1)
                if k < 2 + 2 * ADA_CH:
                    ada_chunk(k - 2)
            dve.wait_ge(ada_ps, 2)
            dve.wait_ge(g2_row_landed, 16)
            dve.scalar_tensor_tensor(rows[:, 0, :], ps[:, 0:2, :].rearrange("p b n -> p (b n)"), 1.0, rows[:, 0, :],
                                     ALU.add, ALU.mult).then_inc(ada_row_v, 1)
            dve.wait_ge(ada_row_v, 1)
            dve.wait_ge(ada_row_a, 2)
            between(CONV)

            def scaled(s, i, bias, sink=None):
                item = first_item[s] + i
                c = 4 * item
                p = p_of[s]
                dve.wait_ge(s_ps, item + 1)
                dve.scalar_tensor_tensor(p[:, i % 2, :, :], ps[:, item_bank(i):item_bank(i) + 2, 0:384], DH ** -0.5, bias,
                                         ALU.mult, ALU.add).then_inc(s_sb, 1)
                dve.wait_ge(s_sb, item + 1)
                for b in range(2):
                    d = p[:, i % 2, :, 0:P] if b == 0 else p[:, i % 2, :, P:3 * P]
                    mx = dve.tensor_reduce(soft[:, 0, c + 2 * b:c + 2 * b + 2], d, AX_X, ALU.max)
                    if b == 1:
                        link(mx)
                if sink is not None:
                    link(dve.tensor_tensor(soft[:, 4, c:c + 4].rearrange("p (b g) -> p b g", b=2),
                                           soft[:, 0, c:c + 4].rearrange("p (b g) -> p b g", b=2), sink, ALU.max))
                    link(dve.tensor_tensor(soft[:, 2, c:c + 4].rearrange("p (b g) -> p b g", b=2), sink,
                                           soft[:, 4, c:c + 4].rearrange("p (b g) -> p b g", b=2), ALU.subtract))
                dve.tensor_scalar(soft[:, 1, c:c + 4], soft[:, 0 if sink is None else 4, c:c + 4], -1.0, None,
                                  ALU.mult).then_inc(m_ok, 1)

            def normed(s, i):
                item = first_item[s] + i
                c = 4 * item
                dve.wait_ge(e_done, item + 1)
                z = soft[:, 3, c:c + 4]
                if s == AB:
                    link(dve.tensor_tensor(soft[:, 6, c:c + 4], z, soft[:, 5, c:c + 4], ALU.add))
                    z = soft[:, 6, c:c + 4]
                link(dve.reciprocal(soft[:, 7, c:c + 4], z))
                for b in range(2):
                    for g in range(2):
                        d = p_of[s][:, i % 2, g, 0:P] if b == 0 else p_of[s][:, i % 2, g, P:3 * P]
                        a = c + 2 * b + g
                        q = dve.tensor_scalar(d, d, soft[:, 7, a:a + 1], None, ALU.mult)
                q.then_inc(p_done, 1)

            def probs_out(s, i):
                dve.wait_ge(pT_psd, first_item[s] + i + 1)
                dve.tensor_copy(pT_of[s][:, i % 2, 1, :], ps[:, item_bank(i) + 1, 0:384]).then_inc(pT_okV, 1)

            def outputs_lo(s, i):
                dve.wait_ge(oT_hi_ok, first_item[s] + i + 1)
                dve.tensor_tensor(yT_lo[:, out_kt[s] + i, :], ps[:, item_bank(i), 0:SEQ],
                                  yT_hi[:, out_kt[s] + i, :].bitcast(F32), ALU.subtract).then_inc(oT_ok, 1)

            ffn(FFN0)
            between(FFN0)
            ffn(FFN1)
            between(FFN1)
            n = BASE[AB]
            done = [0]
            last_of = {}

            def taps(count):
                for m in range(done[0], min(done[0] + count, len(V_TAPS))):
                    k, c = V_TAPS[m]
                    w_kc = cw31[:, k * CCT + c:k * CCT + c + 1]
                    src = a_pad[:, c, k:k + SEQ]
                    if k == 0:
                        o = dve.tensor_scalar(acc31[:, c, :], src, w_kc, par[:, C_CB + c:C_CB + c + 1], ALU.mult, ALU.add)
                    else:
                        dve.wait_ge(tap, last_of[c])
                        o = dve.scalar_tensor_tensor(acc31[:, c, :], src, w_kc, acc31[:, c, :], ALU.mult, ALU.add)
                    o.then_inc(tap, 1)
                    last_of[c] = 24 + m + 1
                done[0] = min(done[0] + count, len(V_TAPS))

            def glu(t):
                dve.tensor_tensor(sig.rearrange("p a b -> p (a b)")[:, t * 512:(t + 1) * 512], ps[:, 6 + t, :],
                                  sig.rearrange("p a b -> p (a b)")[:, t * 512:(t + 1) * 512], ALU.mult).then_inc(evac_v, 1)

            split(n + 3)
            split(n + 4)
            dve.wait_ge(evac_a, 3)
            dve.wait_ge(a_tok0, 1)
            glu(0)
            split(n + 5)
            dve.wait_ge(w_used, weight_count(n + 3))
            glu(1)
            split(n + 6)
            dve.wait_ge(evac_a, 5)
            taps(12)
            split(n + 7)
            dve.wait_ge(bias_built, 1)
            dve.wait_ge(misc_landed, 48)
            sink_v = sinks[:, :].rearrange("p (c g) -> p c g", g=2)
            for i in range(5):
                if i:
                    probs_out(AB, i - 1)
                if i < 4:
                    scaled(AB, i, alibi[:, 2 * i:2 * i + 2, :], sink_v[:, i:i + 1, :].to_broadcast([P, 2, 2]))
                taps(5)
                if i < 4:
                    normed(AB, i)
                if i:
                    outputs_lo(AB, i - 1)
                if i < 2:
                    split(n + 8 + i)
                else:
                    taps(4)
            taps(len(V_TAPS))
            dve.wait_ge(tap, 24 + len(V_TAPS))
            dve.wait_ge(sum_p, len(A_TAPS))
            dve.tensor_tensor(acc31[:, 1, :], acc31[:, 1, :], acc_p, ALU.add).then_inc(conv_done, 1)
            for t in range(TOKT):
                dve.wait_ge(ln_ps, t + 1)
                link(dve.bn_stats(soft[:, 0, 50 + 6 * t:56 + 6 * t], ps[:, t, :]))
                dve.bn_aggr(zf[:, 7, 8 * t:8 * t + 2], soft[:, 0, 50 + 6 * t:56 + 6 * t]).then_inc(ln_stat, 1)
            for t in range(TOKT):
                dve.wait_ge(ln_std, t + 1)
                link(dve.reciprocal(zf[:, 7, 8 * t + 3:8 * t + 4], zf[:, 7, 8 * t + 2:8 * t + 3]))
                dve.tensor_scalar(ln_y[:, t, :], ps[:, t, :], zf[:, 7, 8 * t:8 * t + 1], zf[:, 7, 8 * t + 3:8 * t + 4],
                                  ALU.subtract, ALU.mult).then_inc(ln_out, 1)
            dve.wait_ge(yT_hi_ok, 3)
            dve.tensor_tensor(yT_lo[:, 0:4, :], ab_y, yT_hi[:, 0:4, :].bitcast(F32), ALU.subtract).then_inc(yT_ok, 1)
            split(n + 10)
            split(n + 11)
            between(AB)
            ffn(FFN2)
            between(FFN2)
            dve.tensor_copy(zf_hi[:, :, :], zf_raw[:, :, :]).then_inc(zf_ok, 1)
            dve.wait_ge(zf_ok, 1)
            dve.tensor_tensor(zf_lo[:, :, :], zf_raw[:, :, :], zf_hi[:, :, :].bitcast(F32), ALU.subtract).then_inc(zf_ok, 1)
            ffn(FFN3)
            between(FFN3)
            n = BASE[FOX]
            dve.wait_ge(zf_p, 1)
            for t in range(TOKT):
                o = dve.tensor_tensor(zf[:, 0, t * 16:(t + 1) * 16], ps[:, 0, t * 16:(t + 1) * 16], b_f[:, :], ALU.add)
            link(o)
            dve.scalar_tensor_tensor(zf[:, 1, :], zf[:, 0, :], -1.0, zf[:, 0, :], ALU.mult, ALU.max).then_inc(zf_z, 1)
            link(dve.tensor_scalar(zf[:, 4, :], zf[:, 0, :], 0.0, None, ALU.min))
            dve.wait_ge(zf_e, 2)
            dve.tensor_tensor(zf[:, 5, :], zf[:, 4, :], zf[:, 3, :], ALU.subtract).then_inc(zf_v, 1)

            def distances(i):
                dve.wait_ge(d_ps, i + 1)
                for g in range(2):
                    h = 2 * i + g
                    src = ps[:, 1, g * SEQ:(g + 1) * SEQ]
                    dve.tensor_scalar(decay[:, h, 0:P], src[:, 0:P], zf[:, 6, h:h + 1], None, ALU.add)
                    o = dve.tensor_scalar(decay[:, h, P:3 * P], src, zf[:, 6, 16 + h:17 + h], None, ALU.add)
                o.then_inc(d_raw_v, 1)

            split(n + 3)
            split(n + 4)
            split(n + 5)
            distances(1)
            split(n + 6)
            distances(3)
            split(n + 7)
            distances(5)
            distances(7)
            for i in range(FOX_H // 2):
                if i:
                    probs_out(FOX, i - 1)
                dve.wait_ge(d_ok, i + 1)
                scaled(FOX, i, decay[:, 2 * i:2 * i + 2, :])
                split(n + 8 + i)
                normed(FOX, i)
                if i:
                    outputs_lo(FOX, i - 1)
            probs_out(FOX, 7)
            split(n + 16)
            outputs_lo(FOX, 7)
            between(FOX)
            ffn(FFN4)
            between(FFN4)

        @block.gpsimd
        def _(pool):
            step = [0]

            def link(ins):
                step[0] += 1
                ins.then_inc(pool_chain, 1)
                pool.wait_ge(pool_chain, step[0])

            pool.memset(eps[:, :], EPS)
            pool.memset(ada_sum0, 0.0).then_inc(ada0_cleared, 1)
            pool.memset(ones[:, :], 1.0)
            link(pool.memset(ident[:, :], 0.0))
            link(pool.affine_select(out=ident[:, :], in_=ident[:, :], compare_op=ALU.not_equal, fill=1.0, base=0,
                                    pattern=[[-1, P]], channel_multiplier=1))
            pool.affine_select(out=upper[:, :], in_=ones[:, :], compare_op=ALU.is_ge, fill=0.0, base=0,
                               pattern=[[1, P]], channel_multiplier=-1).then_inc(consts, 1)
            pool.memset(u_pad[:, :, :, 0:1], 0.0)
            pool.memset(u_pad[:, :, :, GRID_W + 1:GRID_W + 2], 0.0).then_inc(pads, 1)

            def load_ada_p(q):
                c0, k = ADA_P[q // ADA_CH] * D, 2 * (q % ADA_CH)
                pool.dma_start(ada_p_slot(q), ada_w[:, k:k + 2, c0:c0 + D]).then_inc(ada_p_landed[q % 2], 16)

            def ada_p_slot(q):
                return ada_v_raw[:, 1, :, :] if q >= ADA_CH and q % 2 else ada_p_raw[q % 2]

            def ada_p_chunk(q):
                pool.wait_ge(ada_p_landed[q % 2], 16 * (q // 2 + 1))
                for i in range(2):
                    k = 2 * (q % ADA_CH) + i
                    a = ada_p_slot(q)[:, i, :]
                    link(pool.tensor_scalar(a, a, cond[:, k:k + 1], None, ALU.mult))
                    o = pool.tensor_tensor(ada_acc, a, ada_acc, ALU.add)
                    if i == 0:
                        link(o)
                    else:
                        o.then_inc(ada_p_done, 1)
                        pool.wait_ge(ada_p_done, q + 1)

            def ada_p_section(i):
                link(pool.memset(ada_acc, 0.0))
                pool.dma_start(ada_acc[0:1, :], w["ada_b"][:, ADA_P[i] * D:(ADA_P[i] + 1) * D]).then_inc(ada_p_bias, 16)
                pool.wait_ge(ada_p_bias, 16 * (i + 1))

            ada_p_section(0)
            pool.wait_ge(raw_done, ADA_FIRST)
            load_ada_p(0)
            pool.wait_ge(mod_ps, 2)
            pool.memset(tmp[:, 0, :], 0.0)
            link(pool.memset(tmp[:, 1, :], 0.0))
            for i, section in enumerate(ADA_V):
                pool.dma_start(tmp[0:1, i, :], w["ada_b"][:, section * D:(section + 1) * D]).then_inc(ada_v_bias, 16)
            load_ada_p(1)
            pool.wait_ge(par_ready, 1)
            for q in range(ADA_CH):
                ada_p_chunk(q)
                if q + 2 < ADA_CH:
                    load_ada_p(q + 2)
            pool.wait_ge(ada_ps, 3)
            ada_p_section(1)
            load_ada_p(ADA_CH)
            load_ada_p(ADA_CH + 1)
            for q in range(ADA_CH, 2 * ADA_CH):
                ada_p_chunk(q)
                if q + 2 < 2 * ADA_CH:
                    load_ada_p(q + 2)
            pool.wait_ge(ada_ps, 5)
            pool.wait_ge(x_new, x_count(CONV, 0, 0))
            pool.memset(a_pad[:, :, 0:CONV_K - 1], 0.0).then_inc(pads, 1)
            dist_i = pT_ab[:, 0, 0, :].bitcast(mybir.dt.int32)
            dist = pT_ab[:, 0, 1, :]
            pool.iota(dist_i[:, 0:P], pattern=[[-1, P]], base=0, channel_multiplier=1)
            link(pool.iota(dist_i[:, P:3 * P], pattern=[[-1, 2 * P]], base=P, channel_multiplier=1))
            link(pool.tensor_copy(dist, dist_i))
            for h in range(SWA_HQ):
                slope = 2.0 ** (-8.0 * (h + 1) / SWA_HQ)
                b0, b1 = alibi[:, h, 0:P], alibi[:, h, P:3 * P]
                link(pool.tensor_scalar(alibi[:, h, :], dist, -slope, None, ALU.mult))
                link(pool.affine_select(out=b1, in_=b1, compare_op=ALU.is_ge, fill=NEG, base=P,
                                        pattern=[[-1, 2 * P]], channel_multiplier=1))
                pool.affine_select(out=b0, in_=b0, compare_op=ALU.is_ge, fill=NEG, base=0,
                                   pattern=[[-1, P]], channel_multiplier=1)
                a = pool.affine_select(out=b1, in_=b1, compare_op=ALU.is_ge, fill=NEG, base=-1,
                                       pattern=[[1, 2 * P]], channel_multiplier=-1)
            a.then_inc(bias_built, 1)
            pool.wait_ge(xT_ok, 4 * AB + 4)
            for k in range(CONV_K):
                o = pool.tensor_scalar(diag[k], ident[:, :], cw31[:, k * CCT + 3:k * CCT + 4], None, ALU.mult)
            o.then_inc(diag_ok, 1)
            link(pool.memset(acc31[:, 2, :], 0.0))
            link(pool.memset(acc_p, 0.0))
            last_of = {}
            for m, (k, c) in enumerate(A_TAPS):
                acc = acc31[:, 2, :] if c == 2 else acc_p
                pool.wait_ge(prod_a, m + 1)
                if c in last_of:
                    pool.wait_ge(sum_p, last_of[c])
                pool.tensor_tensor(acc, acc, ring[m % RING], ALU.add).then_inc(sum_p, 1)
                last_of[c] = m + 1
            for i in range(FOX_H // 2):
                pool.wait_ge(d_raw_v if i % 2 else d_raw_a, i // 2 + 1)
                for h in (2 * i, 2 * i + 1):
                    d = decay[:, h, :].rearrange("p (k s) -> p k s", k=3)[:, 0::2, :]
                    a = pool.affine_select(out=d, in_=d, compare_op=ALU.is_ge, fill=NEG, base=0,
                                           pattern=[[0, 2], [-1, P]], channel_multiplier=1)
                a.then_inc(d_ok, 1)


_INS = ["x", "c", "ada_w", "ada_b", "norm1_g", "norm2_g", "conv_w_in", "conv_w", "conv_w_out", "ffn_w_in", "ffn_w_out",
        "final_g", "norm_g_2", "ffn_w_gate_2", "ffn_w_up_2", "ffn_w_down_2", "ab_w_in_2", "conv_w_2", "conv_b_2",
        "conv_ln_g_2", "conv_ln_b_2", "swa_sinks_2", "ab_w_out_2", "fox_w_in_2", "fox_b_f_2", "fox_w_out_2"]


def kernel(**inputs):
    import numpy as np
    from concourse import bacc
    from concourse.bass_utils import run_bass_kernel_spmd

    nc = bacc.Bacc("TRN2", target_bir_lowering=False, num_devices=1)
    arrays, args = {}, {}
    for name in _INS:
        a = np.ascontiguousarray(inputs[name])
        arrays[f"in_{name}"] = a
        args[name] = nc.dram_tensor(f"in_{name}", a.shape, mybir.dt.from_np(a.dtype), kind="ExternalInput").ap()
    out = nc.dram_tensor("out", (1, SEQ, D), F32, kind="ExternalOutput").ap()
    block_program(nc, out, **args)
    r = run_bass_kernel_spmd(nc, [arrays], core_ids=[0])
    return r.results[0]["out"]
```
